# Optimizing a Trainium2 kernel written in Bass

```python
import math
import jax, jax.numpy as jnp
from jax import lax
import numpy as np

D_MODEL = 1024
BATCH = 1
SEQ = 512
DEPTH = 2

CHUNK = 64
MEM_LEN = 256
N_MIXERS = 2
N_A = (DEPTH + 1) // 2
N_B = DEPTH // 2

D_LRU = D_MODEL // 2
LRU_BLOCKS = 8
LRU_BLK = D_LRU // LRU_BLOCKS
CONV_WIDTH = 4
LRU_C = 8.0

FOX_HEADS = 8
FOX_HD = 64
FOX_WIDTH = FOX_HEADS * FOX_HD
Q_BLOCK = 128

XA_HEADS = 4
XA_HD = 128
XA_WIDTH = XA_HEADS * XA_HD

D_FF = 4 * D_MODEL
EPS = 1e-6
NEG_INF = -1e30


def rms_norm(x, g):
    xf = x.astype(jnp.float32)
    y = xf * lax.rsqrt(jnp.mean(xf * xf, axis=-1, keepdims=True) + EPS)
    return (y * g.astype(jnp.float32)).astype(x.dtype)

def _lin_combine(left, right):
    a1, b1 = left
    a2, b2 = right
    return a1 * a2, a2 * b1 + b2

def rglru_group(h, w_in, conv_w, conv_b, w_r, b_r, w_i, b_i, lam):
    B, S, _ = h.shape
    proj = h @ w_in
    u, gate, xq = jnp.split(proj, [D_LRU, 2 * D_LRU], axis=-1)
    u = lax.conv_general_dilated(
        u, conv_w[:, None, :].astype(u.dtype), window_strides=(1,),
        padding=[(CONV_WIDTH - 1, 0)], dimension_numbers=("NWC", "WIO", "NWC"),
        feature_group_count=D_LRU) + conv_b
    ub = u.reshape(B, S, LRU_BLOCKS, LRU_BLK)
    r = jax.nn.sigmoid(jnp.einsum("bsnc,ncd->bsnd", ub, w_r).reshape(B, S, D_LRU) + b_r)
    i = jax.nn.sigmoid(jnp.einsum("bsnc,ncd->bsnd", ub, w_i).reshape(B, S, D_LRU) + b_i)
    log_a = -LRU_C * r.astype(jnp.float32) * jax.nn.softplus(-lam.astype(jnp.float32))
    a = jnp.exp(log_a)
    b = jnp.sqrt(-jnp.expm1(2.0 * log_a)) * (i.astype(jnp.float32) * u.astype(jnp.float32))
    _, hs = lax.associative_scan(_lin_combine, (a, b), axis=1)
    y = hs.astype(h.dtype) * jax.nn.gelu(gate, approximate=True)
    return y, xq

def fox_group(h, w_in, b_f, q_gain, k_gain):
    B, S, _ = h.shape
    n_qb = S // Q_BLOCK
    proj = h @ w_in
    q, k, v, f_logit, xq = jnp.split(
        proj, [FOX_WIDTH, 2 * FOX_WIDTH, 3 * FOX_WIDTH, 3 * FOX_WIDTH + FOX_HEADS], axis=-1)
    q = rms_norm(q.reshape(B, S, FOX_HEADS, FOX_HD), q_gain)
    k = rms_norm(k.reshape(B, S, FOX_HEADS, FOX_HD), k_gain)
    v = v.reshape(B, S, FOX_HEADS, FOX_HD)
    log_f = jax.nn.log_sigmoid(f_logit.astype(jnp.float32) + b_f.astype(jnp.float32))
    c = jnp.cumsum(log_f, axis=1).transpose(0, 2, 1)
    kh = k.transpose(0, 2, 1, 3)
    vh = v.transpose(0, 2, 1, 3)
    q_blocks = q.reshape(B, n_qb, Q_BLOCK, FOX_HEADS, FOX_HD).transpose(1, 0, 3, 2, 4)
    c_blocks = c.reshape(B, FOX_HEADS, n_qb, Q_BLOCK).transpose(2, 0, 1, 3)
    q_pos = jnp.arange(S, dtype=jnp.int32).reshape(n_qb, Q_BLOCK)
    k_pos = jnp.arange(S, dtype=jnp.int32)
    scale = 1.0 / math.sqrt(FOX_HD)

    def one_block(args):
        qb, cb, pos = args
        s = jnp.einsum("bhqd,bhkd->bhqk", qb, kh).astype(jnp.float32) * scale
        s = s + cb[..., :, None] - c[:, :, None, :]
        s = jnp.where(pos[:, None] >= k_pos[None, :], s, NEG_INF)
        p = jax.nn.softmax(s, axis=-1)
        return jnp.einsum("bhqk,bhkd->bhqd", p.astype(vh.dtype), vh)

    o = lax.map(one_block, (q_blocks, c_blocks, q_pos))
    o = o.transpose(1, 0, 3, 2, 4).reshape(B, S, FOX_WIDTH)
    return o, xq

def memory_group(xq, mem, g_mem, w_kv, q_gain, k_gain):
    B, S, _ = xq.shape
    M = mem.shape[1]
    kv = rms_norm(mem, g_mem) @ w_kv
    k, v = jnp.split(kv, [XA_WIDTH], axis=-1)
    q = rms_norm(xq.reshape(B, S, XA_HEADS, XA_HD), q_gain)
    k = rms_norm(k.reshape(B, M, XA_HEADS, XA_HD), k_gain)
    v = v.reshape(B, M, XA_HEADS, XA_HD)
    s = jnp.einsum("bshd,bmhd->bhsm", q, k).astype(jnp.float32) * (1.0 / math.sqrt(XA_HD))
    p = jax.nn.softmax(s, axis=-1)
    o = jnp.einsum("bhsm,bmhd->bshd", p.astype(v.dtype), v)
    return o.reshape(B, S, XA_WIDTH)

def sqrelu_mlp(h, w1, w2):
    return jnp.square(jax.nn.relu(h @ w1)) @ w2

def first_inputs(seed: int = 0) -> dict:
    key = jax.random.key(seed)
    ks = jax.random.split(key, 32)
    f32 = jnp.float32

    def nrm(k, shape, fan_in):
        return jax.random.normal(k, shape, f32) * (fan_in ** -0.5)

    def gain(k, shape):
        return 1.0 + 0.05 * jax.random.normal(k, shape, f32)

    def small(k, shape):
        return 0.02 * jax.random.normal(k, shape, f32)

    x = jax.random.normal(ks[0], (BATCH, SEQ, D_MODEL), f32)
    mem = jax.random.normal(ks[1], (BATCH, MEM_LEN, D_MODEL), f32)
    a_c = jax.random.uniform(ks[2], (N_A, D_LRU), f32, 0.9, 0.999)
    s_lam = a_c ** (1.0 / LRU_C)
    lru_lambda = jnp.log(s_lam) - jnp.log1p(-s_lam)
    return {
        "x": x,
        "mem": mem,
        "norm_mix": gain(ks[3], (DEPTH, D_MODEL)),
        "norm_mem": gain(ks[4], (DEPTH, D_MODEL)),
        "w_mem_kv": nrm(ks[5], (DEPTH, D_MODEL, 2 * XA_WIDTH), D_MODEL),
        "xa_q_gain": gain(ks[6], (DEPTH, XA_HD)),
        "xa_k_gain": gain(ks[7], (DEPTH, XA_HD)),
        "w_out": nrm(ks[8], (DEPTH, D_LRU + XA_WIDTH, D_MODEL), D_LRU + XA_WIDTH),
        "norm_mlp": gain(ks[9], (DEPTH, D_MODEL)),
        "w_mlp_in": nrm(ks[10], (DEPTH, D_MODEL, D_FF), D_MODEL),
        "w_mlp_out": nrm(ks[11], (DEPTH, D_FF, D_MODEL), D_FF),
        "w_in_a": nrm(ks[12], (N_A, D_MODEL, 2 * D_LRU + XA_WIDTH), D_MODEL),
        "conv_w": nrm(ks[13], (N_A, CONV_WIDTH, D_LRU), CONV_WIDTH),
        "conv_b": small(ks[14], (N_A, D_LRU)),
        "w_rgate": nrm(ks[15], (N_A, LRU_BLOCKS, LRU_BLK, LRU_BLK), LRU_BLK),
        "b_rgate": small(ks[16], (N_A, D_LRU)),
        "w_igate": nrm(ks[17], (N_A, LRU_BLOCKS, LRU_BLK, LRU_BLK), LRU_BLK),
        "b_igate": small(ks[18], (N_A, D_LRU)),
        "lru_lambda": lru_lambda,
        "w_in_b": nrm(ks[19], (N_B, D_MODEL, 3 * FOX_WIDTH + FOX_HEADS + XA_WIDTH), D_MODEL),
        "b_forget": jax.random.uniform(ks[20], (N_B, FOX_HEADS), f32, 1.0, 6.0),
        "fox_q_gain": gain(ks[21], (N_B, FOX_HD)),
        "fox_k_gain": gain(ks[22], (N_B, FOX_HD)),
    }

def first_block(x, mem, norm_mix, norm_mem, w_mem_kv, xa_q_gain, xa_k_gain, w_out,
              norm_mlp, w_mlp_in, w_mlp_out, w_in_a, conv_w, conv_b, w_rgate, b_rgate,
              w_igate, b_igate, lru_lambda, w_in_b, b_forget, fox_q_gain, fox_k_gain):
    for layer in range(DEPTH):
        h = rms_norm(x, norm_mix[layer])
        j = layer // N_MIXERS
        if layer % N_MIXERS == 0:
            y_mix, xq = rglru_group(h, w_in_a[j], conv_w[j], conv_b[j], w_rgate[j], b_rgate[j],
                                    w_igate[j], b_igate[j], lru_lambda[j])
        else:
            y_mix, xq = fox_group(h, w_in_b[j], b_forget[j], fox_q_gain[j], fox_k_gain[j])
        y_mem = memory_group(xq, mem, norm_mem[layer], w_mem_kv[layer],
                             xa_q_gain[layer], xa_k_gain[layer])
        x = x + jnp.concatenate([y_mix, y_mem], axis=-1) @ w_out[layer]
        x = x + sqrelu_mlp(rms_norm(x, norm_mlp[layer]), w_mlp_in[layer], w_mlp_out[layer])
    return x


D_RWKV = D_MODEL // 2
HEAD_SIZE = 64
N_HEADS = D_RWKV // HEAD_SIZE
D_DECAY_LORA = max(32, int(round(1.8 * D_MODEL ** 0.5 / 32)) * 32)
D_AAA_LORA = max(32, int(round(1.8 * D_MODEL ** 0.5 / 32)) * 32)
D_MV_LORA = max(32, int(round(0.7 * D_MODEL ** 0.5 / 32)) * 32)
D_GATE_LORA = max(32, int(round(0.6 * D_MODEL ** 0.8 / 32)) * 32)

D_POOL = D_MODEL // 2
POOL_WINDOWS = (2, 4, 8, 16)
N_POOL_GROUPS = len(POOL_WINDOWS)
POOL_GROUP = D_POOL // N_POOL_GROUPS

D_FF_2 = ((8 * D_MODEL // 3 + 255) // 256) * 256

N_SHIFT = 3 * D_RWKV + D_DECAY_LORA + D_AAA_LORA + D_GATE_LORA
N_IN = N_SHIFT + D_POOL + 2 * D_MODEL
N_MOD = 6 * D_MODEL

EPS_RMS = 1e-6
EPS_GN = 64e-5


def rms_norm_2(x, g):
    xf = x.astype(jnp.float32)
    y = xf * lax.rsqrt(jnp.mean(xf * xf, axis=-1, keepdims=True) + EPS_RMS)
    return (y * g.astype(jnp.float32)).astype(x.dtype)

def token_shift(z, mu):
    prev = jnp.pad(z, ((0, 0), (1, 0), (0, 0)))[:, :-1]
    return z + (prev - z) * mu

def wkv7_scan(r, w, k, v, kk, a):
    B, S, H, N = r.shape

    def to_chunks(t):
        return jnp.moveaxis(t, 1, 0).reshape(S // CHUNK, CHUNK, B, H, N)

    def step(state, inp):
        r_t, w_t, k_t, v_t, kk_t, a_t = inp
        sk = jnp.einsum('bhvk,bhk->bhv', state, kk_t)
        state = (state * w_t[:, :, None, :]
                 - sk[..., None] * (a_t * kk_t)[:, :, None, :]
                 + v_t[..., None] * k_t[:, :, None, :])
        return state, jnp.einsum('bhvk,bhk->bhv', state, r_t)

    def chunk_step(state, chunk_inp):
        return lax.scan(step, state, chunk_inp)

    state0 = jnp.zeros((B, H, N, N), jnp.float32)
    _, ys = lax.scan(chunk_step, state0, tuple(to_chunks(t) for t in (r, w, k, v, kk, a)))
    return jnp.moveaxis(ys.reshape(S, B, H, N), 0, 1)

def rwkv7_time_mix(ps, vl, v_first, w0, w_up, a0, a_up, v0, v_up, g_up, k_k, k_a, r_k, lnx_g, lnx_b):
    B, S, _ = ps.shape
    dt = ps.dtype
    f32 = jnp.float32
    o = 0
    r = ps[..., o:o + D_RWKV]; o += D_RWKV
    k = ps[..., o:o + D_RWKV]; o += D_RWKV
    v = ps[..., o:o + D_RWKV]; o += D_RWKV
    wl = ps[..., o:o + D_DECAY_LORA]; o += D_DECAY_LORA
    al = ps[..., o:o + D_AAA_LORA]; o += D_AAA_LORA
    gl = ps[..., o:o + D_GATE_LORA]

    log_w = -jax.nn.softplus(-(w0 + jnp.tanh(wl) @ w_up)) - 0.5
    decay = jnp.exp(-jnp.exp(log_w.astype(f32)))
    a = jax.nn.sigmoid(a0 + al @ a_up)
    g = jax.nn.sigmoid(gl) @ g_up
    if vl is None:
        v_first = v
    else:
        v = v + (v_first - v) * jax.nn.sigmoid(v0 + vl @ v_up)

    def heads(t):
        return t.reshape(B, S, N_HEADS, HEAD_SIZE).astype(f32)

    kk = heads(k * k_k)
    kk = kk / jnp.maximum(jnp.sqrt(jnp.sum(kk * kk, axis=-1, keepdims=True)), 1e-12)
    k = k * (1 + (a - 1) * k_a)
    r_h, k_h, v_h, a_h, w_h = heads(r), heads(k), heads(v), heads(a), heads(decay)

    y = wkv7_scan(r_h, w_h, k_h, v_h, kk, a_h)
    mean = jnp.mean(y, axis=-1, keepdims=True)
    var = jnp.mean(jnp.square(y - mean), axis=-1, keepdims=True)
    y = (y - mean) * lax.rsqrt(var + EPS_GN)
    y = y.reshape(B, S, D_RWKV) * lnx_g.astype(f32) + lnx_b.astype(f32)
    bonus = jnp.sum(r_h * k_h * r_k.astype(f32), axis=-1, keepdims=True) * v_h
    y = (y + bonus.reshape(B, S, D_RWKV)) * g.astype(f32)
    return y.astype(dt), v_first

def multiscale_pool(z, pool_w, pool_scale):
    B, S, _ = z.shape
    zg = z.reshape(B, S, N_POOL_GROUPS, POOL_GROUP).astype(jnp.float32)
    cs = jnp.cumsum(zg, axis=1)
    pos = jnp.arange(1, S + 1, dtype=jnp.float32)
    means = []
    for gi, win in enumerate(POOL_WINDOWS):
        cg = cs[:, :, gi]
        lower = jnp.pad(cg, ((0, 0), (win, 0), (0, 0)))[:, :S]
        count = jnp.minimum(pos, float(win))[None, :, None]
        means.append((cg - lower) / count)
    pooled = (jnp.stack(means, axis=2) - zg).astype(z.dtype)
    y = jnp.einsum('bsgc,gcd->bsgd', pooled, pool_w)
    return y.reshape(B, S, D_POOL) * pool_scale

def second_inputs(seed: int = 0) -> dict:
    key = jax.random.key(seed)
    ks = iter(jax.random.split(key, 32))
    f32 = jnp.float32

    def nrm(shape, s):
        return jax.random.normal(next(ks), shape, f32) * s

    def uni(shape, lo, hi):
        return jax.random.uniform(next(ks), shape, f32, lo, hi)

    L, Lv = DEPTH, DEPTH - 1
    return {
        "x": nrm((BATCH, SEQ, D_MODEL), 1.0),
        "c": nrm((BATCH, D_MODEL), 1.0),
        "ada_w": nrm((L, D_MODEL, N_MOD), 0.5 * D_MODEL ** -0.5),
        "ada_b": nrm((L, N_MOD), 0.1),
        "norm1_g": 1.0 + nrm((L, D_MODEL), 0.1),
        "w_in": nrm((L, D_MODEL, N_IN), D_MODEL ** -0.5),
        "v_down": nrm((Lv, D_MODEL, D_MV_LORA), D_MODEL ** -0.5),
        "mu_shift": uni((L, N_SHIFT), 0.0, 1.0),
        "mu_v": uni((Lv, D_MV_LORA), 0.0, 1.0),
        "w0": uni((L, D_RWKV), -6.0, -1.0),
        "w_up": nrm((L, D_DECAY_LORA, D_RWKV), 0.5 * D_DECAY_LORA ** -0.5),
        "a0": nrm((L, D_RWKV), 0.1),
        "a_up": nrm((L, D_AAA_LORA, D_RWKV), 0.5 * D_AAA_LORA ** -0.5),
        "v0": nrm((Lv, D_RWKV), 0.1),
        "v_up": nrm((Lv, D_MV_LORA, D_RWKV), 0.5 * D_MV_LORA ** -0.5),
        "g_up": nrm((L, D_GATE_LORA, D_RWKV), D_GATE_LORA ** -0.5),
        "k_k": 0.85 + nrm((L, D_RWKV), 0.05),
        "k_a": 1.0 + nrm((L, D_RWKV), 0.05),
        "r_k": nrm((L, N_HEADS, HEAD_SIZE), 0.1),
        "lnx_g": 1.0 + nrm((L, D_RWKV), 0.1),
        "lnx_b": nrm((L, D_RWKV), 0.02),
        "pool_w": nrm((L, N_POOL_GROUPS, POOL_GROUP, POOL_GROUP), POOL_GROUP ** -0.5),
        "pool_scale": 1.0 + nrm((L, D_POOL), 0.1),
        "proj_a": nrm((L, D_RWKV, D_MODEL), D_RWKV ** -0.5),
        "proj_b": nrm((L, D_POOL, D_MODEL), D_POOL ** -0.5),
        "w_out": nrm((L, D_MODEL, D_MODEL), D_MODEL ** -0.5),
        "norm2_g": 1.0 + nrm((L, D_MODEL), 0.1),
        "w_gu": nrm((L, D_MODEL, 2 * D_FF_2), D_MODEL ** -0.5),
        "w_down": nrm((L, D_FF_2, D_MODEL), D_FF_2 ** -0.5),
        "final_g": 1.0 + nrm((D_MODEL,), 0.1),
    }

def second_block(x, c, ada_w, ada_b, norm1_g, w_in, v_down, mu_shift, mu_v, w0, w_up, a0, a_up, v0, v_up,
              g_up, k_k, k_a, r_k, lnx_g, lnx_b, pool_w, pool_scale, proj_a, proj_b, w_out, norm2_g,
              w_gu, w_down, final_g):
    B, S, D = x.shape
    c_act = jax.nn.silu(c)
    v_first = None
    for l in range(DEPTH):
        mod = c_act @ ada_w[l] + ada_b[l]
        sh1, sc1, gt1, sh2, sc2, gt2 = [m[:, None, :] for m in jnp.split(mod, 6, axis=-1)]

        h = rms_norm_2(x, norm1_g[l]) * (1 + sc1) + sh1
        if l == 0:
            p = h @ w_in[0]
            vl = None
        else:
            p = h @ jnp.concatenate([w_in[l], v_down[l - 1]], axis=1)
            vl = token_shift(p[..., N_IN:], mu_v[l - 1])
        ps = token_shift(p[..., :N_SHIFT], mu_shift[l])
        z_pool = p[..., N_SHIFT:N_SHIFT + D_POOL]
        br_gate = jax.nn.sigmoid(p[..., N_SHIFT + D_POOL:N_IN]).reshape(B, S, 2, D)

        y_a, v_first = rwkv7_time_mix(ps, vl, v_first, w0[l], w_up[l], a0[l], a_up[l],
                                      None if l == 0 else v0[l - 1], None if l == 0 else v_up[l - 1],
                                      g_up[l], k_k[l], k_a[l], r_k[l], lnx_g[l], lnx_b[l])
        y_b = multiscale_pool(z_pool, pool_w[l], pool_scale[l])
        mixed = br_gate[:, :, 0] * (y_a @ proj_a[l]) + br_gate[:, :, 1] * (y_b @ proj_b[l])
        x = x + gt1 * (mixed @ w_out[l])

        h2 = rms_norm_2(x, norm2_g[l]) * (1 + sc2) + sh2
        gate, up = jnp.split(h2 @ w_gu[l], 2, axis=-1)
        x = x + gt2 * ((jax.nn.silu(gate) * up) @ w_down[l])
    return rms_norm_2(x, final_g)


def setup_inputs(seed=0):
    out = dict(first_inputs(seed))
    for name, value in second_inputs(seed + 1).items():
        if name != "x":
            out[name + "_2"] = value
    return out


def reference(
    x, mem, norm_mix, norm_mem, w_mem_kv, xa_q_gain, xa_k_gain, w_out, norm_mlp, w_mlp_in,
    w_mlp_out, w_in_a, conv_w, conv_b, w_rgate, b_rgate, w_igate, b_igate, lru_lambda, w_in_b,
    b_forget, fox_q_gain, fox_k_gain, c_2, ada_w_2, ada_b_2, norm1_g_2, w_in_2, v_down_2,
    mu_shift_2, mu_v_2, w0_2, w_up_2, a0_2, a_up_2, v0_2, v_up_2, g_up_2, k_k_2, k_a_2, r_k_2,
    lnx_g_2, lnx_b_2, pool_w_2, pool_scale_2, proj_a_2, proj_b_2, w_out_2, norm2_g_2, w_gu_2,
    w_down_2, final_g_2,
):
    x = first_block(
        x, mem, norm_mix, norm_mem, w_mem_kv, xa_q_gain, xa_k_gain, w_out, norm_mlp, w_mlp_in,
        w_mlp_out, w_in_a, conv_w, conv_b, w_rgate, b_rgate, w_igate, b_igate, lru_lambda,
        w_in_b, b_forget, fox_q_gain, fox_k_gain,
    )
    return second_block(
        x, c_2, ada_w_2, ada_b_2, norm1_g_2, w_in_2, v_down_2, mu_shift_2, mu_v_2, w0_2, w_up_2,
        a0_2, a_up_2, v0_2, v_up_2, g_up_2, k_k_2, k_a_2, r_k_2, lnx_g_2, lnx_b_2, pool_w_2,
        pool_scale_2, proj_a_2, proj_b_2, w_out_2, norm2_g_2, w_gu_2, w_down_2, final_g_2,
    )


_drawn_inputs = setup_inputs


def setup_inputs(seed=0):
    import zlib

    import numpy as np

    out = dict(_drawn_inputs(seed))
    spreads = {}
    factors = {'norm_mem': 8.0,
     'xa_q_gain': 8.0,
     'xa_k_gain': 8.0,
     'b_rgate': 8.0,
     'b_igate': 8.0,
     'fox_q_gain': 8.0,
     'fox_k_gain': 8.0,
     'norm1_g_2': 3.423,
     'v_down_2': 5.148,
     'mu_v_2': 8.0,
     'w_up_2': 8.0,
     'a0_2': 8.0,
     'a_up_2': 3.713,
     'v0_2': 41.435,
     'v_up_2': 5.525,
     'k_k_2': 35.336,
     'k_a_2': 5.481,
     'r_k_2': 2.855,
     'lnx_g_2': 7.761,
     'lnx_b_2': 64.0,
     'pool_scale_2': 5.754,
     'norm2_g_2': 7.276}
    for name, (base, spread) in spreads.items():
        noise = np.random.default_rng([zlib.crc32(name.encode()), seed]).standard_normal(out[name].shape)
        drawn = base * np.exp(spread * noise) if base else spread * noise
        out[name] = __import__('jax').numpy.asarray(drawn.astype(out[name].dtype))
    for name, factor in factors.items():
        out[name] = (out[name] * factor).astype(out[name].dtype)
    return out
```

```python
from contextlib import ExitStack

import concourse.bass as bass
from concourse import mybir

F32 = mybir.dt.float32
F32R = mybir.dt.float32r
ALU = mybir.AluOpType
ACT = mybir.ActivationFunctionType
AX = mybir.AxisListType

P = 128
D = 1024
T = 512
KT = D // P
NT = T // P
MEM = 256
MT_ = MEM // P
D_FF = 4096
D_FF2 = 2816
FOX_H = 8
HD = 64
XA_H = 4
CH = 64
SLAB = 256
BANKS = 8
NORMS = 9
EPS = 1e-6
EPS_GN = 64e-5
KAPPA = 0.6065306597126334
WINDOWS = (2, 4, 8, 16)
SHIFT_TILES = 15
ADA_COLS = 192
N_MOD = 6 * D
LEVELS = (2, 4, 8, 16, 32)
FF_TILES = 8
CHUNKS1 = D_FF // (FF_TILES * P)
CHUNKS2 = [8, 8, 6]


def loop(eng, n):
    with eng.Fori(0, n) as c:
        yield c


def vector_rows():
    tiles = [
        [("norm_mix", 16), ("norm_mem", 16), ("norm_mlp", 16), ("conv_w", 16), ("conv_b", 4), ("b_rgate", 4),
         ("b_igate", 4), ("lru_lambda", 4), ("xa_q_gain", 2), ("xa_k_gain", 2), ("fox_q_gain", 1),
         ("fox_k_gain", 1), ("c_2", 8), ("final_g_2", 8), ("norm1_g_2", 16)],
        [("norm2_g_2", 16), ("w0_2", 8), ("a0_2", 8), ("v0_2", 4), ("k_k_2", 8), ("k_a_2", 8), ("r_k_2", 8),
         ("lnx_g_2", 8), ("lnx_b_2", 8), ("pool_scale_2", 8), ("mu_shift_2", 30), ("mu_v_2", 1),
         ("b_forget", 1)],
        [("ada_b_2", 96)],
    ]
    at = {}
    for i, tile in enumerate(tiles):
        row = 0
        for name, n in tile:
            at[name] = (i * P + row, n)
            row += n
        assert row <= P
    return at


class Plan:

    def __init__(self):
        self.job = {}
        self.slab = {}
        self.last = []
        self.n = 0
        self.walk()

    def add(self, *key):
        assert key not in self.job, key
        self.job[key] = self.n
        self.n += 1

    def lin(self, name, layer, slabs, blocks=2):
        for s in range(slabs):
            self.slab[name, layer, s] = len(self.last)
            for b in range(blocks):
                self.add(name, layer, s, b)
            self.last.append(self.n - 1)

    def attend(self, name, layer, units):
        for i in range(units + 2):
            if i < units:
                self.add(name + "_s", layer, i)
            if 1 <= i <= units:
                self.add(name + "_t", layer, i - 1)
            if i >= 2:
                self.add(name + "_o", layer, i - 2)

    def walk(self):
        for i in range(3):
            self.add("vec", i)
        for t in range(KT):
            self.add("xT", t)
        for i in range(4):
            self.add("memT", i)
        for l in range(2):
            self.add("ms", 2 * l)
            self.lin("memk", l, 2)
            self.lin("memv", l, 2)
            if l == 0:
                for name in ("u", "gate", "xq"):
                    self.lin(name, l, 2)
                for i in range(8):
                    self.add("hn", l, i)
                for t in range(4):
                    self.add("rgate", t)
                    self.add("igate", t)
            else:
                for name in ("q", "k"):
                    self.lin(name, l, 2)
                self.lin("v", l, 2, 4)
                self.lin("f", l, 1, 1)
                self.lin("xq", l, 2)
                for i in range(24):
                    self.add("hn", l, i)
                self.attend("fox", l, 4 * FOX_H)
            self.attend("xa", l, 2 * XA_H)
            self.lin("wo", l, 4)
            self.add("ms", 2 * l + 1)
            for c in range(CHUNKS1):
                self.lin("up", (l, c), 4)
                self.lin("down", (l, c), 4)
            self.add("mod", l)
        for l in range(2):
            self.add("ms", 4 + 2 * l)
            for name in ("r2", "k2", "v2"):
                self.lin(name, l, 2)
            self.lin("lat", l, 1)
            self.lin("gl1", l, 1, 1)
            if l:
                self.lin("vl", l, 1, 1)
            for t in range(4):
                self.add("lw", l, t)
            for t in range(4):
                self.add("la", l, t)
            if l:
                for t in range(4):
                    self.add("lv", l, t)
            for t in range(4):
                self.add("kn", l, t)
            for t in range(4):
                self.add("bon", l, t)
            for m in range(NT):
                for x in range(4):
                    self.add("tok", l, m, x)
                for i in range(2):
                    self.add("LT", l, m, i)
                for i in range(2):
                    self.add("Akk", l, m, i)
                for i in range(2):
                    self.add("L1", l, m, i)
                for b in LEVELS:
                    for i in range(2):
                        self.add("LM", l, m, b, i)
                    for i in range(2):
                        if b < LEVELS[-1]:
                            self.add("MLM", l, m, b, i)
                        self.add("MLMt", l, m, b, i)
                for i in range(2):
                    self.add("Ark", l, m, i)
                for i in range(2):
                    self.add("Arb", l, m, i)
                self.add("AkkV", l, m)
                for i in range(2):
                    self.add("WU", l, m, i)
                self.add("WT", l, m)
                for c in range(2):
                    self.add("NH", l, m, c)
                for c in range(2):
                    for i in range(2):
                        self.add("S", l, m, c, i)
                for i in range(2):
                    self.add("U", l, m, i)
                for i in range(2):
                    self.add("Y", l, m, i)
            for t in range(4):
                self.add("gmean", l, t)
            for t in range(4):
                self.add("gvar", l, t)
            for t in range(4):
                self.add("g", l, t)
            self.lin("z", l, 2)
            for t in range(4):
                self.add("pool", l, t)
            for p in range(4):
                for name in ("g0", "g1", "pa", "pb"):
                    self.lin(name, (l, p), 1)
            self.lin("wo2", l, 4)
            self.add("ms", 5 + 2 * l)
            for c, n in enumerate(CHUNKS2):
                for i in range(n // 2):
                    self.lin("fg", (l, c, i), 1)
                    self.lin("fu", (l, c, i), 1)
                self.lin("fd", (l, c), 4)
        self.add("ms", 8)
        for i in range(8):
            self.add("outT", i)


class Seq:

    def __init__(self, eng, sem):
        self.eng, self.sem, self.n = eng, sem, 0

    def mark(self, ins):
        self.n += 1
        ins.then_inc(self.sem, 1)

    def step(self, ins):
        self.mark(ins)
        self.settle()

    def settle(self):
        self.eng.wait_ge(self.sem, self.n)


def program(nc, d, out):
    plan = Plan()
    J = plan.job
    VEC = vector_rows()
    ctx = ExitStack()
    with ctx:
        def sb(name, shape, dt=F32, at=None):
            return (at or ctx).enter_context(nc.sbuf_tensor(name, shape, dt))

        def sem(name):
            return ctx.enter_context(nc.semaphore(name))

        psum = ctx.enter_context(nc.psum_tensor("psum", [P, BANKS, 512], F32))
        xT = sb("xT", [P, KT, T])
        raw = sb("raw", [P, 2, KT, SLAB])
        whi = sb("whi", [P, 2, KT, SLAB], F32R)
        wlo = sb("wlo", [P, 2, KT, SLAB], F32R)
        vrows = sb("vrows", [P, 3, P])
        vec = sb("vec", [P, 3 * P])
        ident = sb("ident", [P, P])
        ident2 = sb("ident2", [P, HD])
        mean_all = sb("mean_all", [P, P])
        mean_128 = sb("mean_128", [P, P])
        mean_64 = sb("mean_64", [P, P])
        sum_64 = sb("sum_64", [P, P])
        ones = sb("ones", [P, 8])
        zeros = sb("zeros", [P, P])
        causal = sb("causal", [P, P])
        strict = sb("strict", [P, P])
        incl = sb("incl", [P, P])
        pairup = sb("pairup", [P, P])
        lvl = sb("lvl", [P, 1 + len(LEVELS), P])
        keep = sb("keep", [P, T])
        invc = sb("invc", [P, 4, 16])
        epst = sb("epst", [P, 2])
        cact = sb("cact", [P, 8])
        mod = sb("mod", [P, 2, 48])
        gmod = sb("gmod", [P, 4, 8])
        omm = sb("omm", [P, 31])
        nsp = sb("nsp", [P, 4])
        tiny = sb("tiny", [P, 8, 8])
        gq8 = sb("gq8", [P, 2])
        stat = sb("stat", [P, 3, 4])
        PC = sb("PC", [P, 4, T // CH])
        e = ExitStack()
        hh = sb("hh", [P, KT, T], F32R, e)
        hl = sb("hl", [P, KT, T], F32R, e)
        e.close()
        ho = sb("ho", [P, 2 * KT * T])
        e = ExitStack()
        mh = sb("mh", [P, KT, T], F32R, e)
        ml = sb("ml", [P, KT, T], F32R, e)
        e.close()
        mo = sb("mo", [P, 2 * KT * T])
        REST = 16 * 1024
        rest = sb("rest", [P, REST])

        def carve(buf, off, *shape):
            n = 1
            for x in shape:
                n *= x
            assert off + n <= buf.shape[1], (off, shape)
            v = buf[:, off:off + n]
            names = "abcd"[:len(shape)]
            if len(shape) == 1:
                return v
            return v.rearrange(f"p ({' '.join(names)}) -> p {' '.join(names)}",
                               **{k: s for k, s in zip(names, shape)})

        B = 4 * T
        x_tok = carve(mo, 0, NT, D)
        mem_tok = carve(mo, NT * D, MT_, D)
        mem_sq = carve(mo, NT * D + MT_ * D, D)
        blockm = carve(rest, REST - 7 * P, 7, P)
        memT = carve(rest, 0, KT, MEM)
        V2 = carve(rest, 0, 4, T)
        n_sq = carve(rest, B, 3, T)
        n_acc = carve(rest, B + 3 * T, T)
        n_rs = carve(rest, B + 4 * T, T)
        n_rstd = carve(rest, B + 5 * T, T)
        n_val = carve(rest, B + 6 * T, 3, T)
        f_t = carve(rest, B, 2, T)
        f_v = carve(rest, B + 2 * T, 2, T)
        ada = carve(rest, B + 9 * T, 2, KT, ADA_COLS)
        ada_acc = carve(rest, B + 9 * T + 2 * KT * ADA_COLS, N_MOD)
        mK = carve(rest, B, 4, MEM)
        mV = carve(rest, B + 2 * T, MT_, T)
        XQ = carve(rest, B + 4 * T, 4, T)
        o = B + 8 * T
        U = carve(rest, o, 4, T + 3)
        G = carve(rest, o + B + 12, 4, T)
        UC = carve(rest, o + 2 * B + 12, 4, T)
        WR = carve(rest, o + 3 * B + 12, 4, P)
        WI = carve(rest, o + 3 * B + 12 + T, 4, P)
        RB = carve(ho, 0, 4, T)
        IB = carve(ho, B, 4, T)
        DB = carve(ho, 2 * B, 4, T)
        vtok = carve(rest, o, NT, T)
        qaug = carve(rest, o + B, FOX_H, T)
        kaug = carve(rest, o + B + FOX_H * T, FOX_H, T)
        fbuf = carve(ho, 3 * B, 4, T)
        a_p = carve(ho, 2 * B, 2, T)
        a_t = carve(ho, 2 * B + 2 * T, 2, T)
        h_sq = carve(ho, 0, 2, T)
        h_rs = carve(ho, 2 * T, 2, T)
        R2, K2, A2, KK, BON = (carve(rest, (1 + i) * B, 4, T) for i in range(5))
        o = 6 * B
        GL = carve(rest, o, 2, T)
        ST = carve(rest, o + 2 * T, 3, 4, HD)
        o += 2 * T + 3 * 4 * HD
        LA = carve(rest, o, T)
        VL = carve(rest, o + T, T)
        WA = carve(rest, o + 2 * T, T)
        VU = carve(rest, o + 3 * T, T)
        GU = carve(rest, o, 2, T)
        PW = carve(rest, o + 2 * T, 4, P)
        SG, C2, X1, X2 = (carve(mo, i * B, 4, T) for i in range(4))
        Q = 8 * P
        LT, MM, MT, T1, AK = (carve(mo, i * Q, 2, 4, P) for i in range(5))
        AR, AB = MM, LT
        WU = carve(mo, 3 * Q, 8, P)
        WT = carve(mo, 4 * Q, 4, P)
        NU = carve(mo, 4 * Q + T, 8, HD)
        KA = carve(mo, 5 * Q, 2, T)
        BT = carve(mo, 6 * Q, T)
        KhT = carve(mo, 6 * Q + T, T)
        VT = carve(mo, 7 * Q, T)
        GS = carve(mo, 7 * Q + T, 2, 4, HD)
        HS = KA[:, 1, :].rearrange("p (c j k) -> p c j k", c=2, j=4)
        mixed = [K2[:, t, :] for t in range(4)] + [A2[:, t, :] for t in range(4)]
        o_val = carve(ho, 0, KT, T)
        o_tok = carve(mo, 0, NT, D)

        made = {}

        def S(name):
            if name not in made:
                made[name] = ctx.enter_context(nc.semaphore(name))
            return made[name]

        s_vec = S("vectors_landed")
        s_x = S("x_landed")
        s_mem = S("mem_landed")
        s_const = S("constants")
        s_small = S("small_landed")
        s_lora = S("lora_landed")
        s_aug = S("decay_rows_landed")
        s_out = S("output_written")
        landed = [S(f"slab_landed{i}") for i in range(2)]
        ada_landed = [S(f"ada_landed{i}") for i in range(2)]
        hi_done = S("hi_done")
        raw_used = S("raw_used")
        written = S("written")
        bank_read = [S(f"bank_read{i}") for i in range(BANKS)]
        hid_hi = S("hidden_hi")
        hid_done = S("hidden_done")
        ada_done = S("ada_done")
        block = ctx.enter_context(nc.Block())

        def V(name, i=0, rows=P):
            c = VEC[name][0] + i
            return vec[0:rows, c:c + 1]

        def bank(job):
            return psum[:, job % BANKS, :]

        def half(x):
            return x[:, None, :]

        def ready(eng, job, more=0):
            eng.wait_ge(written, job + 1 + more)

        def evacuated(eng, job, more=0):
            eng.wait_ge(bank_read[job % BANKS], job // BANKS + 1 + more)

        def x_ready(eng, ver, t):
            if ver == 0:
                evacuated(eng, J["xT", t])
            elif ver < 5 and ver % 2:
                evacuated(eng, J["wo", ver // 2, t // 2, t % 2])
            elif ver < 5:
                evacuated(eng, J["down", (ver // 2 - 1, CHUNKS1 - 1), t // 2, t % 2])
            elif ver % 2:
                evacuated(eng, J["wo2", (ver - 5) // 2, t // 2, t % 2])
            else:
                evacuated(eng, J["fd", ((ver - 6) // 2, len(CHUNKS2) - 1), t // 2, t % 2])

        def bc(m, n=4):
            return m.rearrange("p (a b) -> p a b", a=1).to_broadcast([P, n, P])

        @block.sync
        def _(sp):
            def rows(name, src):
                c, n = VEC[name]
                sp.dma_start(vrows[c % P:c % P + n, c // P, :], src).then_inc(s_vec, 16)
                return 16

            sp.dma_start(x_tok, d["x"][0].rearrange("(t p) f -> p t f", p=P)).then_inc(s_x, 16)
            sp.dma_start(mem_tok, d["mem"][0].rearrange("(t p) f -> p t f", p=P)).then_inc(s_mem, 16)
            sp.wait_ge(s_const, 1)
            for name in ("norm_mix", "norm_mem", "norm_mlp", "conv_b", "b_rgate", "b_igate", "lru_lambda",
                         "xa_q_gain", "xa_k_gain", "c_2", "norm1_g_2", "norm2_g_2", "w0_2", "a0_2", "v0_2",
                         "k_k_2", "k_a_2", "lnx_g_2", "lnx_b_2", "pool_scale_2", "ada_b_2"):
                rows(name, d[name].rearrange("l (t p) -> (l t) p", p=P))
            rows("conv_w", d["conv_w"][0].rearrange("j (t p) -> (j t) p", p=P))
            rows("r_k_2", d["r_k_2"].rearrange("l (t h) n -> (l t) (h n)", h=2))
            rows("final_g_2", d["final_g_2"].rearrange("(t p) -> t p", p=P))
            for name in ("fox_q_gain", "fox_k_gain"):
                c = VEC[name][0]
                for i in range(2):
                    sp.dma_start(vrows[c % P:c % P + 1, c // P, i * HD:(i + 1) * HD], d[name]).then_inc(s_vec, 16)
            c = VEC["mu_shift_2"][0]
            for l in range(2):
                a = c % P + SHIFT_TILES * l
                sp.dma_start(vrows[a:a + 14, c // P, :],
                             d["mu_shift_2"][l, 0:14 * P].rearrange("(t p) -> t p", p=P)).then_inc(s_vec, 16)
                sp.dma_start(vrows[a + 14:a + 15, c // P, 0:32], d["mu_shift_2"][l:l + 1, 14 * P:14 * P + 32])\
                    .then_inc(s_vec, 16)
            for name, n in (("mu_v_2", 32), ("b_forget", 8)):
                c = VEC[name][0]
                sp.dma_start(vrows[c % P:c % P + 1, c // P, 0:n], d[name]).then_inc(s_vec, 16)
            for n in range(8):
                a, t = HD * (n % 2), n // 2
                sp.dma_start(WR[a:a + HD, t, a:a + HD], d["w_rgate"][0, n]).then_inc(s_small, 16)
                sp.dma_start(WI[a:a + HD, t, a:a + HD], d["w_igate"][0, n]).then_inc(s_small, 16)

            def cols(w):
                return w.rearrange("(k p) n -> p k n", p=P)

            def slab(g, src, K=KT, n=SLAB, more=0):
                if g >= 2:
                    sp.wait_ge(raw_used, g - 1 + more)
                sp.dma_start(raw[:, g % 2, 0:K, 0:n], src).then_inc(landed[g % 2], 16)

            def lin(name, layer, w, col, slabs=2):
                for s in range(slabs):
                    slab(plan.slab[name, layer, s], cols(w)[:, :, col + s * SLAB:col + (s + 1) * SLAB])

            for l in range(2):
                lin("memk", l, d["w_mem_kv"][l], 0)
                lin("memv", l, d["w_mem_kv"][l], T)
                if l == 0:
                    for i, name in enumerate(("u", "gate", "xq")):
                        lin(name, l, d["w_in_a"][0], i * T)
                else:
                    for i, name in enumerate(("q", "k", "v")):
                        lin(name, l, d["w_in_b"][0], i * T)
                    slab(plan.slab["f", l, 0], cols(d["w_in_b"][0])[:, :, 3 * T:3 * T + P], n=P)
                    lin("xq", l, d["w_in_b"][0], 3 * T + FOX_H)
                lin("wo", l, d["w_out"][l], 0, 4)
                g0 = plan.slab["up", (l, 0), 0]
                for c in loop(sp, CHUNKS1):
                    for i in range(4):
                        slab(g0 + i, cols(d["w_mlp_in"][l])[:, :, bass.ds(c * D + i * SLAB, SLAB)], more=8 * c)
                    for i in range(4):
                        slab(g0 + 4 + i, cols(d["w_mlp_out"][l])[:, bass.ds(c * KT, KT), i * SLAB:(i + 1) * SLAB],
                             more=8 * c)
            for l in range(2):
                w = d["w_in_2"][l]
                lin("r2", l, w, 0)
                lin("k2", l, w, T)
                lin("v2", l, w, 2 * T)
                lin("lat", l, w, 3 * T, 1)
                slab(plan.slab["gl1", l, 0], cols(w)[:, :, 14 * P:15 * P], n=P)
                if l:
                    slab(plan.slab["vl", l, 0], cols(d["v_down_2"][0]), n=32)
                lin("z", l, w, 1824)
                for p in range(4):
                    for i, name in enumerate(("g0", "g1")):
                        slab(plan.slab[name, (l, p), 0],
                             cols(w)[:, :, 1824 + T + i * D + p * SLAB:1824 + T + i * D + (p + 1) * SLAB])
                    for name in ("pa", "pb"):
                        slab(plan.slab[name, (l, p), 0],
                             cols(d[{"pa": "proj_a_2", "pb": "proj_b_2"}[name]][l])[:, :, p * SLAB:(p + 1) * SLAB], K=4)
                lin("wo2", l, d["w_out_2"][l], 0, 4)
                wg, wd = d["w_gu_2"][l], d["w_down_2"][l]
                for c in loop(sp, 2):
                    g0 = plan.slab["fg", (l, 0, 0), 0]
                    for i in range(4):
                        slab(g0 + 2 * i, cols(wg)[:, :, bass.ds(c * D + i * SLAB, SLAB)], more=12 * c)
                        slab(g0 + 2 * i + 1, cols(wg)[:, :, bass.ds(c * D + D_FF2 + i * SLAB, SLAB)], more=12 * c)
                    for i in range(4):
                        slab(g0 + 8 + i, cols(wd)[:, bass.ds(c * KT, KT), i * SLAB:(i + 1) * SLAB], more=12 * c)
                for i in range(3):
                    g0 = plan.slab["fg", (l, 2, i), 0]
                    slab(g0, cols(wg)[:, :, 2 * D + i * SLAB:2 * D + (i + 1) * SLAB])
                    slab(g0 + 1, cols(wg)[:, :, 2 * D + D_FF2 + i * SLAB:2 * D + D_FF2 + (i + 1) * SLAB])
                for i in range(4):
                    slab(plan.slab["fd", (l, 2), i], cols(wd)[:, 16:22, i * SLAB:(i + 1) * SLAB], K=6)
            for t in range(NT):
                evacuated(sp, J["outT", 2 * t])
                evacuated(sp, J["outT", 2 * t + 1])
                sp.dma_start(out[0, t * P:(t + 1) * P, :], o_tok[:, t, :]).then_inc(s_out, 16)
            sp.wait_ge(s_out, 16 * NT)

        @block.gpsimd
        def _(pool):
            q = Seq(pool, S("pool_seq"))
            q.step(pool.memset(vrows[:, :, :], 0.0))
            q.step(pool.memset(WR, 0.0))
            pool.memset(WI, 0.0).then_inc(s_const, 1)
            pool.wait_ge(s_const, 1)
            q.step(pool.memset(zeros[:, :], 0.0))
            q.step(pool.memset(blockm[:, :, :], 1.0))
            q.step(pool.memset(ones[:, :], 1.0))
            q.step(pool.memset(mean_all[:, :], 1.0 / D))
            q.step(pool.memset(mean_128[:, :], 1.0 / P))
            for m, v in ((mean_64, 1.0 / HD), (sum_64, 1.0)):
                q.step(pool.memset(m[:, :], 0.0))
                q.step(pool.memset(m[0:HD, 0:HD], v))
                q.step(pool.memset(m[HD:P, HD:P], v))
            q.step(pool.memset(epst[:, 0:1], EPS))
            q.step(pool.memset(epst[:, 1:2], EPS_GN))
            q.step(pool.memset(keep[:, :], 1.0))
            for g, w in enumerate(WINDOWS):
                q.step(pool.memset(invc[:, g, :], 1.0 / w))
            for g, w in enumerate(WINDOWS):
                for t in range(w - 1):
                    q.step(pool.memset(invc[:, g, t:t + 1], 1.0 / (t + 1)))
            q.step(pool.memset(keep[:, 0:T:CH], 0.0))
            q.step(pool.affine_select(out=ident[:, :], in_=zeros[:, :], compare_op=ALU.not_equal, fill=1.0, base=0,
                                      pattern=[[-1, P]], channel_multiplier=1))
            q.step(pool.affine_select(out=causal[:, :], in_=zeros[:, :], compare_op=ALU.is_ge, fill=-1e30, base=0,
                                      pattern=[[-1, P]], channel_multiplier=1))
            for i in range(7):
                b = 2 ** i
                m = blockm[:, i, :].rearrange("p (a b) -> p a b", b=b)
                q.step(pool.affine_select(out=m, in_=m, compare_op=ALU.is_ge, fill=0.0, base=0,
                                          pattern=[[-b, P // b], [0, b]], channel_multiplier=1))
                q.step(pool.affine_select(out=m, in_=m, compare_op=ALU.is_ge, fill=0.0, base=b - 1,
                                          pattern=[[b, P // b], [0, b]], channel_multiplier=-1))
            q.step(pool.tensor_tensor(ident2[:, :], ident[:, 0:HD], ident[:, HD:P], ALU.add))
            q.step(pool.affine_select(out=strict[:, :], in_=blockm[:, 6, :], compare_op=ALU.is_gt, fill=0.0, base=0,
                                      pattern=[[1, P]], channel_multiplier=-1))
            q.step(pool.affine_select(out=incl[:, :], in_=blockm[:, 6, :], compare_op=ALU.is_ge, fill=0.0, base=0,
                                      pattern=[[1, P]], channel_multiplier=-1))
            q.step(pool.affine_select(out=pairup[:, :], in_=blockm[:, 1, :], compare_op=ALU.is_gt, fill=0.0, base=0,
                                      pattern=[[1, P]], channel_multiplier=-1))
            for i in range(6):
                q.step(pool.tensor_tensor(lvl[:, i, :], blockm[:, i + 1, :], blockm[:, i, :], ALU.subtract))
            for i in range(6):
                q.step(pool.affine_select(out=lvl[:, i, :], in_=lvl[:, i, :], compare_op=ALU.is_gt, fill=0.0, base=0,
                                          pattern=[[-1, P]], channel_multiplier=1))
            pool.memset(tiny[:, :, :], 0.0).then_inc(s_const, 1)
            pool.sem_inc(hid_done, 2)
            pool.sem_inc(ada_done, 16)
            per = N_MOD // ADA_COLS // CHUNKS1
            for l in range(2):
                if l:
                    pool.wait_ge(S("decay_rows"), 2)
                    pool.dma_start(qaug[HD:HD + 1, :, :], fbuf[0:FOX_H, 0, :]).then_inc(s_aug, 16)
                    pool.dma_start(kaug[HD + 1:HD + 2, :, :], fbuf[0:FOX_H, 1, :]).then_inc(s_aug, 16)
                ready(pool, J["ms", 2 * l + 1])
                w = d["ada_w_2"][l].rearrange("(k p) n -> p k n", p=P)
                n0 = l * CHUNKS1 * per
                for c in loop(pool, CHUNKS1):
                    for s in range(per):
                        pool.wait_ge(ada_done, 8 * (n0 + s) + 8 + c * (8 * per))
                        pool.dma_start(ada[:, s % 2, :, :], w[:, :, bass.ds(c * (per * ADA_COLS) + s * ADA_COLS, ADA_COLS)])\
                            .then_inc(ada_landed[s % 2], 16)
            for l in range(2):
                ready(pool, J["mod", 1] if l == 0 else J["pool", 0, 3])
                pool.dma_start(WA[0:HD, :], d["w_up_2"][l]).then_inc(s_lora, 16)
                pool.dma_start(WA[HD:P, :], d["a_up_2"][l]).then_inc(s_lora, 16)
                if l:
                    pool.dma_start(VU[0:32, :], d["v_up_2"][0]).then_inc(s_lora, 16)
                ready(pool, J["kn", l, 0])
                pool.dma_start(GU[:, 0, :], d["g_up_2"][l, 0:P, :]).then_inc(s_lora, 16)
                pool.dma_start(GU[0:32, 1, :], d["g_up_2"][l, P:P + 32, :]).then_inc(s_lora, 16)
                pool.dma_start(PW, d["pool_w_2"][l].rearrange("g c d -> c g d")).then_inc(s_lora, 16)

        @block.scalar
        def _(act):
            q = Seq(act, S("act_seq"))

            def hi(g, c=0, slabs=0, last=None, jobs=0):
                if g >= len(plan.last):
                    return
                act.wait_ge(landed[g % 2], 16 * (g // 2 + 1) + 8 * slabs * c)
                if g >= 2:
                    act.wait_ge(written, (plan.last[g - 2] if last is None else last) + 1 + jobs * c)
                act.activation(whi[:, g % 2, :, :], raw[:, g % 2, :, :], ACT.Copy).then_inc(hi_done, 1)

            def free(ins, job):
                ins.then_inc(bank_read[job % BANKS], 1)

            def evac(name, layer, dest, slabs=2, n=T, func=ACT.Copy):
                for s in range(slabs):
                    hi(plan.slab[name, layer, s] + 1)
                    for b in range(2):
                        j = J[name, layer, s, b]
                        ready(act, j)
                        free(act.activation(dest(2 * s + b), bank(j)[:, 0:n], func), j)

            def evac_tokens(name, layer, dest, tiles):
                for s in range(2):
                    hi(plan.slab[name, layer, s] + 1)
                    for b in range(tiles):
                        j = J[name, layer, s, b]
                        ready(act, j)
                        free(act.activation(dest[:, b, s * SLAB:(s + 1) * SLAB], bank(j)[:, 0:SLAB], ACT.Copy), j)

            def norm_squares(ni):
                for t in range(KT):
                    x_ready(act, ni, t)
                    if t >= 3:
                        act.wait_ge(S("norm_added"), 7 * ni + max(1, t - 3))
                    act.activation(n_sq[:, t % 3, :], xT[:, t, :], ACT.Square).then_inc(S("norm_sq"), 1)

            def norm_root(ni):
                j = J["ms", ni]
                ready(act, j)
                free(act.activation(n_rs, bank(j), ACT.Sqrt, bias=epst[:, 0:1]), j)

            def norm_hi(ni, shift=None):
                for t in range(KT):
                    act.wait_ge(S("norm_val"), 8 * ni + t + 1)
                    b = mod[:, shift[0], shift[1] + t:shift[1] + t + 1] if shift else 0.0
                    act.activation(hh[:, t, :], n_val[:, t % 3, :], ACT.Identity, bias=b).then_inc(S("norm_hi"), 1)

            def head_norm(l, tiles):
                base = 0 if l == 0 else 8
                for i in range(len(tiles) + 1):
                    if i < len(tiles):
                        x, r, n = tiles[i]
                        if i >= 2:
                            ready(act, J["hn", l, i - 2])
                        act.activation(h_sq[0:r, i % 2, 0:n], x, ACT.Square).then_inc(S("head_sq"), 1)
                    if i >= 1:
                        x, r, n = tiles[i - 1]
                        j = J["hn", l, i - 1]
                        ready(act, j)
                        if i >= 3:
                            act.wait_ge(S("head_done"), base + i - 2)
                        free(act.activation(h_rs[0:r, (i - 1) % 2, 0:n], bank(j)[0:r, 0:n], ACT.Sqrt,
                                            bias=epst[0:r, 0:1]), j)

            def attention(name, l, units, base, parts, cols, o):
                for i in range(units + 2):
                    if i < units:
                        act.wait_ge(S("att_max"), base + i + 1)
                        if i >= 2:
                            ready(act, J[name + "_t", l, i - 2])
                        for s, (dst, src, scale) in enumerate(parts(i)):
                            c = 2 * (i % 2) + s
                            ins = act.activation(dst, src, ACT.Exp, bias=stat[:, 0, c:c + 1], scale=scale,
                                                 accum_out=stat[:, 1, c:c + 1])
                        free(ins, J[name + "_s", l, i])
                    if 1 <= i <= units:
                        j = J[name + "_t", l, i - 1]
                        ready(act, j)
                        if i >= 3:
                            ready(act, J[name + "_o", l, i - 3])
                        n = cols(i - 1)
                        free(act.activation(a_t[:, (i - 1) % 2, 0:n], bank(j)[:, 0:n], ACT.Copy), j)
                    if i >= 2:
                        j = J[name + "_o", l, i - 2]
                        ready(act, j)
                        dst, src = o(i - 2, bank(j))
                        act.activation(dst, src, ACT.Copy).then_inc(S("att_hi"), 1)

            for i in range(3):
                evacuated(act, J["vec", i])
            act.activation(cact[:, :], vec[:, VEC["c_2"][0]:VEC["c_2"][0] + 8], ACT.Silu).then_inc(S("c_act"), 1)
            act.wait_ge(s_mem, 16)
            act.wait_ge(s_const, 2)
            for t in range(MT_):
                q.mark(act.activation(mem_sq, mem_tok[:, t, :], ACT.Square, accum_out=tiny[:, 0, t:t + 1]))
                q.settle()
            act.activation(tiny[:, 1, 0:2], tiny[:, 0, 0:2], ACT.Sqrt, scale=1.0 / D, bias=epst[:, 0:1])\
               .then_inc(S("mem_root"), 1)
            for t in range(KT):
                j = J["xT", t]
                ready(act, j)
                free(act.activation(xT[:, t, :], bank(j), ACT.Copy), j)
            for i in range(4):
                j = J["memT", i]
                ready(act, j)
                free(act.activation(memT[:, 2 * i:2 * i + 2, :], bank(j).rearrange("p (a b) -> p a b", a=2), ACT.Copy), j)
            act.wait_ge(S("lam_abs"), 1)
            act.activation(tiny[:, 3, 0:4], tiny[:, 2, 0:4], ACT.Exp, scale=-1.0).then_inc(S("lam_exp"), 1)
            hi(0)
            for l in range(2):
                norm_squares(2 * l)
                for i in range(4):
                    evacuated(act, J["memT", i])
                for t in range(KT):
                    act.activation(mh[:, t, 0:MEM], memT[:, t, :], ACT.Copy, scale=V("norm_mem", 8 * l + t))\
                       .then_inc(S("mem_hi"), 1)
                norm_root(2 * l)
                norm_hi(2 * l)
                evac("memk", l, lambda t: mK[:, t, :], n=MEM)
                evac_tokens("memv", l, mV, MT_)
                if l == 0:
                    evac("u", l, lambda t: U[:, t, 3:T + 3])
                    evac("gate", l, lambda t: G[:, t, :], func=ACT.Gelu_apprx_tanh)
                    evac("xq", l, lambda t: XQ[:, t, :])
                    for i in range(4):
                        evacuated(act, J["xq", l, i // 2, i % 2])
                    head_norm(l, [(mK[:, t, :], P, MEM) for t in range(4)] + [(XQ[:, t, :], P, T) for t in range(4)])
                    act.wait_ge(S("head_done"), 8)
                    for t in range(4):
                        for dst, name, b in ((RB, "rgate", "b_rgate"), (IB, "igate", "b_igate")):
                            j = J[name, t]
                            ready(act, j)
                            free(act.activation(dst[:, t, :], bank(j), ACT.Sigmoid, bias=V(b, t)), j)
                    act.wait_ge(S("lru_loga"), 4)
                    act.activation(U[:, :, 0:T], RB, ACT.Tanh, scale=-1.0).then_inc(S("lru_tanh"), 1)
                    act.wait_ge(S("lru_tanh"), 1)
                    act.activation(RB, RB, ACT.Exp).then_inc(S("lru_a"), 1)
                    act.wait_ge(S("lru_1ma2"), 4)
                    act.activation(U[:, :, 0:T], U[:, :, 0:T], ACT.Sqrt).then_inc(S("lru_root"), 1)
                    act.wait_ge(S("lru_y"), 1)
                    act.activation(mh[:, 0:4, :], UC, ACT.Copy).then_inc(S("lru_hi"), 1)
                else:
                    for name, dst in (("q", qaug), ("k", kaug)):
                        for s in range(2):
                            hi(plan.slab[name, l, s] + 1)
                            for b in range(2):
                                j = J[name, l, s, b]
                                ready(act, j)
                                for i in range(2):
                                    ins = act.activation(dst[0:HD, 4 * s + 2 * b + i, :],
                                                         bank(j)[i * HD:(i + 1) * HD, :], ACT.Copy)
                                free(ins, j)
                    evac_tokens("v", l, vtok, NT)
                    hi(plan.slab["f", l, 0] + 1)
                    evac("xq", l, lambda t: XQ[:, t, :])
                    act.wait_ge(S("forget_x"), 1)
                    q.mark(act.activation(fbuf[0:FOX_H, 1, :], fbuf[0:FOX_H, 0, :], ACT.Abs))
                    q.settle()
                    act.activation(fbuf[0:FOX_H, 1, :], fbuf[0:FOX_H, 1, :], ACT.Exp, scale=-1.0).then_inc(S("forget_exp"), 1)
                    for i in range(4):
                        evacuated(act, J["xq", l, i // 2, i % 2])
                    head_norm(l, [(qaug[0:HD, h, :], HD, T) for h in range(FOX_H)]
                              + [(kaug[0:HD, h, :], HD, T) for h in range(FOX_H)]
                              + [(mK[:, t, :], P, MEM) for t in range(4)] + [(XQ[:, t, :], P, T) for t in range(4)])

                    def fox_parts(i):
                        n = P * (i % NT + 1)
                        return [(a_p[:, i % 2, 0:n], bank(J["fox_s", 1, i])[:, 0:n], 1.0)]

                    def fox_o(i, p):
                        h, t = i // NT, i % NT
                        a = HD * (h % 2)
                        return mh[a:a + HD, h // 2, t * P:(t + 1) * P], p[a:a + HD, 0:P]
                    attention("fox", l, 4 * FOX_H, 8, fox_parts, lambda i: P * (i % NT + 1), fox_o)

                def xa_parts(i):
                    b = bank(J["xa_s", l, i])
                    return [(a_p[:, i % 2, s * MEM:(s + 1) * MEM], b[:, s * MEM:(s + 1) * MEM], float(P) ** -0.5)
                            for s in range(2)]
                attention("xa", l, 2 * XA_H, 40 * l, xa_parts, lambda i: T,
                          lambda i, p: (mh[:, 4 + i // 2, (i % 2) * MEM:(i % 2 + 1) * MEM], p[:, 0:MEM]))
                for s in range(4):
                    hi(plan.slab["wo", l, s] + 1)
                norm_squares(2 * l + 1)
                norm_root(2 * l + 1)
                norm_hi(2 * l + 1)
                g0, j0, n0 = plan.slab["up", (l, 0), 0], J["up", (l, 0), 0, 0], 32 * l
                for c in loop(act, CHUNKS1):
                    for i in range(8):
                        hi(g0 + i + 1, c, 8, j0 + 2 * i - 1, 16)
                        for b in range(2) if i < 4 else ():
                            m, j = 2 * i + b, j0 + 2 * i + b
                            ready(act, j, 16 * c)
                            act.wait_ge(hid_done, n0 + m + 1 + 8 * c)
                            free(act.activation(f_t[:, m % 2, :], bank(j), ACT.Relu), j)
                            evacuated(act, j, 2 * c)
                            act.activation(mh[:, m, :], f_t[:, m % 2, :], ACT.Square).then_inc(hid_hi, 1)
            for l in range(2):
                norm_squares(4 + 2 * l)
                norm_root(4 + 2 * l)
                norm_hi(4 + 2 * l, (l, 0))

                def own_part(name, s, b, c, dst, rows=P):
                    j = J[name, l, s, b]
                    ready(act, j)
                    act.activation(dst, bank(j)[0:rows, :], ACT.Copy, scale=omm[0:rows, c:c + 1])\
                       .then_inc(S("shift_own"), 1)

                c0 = SHIFT_TILES * l
                for i, (name, dst) in enumerate((("r2", R2), ("k2", K2), ("v2", A2 if l else V2))):
                    for s in range(2):
                        hi(plan.slab[name, l, s] + 1)
                        for b in range(2):
                            own_part(name, s, b, c0 + 4 * i + 2 * s + b, dst[:, 2 * s + b, :])
                hi(plan.slab["lat", l, 0] + 1)
                own_part("lat", 0, 0, c0 + 12, LA)
                own_part("lat", 0, 1, c0 + 13, GL[:, 0, :])
                hi(plan.slab["gl1", l, 0] + 1)
                own_part("gl1", 0, 0, c0 + 14, GL[0:32, 1, :], 32)
                if l:
                    hi(plan.slab["vl", l, 0] + 1)
                    own_part("vl", 0, 0, 2 * SHIFT_TILES, VL[0:32, :], 32)
                evacuated(act, J["gl1", l, 0, 0])
                act.activation(LA[0:HD, :], LA[0:HD, :], ACT.Tanh).then_inc(S("decay_latent"), 1)
                act.activation(GL[:, 0, :], GL[:, 0, :], ACT.Sigmoid).then_inc(S("gate_latent"), 1)
                act.activation(GL[0:32, 1, :], GL[0:32, 1, :], ACT.Sigmoid).then_inc(S("gate_latent"), 1)
                for name, dst, b0 in (("lw", SG, "w0_2"), ("la", X2, "a0_2")) + ((("lv", X1, "v0_2"),) if l else ()):
                    for t in range(4):
                        j = J[name, l, t]
                        ready(act, j)
                        b = V(b0, t if name == "lv" else 4 * l + t)
                        free(act.activation(dst[:, t, :], bank(j), ACT.Sigmoid, bias=b), j)
                act.wait_ge(S("kk_raw"), 4 * l + 4)
                act.activation(BON, KK, ACT.Square).then_inc(S("kk_sq"), 1)
                for t in range(4):
                    j = J["kn", l, t]
                    ready(act, j)
                    free(act.activation(BON[:, t, :], bank(j), ACT.Sqrt), j)
                act.wait_ge(S("cum_decay"), l + 1)
                act.activation(X1, C2, ACT.Exp, scale=-KAPPA).then_inc(S("decays"), 1)
                act.activation(SG, SG, ACT.Exp, scale=-KAPPA).then_inc(S("decays"), 1)
                act.wait_ge(S("decays"), 3 * l + 2)
                act.activation(C2, C2, ACT.Exp, scale=KAPPA).then_inc(S("decays"), 1)
                for m in range(NT):
                    for x, dst in ((0, KA[:, 0, :]), (1, BT)):
                        j = J["tok", l, m, x]
                        ready(act, j)
                        free(act.activation(dst, bank(j), ACT.Copy), j)
                    j = J["AkkV", l, m]
                    ready(act, j)
                    free(act.activation(KA[:, 1, :], bank(j), ACT.Copy), j)
                    for i in range(2):
                        j = J["WU", l, m, i]
                        ready(act, j)
                        p = bank(j).rearrange("p (j n) -> p j n", j=4)
                        act.activation(WU[:, 4 * i:4 * i + 4, 0:HD], p[:, :, 0:HD], ACT.Copy)
                        free(act.activation(WU[:, 4 * i:4 * i + 4, HD:P], p[:, :, HD:P], ACT.Copy, scale=-1.0), j)
                    j = J["WT", l, m]
                    ready(act, j)
                    free(act.activation(WT, bank(j).rearrange("p (j n) -> p j n", j=4), ACT.Copy), j)
                    for i in range(2):
                        j = J["Y", l, m, i]
                        ready(act, j)
                        a = HD * i
                        free(act.activation(R2[a:a + HD, :, m * P:(m + 1) * P],
                                            bank(j)[a:a + HD, :].rearrange("p (j n) -> p j n", j=4), ACT.Copy), j)
                for t in range(4):
                    evacuated(act, J["gmean", l, t])
                    act.activation(K2[:, t, :], R2[:, t, :], ACT.Square).then_inc(S("gn_sq"), 1)
                for t in range(4):
                    j = J["gvar", l, t]
                    ready(act, j)
                    free(act.activation(A2[:, t, :], bank(j), ACT.Sqrt, bias=epst[:, 1:2]), j)
                for t in range(4):
                    evacuated(act, J["g", l, t])
                    act.activation(mh[:, t, :], R2[:, t, :], ACT.Copy).then_inc(S("ya_hi"), 1)
                evac("z", l, lambda t: K2[:, t, :])
                for t in range(4):
                    j = J["pool", l, t]
                    ready(act, j)
                    act.activation(mh[:, 4 + t, :], bank(j), ACT.Copy, scale=V("pool_scale_2", 4 * l + t))\
                       .then_inc(S("yb_hi"), 1)
                for p in range(4):
                    for i, name in enumerate(("g0", "g1")):
                        hi(plan.slab[name, (l, p), 0] + 1)
                        for b in range(2):
                            j = J[name, (l, p), 0, b]
                            ready(act, j)
                            if p >= 1:
                                evacuated(act, J["pb", (l, p - 1), 0, 1])
                            free(act.activation(KK[:, 2 * i + b, :], bank(j), ACT.Sigmoid), j)
                    for name in ("pa", "pb"):
                        hi(plan.slab[name, (l, p), 0] + 1)
                ready(act, J["g1", (l, 3), 0, 1])
                for t in range(KT):
                    act.wait_ge(S("mixed"), 8 * l + t + 1)
                    act.activation(hh[:, t, :], mixed[t], ACT.Copy).then_inc(S("mixed_hi"), 1)
                for s in range(4):
                    hi(plan.slab["wo2", l, s] + 1)
                norm_squares(5 + 2 * l)
                norm_root(5 + 2 * l)
                norm_hi(5 + 2 * l, (l, 24))

                def gated(i, g0, j0, n0, c):
                    hi(g0 + 2 * i + 1, c, 12, j0 + 4 * i - 1, 24)
                    for b in range(2):
                        m, j = 2 * i + b, j0 + 4 * i + b
                        ready(act, j, 24 * c)
                        act.wait_ge(hid_done, n0 + m + 1 + 8 * c)
                        free(act.activation(f_t[:, m % 2, :], bank(j), ACT.Silu), j)
                    hi(g0 + 2 * i + 2, c, 12, j0 + 4 * i + 1, 24)
                    for b in range(2):
                        m, j = 2 * i + b, j0 + 4 * i + 2 + b
                        evacuated(act, j, 3 * c)
                        act.activation(mh[:, m, :], f_v[:, m % 2, :], ACT.Copy).then_inc(hid_hi, 1)

                g0, j0, n0 = plan.slab["fg", (l, 0, 0), 0], J["fg", (l, 0, 0), 0, 0], 64 + 22 * l
                for c in loop(act, 2):
                    for i in range(4):
                        gated(i, g0, j0, n0, c)
                    for i in range(4):
                        hi(g0 + 8 + i + 1, c, 12, j0 + 16 + 2 * i - 1, 24)
                g0, j0, n0 = g0 + 24, j0 + 48, n0 + 16
                for i in range(3):
                    gated(i, g0, j0, n0, 0)
                for i in range(4):
                    hi(g0 + 6 + i + 1)
            norm_squares(8)
            norm_root(8)
            for i in range(0, 8, 2):
                j = J["outT", i]
                ready(act, j)
                free(act.activation(o_tok[:, i // 2, 0:T], bank(j), ACT.Copy), j)

        @block.vector
        def _(dve):
            q = Seq(dve, S("dve_seq"))

            def free(ins, job):
                ins.then_inc(bank_read[job % BANKS], 1)

            def f32(x):
                return x.bitcast(F32)

            def lo(g, more=0):
                if g >= len(plan.last):
                    return
                dve.wait_ge(hi_done, g + 1 + more)
                dve.tensor_tensor(wlo[:, g % 2, :, :], raw[:, g % 2, :, :], f32(whi[:, g % 2, :, :]), ALU.subtract)\
                   .then_inc(raw_used, 1)

            def lows(name, layer, slabs):
                for s in range(slabs):
                    lo(plan.slab[name, layer, s] + 1)

            def norm(ni, gain, shift=None, between=None):
                for t in range(1, KT):
                    dve.wait_ge(S("norm_sq"), 8 * ni + t + 1)
                    if t == 1:
                        dve.tensor_tensor(n_acc, n_sq[:, 0, :], n_sq[:, 1, :], ALU.add).then_inc(S("norm_added"), 1)
                    else:
                        dve.wait_ge(S("norm_added"), 7 * ni + t - 1)
                        dve.tensor_tensor(n_acc, n_acc, n_sq[:, t % 3, :], ALU.add).then_inc(S("norm_added"), 1)
                if between:
                    between()
                evacuated(dve, J["ms", ni])
                q.mark(dve.reciprocal(n_rstd, n_rs))
                q.settle()
                for t in range(KT + 1):
                    if t < KT:
                        if 3 <= t and ni < 8:
                            dve.wait_ge(S("norm_lo"), 8 * ni + t - 2)
                        if ni < 8:
                            dst = n_val[:, t % 3, :]
                        else:
                            dst = o_val[:, t, :]
                        dve.scalar_tensor_tensor(dst, xT[:, t, :], gain(t), n_rstd, ALU.mult, ALU.mult)\
                           .then_inc(S("norm_val"), 1)
                    if t >= 1 and ni < 8:
                        s = t - 1
                        dve.wait_ge(S("norm_hi"), 8 * ni + s + 1)
                        if shift:
                            b = mod[:, shift[0], shift[1] + s:shift[1] + s + 1]
                            dve.scalar_tensor_tensor(hl[:, s, :], n_val[:, s % 3, :], b, f32(hh[:, s, :]),
                                                     ALU.add, ALU.subtract).then_inc(S("norm_lo"), 1)
                        else:
                            dve.tensor_tensor(hl[:, s, :], n_val[:, s % 3, :], f32(hh[:, s, :]), ALU.subtract)\
                               .then_inc(S("norm_lo"), 1)

            def head_norm(l, tiles):
                for i, (x, gain, r, n) in enumerate(tiles):
                    evacuated(dve, J["hn", l, i])
                    rs = h_rs[0:r, i % 2, 0:n]
                    q.mark(dve.reciprocal(rs, rs))
                    q.settle()
                    dve.scalar_tensor_tensor(x, x, gain, rs, ALU.mult, ALU.mult).then_inc(S("head_done"), 1)

            def softplus_tail(x, e, s, u, p, dst, scale):
                q.mark(dve.tensor_scalar(u, e, 2.0, None, ALU.add))
                q.settle()
                q.mark(dve.reciprocal(u, u))
                q.settle()
                q.mark(dve.tensor_tensor(s, e, u, ALU.mult))
                q.settle()
                q.mark(dve.tensor_tensor(u, s, s, ALU.mult))
                q.settle()
                q.mark(dve.tensor_scalar(p, u, 1.0 / 19, None, ALU.mult))
                for k in range(17, 1, -2):
                    q.settle()
                    q.mark(dve.scalar_tensor_tensor(p, p, 1.0 / k, u, ALU.add, ALU.mult))
                q.settle()
                q.mark(dve.scalar_tensor_tensor(p, p, 1.0, s, ALU.add, ALU.mult))
                q.mark(dve.tensor_scalar(u, x, 0.0, scale, ALU.max, ALU.mult))
                q.settle()
                ins = dve.scalar_tensor_tensor(dst, p, 2.0 * scale, u, ALU.mult, ALU.add)
                q.mark(ins)
                q.settle()

            def attention(name, l, units, base, width, scale, probs, o):
                for i in range(units + 2):
                    if i < units:
                        j = J[name + "_s", l, i]
                        parts, n = width(i)
                        c = 2 * (i % 2)
                        ready(dve, j)
                        src = bank(j)[:, 0:parts * n].rearrange("p (a n) -> p a n", a=parts)
                        ins = dve.tensor_reduce(stat[:, 0, c:c + parts], src, AX.X, ALU.max, negate=True)
                        if scale != 1.0:
                            q.mark(ins)
                            q.settle()
                            ins = dve.tensor_scalar(stat[:, 0, c:c + parts], stat[:, 0, c:c + parts], scale, None, ALU.mult)
                        ins.then_inc(S("att_max"), 1)
                    if 1 <= i <= units:
                        parts, n = width(i - 1)
                        c = 2 * ((i - 1) % 2)
                        evacuated(dve, J[name + "_s", l, i - 1])
                        q.mark(dve.reciprocal(stat[:, 2, c:c + parts], stat[:, 1, c:c + parts]))
                        q.settle()
                        for s in range(parts):
                            x = a_p[:, (i - 1) % 2, s * n:(s + 1) * n]
                            ins = dve.tensor_scalar(x, x, stat[:, 2, c + s:c + s + 1], None, ALU.mult)
                        ins.then_inc(S("att_probs"), 1)
                    if i >= 2:
                        j = J[name + "_o", l, i - 2]
                        dve.wait_ge(S("att_hi"), base + i - 1)
                        low, high, src = o(i - 2, bank(j))
                        free(dve.tensor_tensor(low, src, f32(high), ALU.subtract), j)

            def add_x(j, t, gate=None):
                if gate is None:
                    free(dve.tensor_tensor(xT[:, t, :], xT[:, t, :], bank(j), ALU.add), j)
                else:
                    free(dve.scalar_tensor_tensor(xT[:, t, :], bank(j), gate, xT[:, t, :], ALU.mult, ALU.add), j)

            dve.wait_ge(s_const, 2)
            for i in range(3):
                j = J["vec", i]
                ready(dve, j)
                free(dve.tensor_copy(vec[:, i * P:(i + 1) * P], bank(j)[:, 0:P]), j)
                evacuated(dve, j)
            c = VEC["mu_shift_2"][0]
            dve.tensor_scalar(omm[:, :], vec[:, c:c + 31], -1.0, 1.0, ALU.mult, ALU.add)
            c = VEC["fox_q_gain"][0]
            q.mark(dve.tensor_scalar(gq8[:, 0:1], vec[:, c:c + 1], float(HD) ** -0.5, None, ALU.mult))
            c = VEC["lru_lambda"][0]
            q.mark(dve.tensor_scalar(tiny[:, 4, 0:4], vec[:, c:c + 4], -1.0, None, ALU.mult))
            q.settle()
            dve.tensor_tensor(tiny[:, 2, 0:4], tiny[:, 4, 0:4], vec[:, c:c + 4], ALU.max).then_inc(S("lam_abs"), 1)
            dve.wait_ge(S("mem_root"), 1)
            q.mark(dve.reciprocal(tiny[:, 1, 2:4], tiny[:, 1, 0:2]))
            q.settle()
            for t in range(MT_):
                dve.tensor_scalar(mem_tok[:, t, :], mem_tok[:, t, :], tiny[:, 1, 2 + t:3 + t], None, ALU.mult)\
                   .then_inc(S("mem_normed"), 1)
            dve.wait_ge(S("lam_exp"), 1)
            softplus_tail(tiny[:, 4, 0:4], tiny[:, 3, 0:4], tiny[:, 5, 0:4], tiny[:, 6, 0:4], tiny[:, 7, 0:4], nsp[:, :], -8.0)
            lo(0)
            for l in range(2):
                def mem_lo():
                    for t in range(KT):
                        dve.wait_ge(S("mem_hi"), 8 * l + t + 1)
                        dve.scalar_tensor_tensor(ml[:, t, 0:MEM], memT[:, t, :], V("norm_mem", 8 * l + t),
                                                 f32(mh[:, t, 0:MEM]), ALU.mult, ALU.subtract).then_inc(S("mem_lo"), 1)
                norm(2 * l, lambda t: V("norm_mix", 8 * l + t), between=mem_lo)
                lows("memk", l, 2)
                lows("memv", l, 2)
                if l == 0:
                    q.mark(dve.memset(U[:, :, 0:3], 0.0))
                    for name in ("u", "gate", "xq"):
                        lows(name, l, 2)
                    head_norm(l, [(mK[:, t, :], V("xa_k_gain", l), P, MEM) for t in range(4)]
                              + [(XQ[:, t, :], V("xa_q_gain", l), P, T) for t in range(4)])
                    q.settle()
                    for t in range(4):
                        evacuated(dve, J["u", l, t // 2, t % 2])
                        q.mark(dve.tensor_scalar(UC[:, t, :], U[:, t, 0:T], V("conv_w", t), V("conv_b", t), ALU.mult, ALU.add))
                    for j in range(1, 4):
                        q.settle()
                        for t in range(4):
                            ins = dve.scalar_tensor_tensor(UC[:, t, :], U[:, t, j:j + T], V("conv_w", 4 * j + t),
                                                           UC[:, t, :], ALU.mult, ALU.add)
                            if j < 3:
                                q.mark(ins)
                            else:
                                ins.then_inc(S("conv"), 1)
                    for t in range(4):
                        evacuated(dve, J["rgate", t])
                        dve.tensor_scalar(RB[:, t, :], RB[:, t, :], nsp[:, t:t + 1], None, ALU.mult).then_inc(S("lru_loga"), 1)
                    dve.wait_ge(S("lru_tanh"), 1)
                    for t in range(4):
                        q.mark(dve.tensor_scalar(DB[:, t, :], U[:, t, 0:T], 1.0, None, ALU.add))
                    q.settle()
                    q.mark(dve.reciprocal(DB, DB))
                    q.settle()
                    for t in range(4):
                        dve.scalar_tensor_tensor(U[:, t, 0:T], U[:, t, 0:T], 2.0, DB[:, t, :], ALU.mult, ALU.mult)\
                           .then_inc(S("lru_1ma2"), 1)
                    evacuated(dve, J["igate", 3])
                    q.mark(dve.tensor_tensor(IB, IB, UC, ALU.mult))
                    q.settle()
                    dve.wait_ge(S("lru_root"), 1)
                    q.mark(dve.tensor_tensor(IB, IB, U[:, :, 0:T], ALU.mult))
                    q.settle()
                    for t in range(4):
                        q.mark(dve.tensor_tensor_scan(UC[:, t, :], RB[:, t, :], IB[:, t, :], 0.0, ALU.mult, ALU.add))
                    q.settle()
                    dve.tensor_tensor(UC, UC, G, ALU.mult).then_inc(S("lru_y"), 1)
                    dve.wait_ge(S("lru_hi"), 1)
                    dve.tensor_tensor(ml[:, 0:4, :], UC, f32(mh[:, 0:4, :]), ALU.subtract).then_inc(S("lru_lo"), 1)
                else:
                    ready(dve, J["mod", 0])
                    for x in (qaug, kaug):
                        dve.memset(x[HD:HD + 2, :, :], 1.0).then_inc(S("decay_rows_one"), 1)
                    for name in ("q", "k", "v"):
                        lows(name, l, 2)
                    lows("f", l, 1)
                    lows("xq", l, 1)
                    j = J["f", l, 0, 0]
                    ready(dve, j)
                    ready(dve, J["xq", l, 1, 1])
                    lo(plan.slab["xq", l, 1] + 1)
                    dve.tensor_scalar(fbuf[0:FOX_H, 0, :], bank(j)[0:FOX_H, :], V("b_forget", 0, FOX_H), -1.0,
                                      ALU.add, ALU.mult).then_inc(S("forget_x"), 1)
                    dve.wait_ge(S("forget_x"), 1)
                    free(dve.memset(fbuf[0:FOX_H, 3, :], 1.0), j)
                    dve.wait_ge(S("forget_exp"), 1)
                    f = [fbuf[0:FOX_H, i, :] for i in range(4)]
                    softplus_tail(f[0], f[1], f[2], a_p[0:FOX_H, 0, :], a_p[0:FOX_H, 1, :], f[1], 1.0)
                    dve.tensor_tensor_scan(f[0], f[3], f[1], 0.0, ALU.mult, ALU.subtract).then_inc(S("decay_rows"), 1)
                    dve.wait_ge(S("decay_rows"), 1)
                    dve.tensor_scalar(f[1], f[0], -1.0, None, ALU.mult).then_inc(S("decay_rows"), 1)
                    head_norm(l, [(qaug[0:HD, h, :], gq8[0:HD, 0:1], HD, T) for h in range(FOX_H)]
                              + [(kaug[0:HD, h, :], V("fox_k_gain", 0, HD), HD, T) for h in range(FOX_H)]
                              + [(mK[:, t, :], V("xa_k_gain", l), P, MEM) for t in range(4)]
                              + [(XQ[:, t, :], V("xa_q_gain", l), P, T) for t in range(4)])

                    def fox_o(i, p):
                        h, t = i // NT, i % NT
                        a = HD * (h % 2)
                        at = (slice(a, a + HD), h // 2, slice(t * P, (t + 1) * P))
                        return ml[at], mh[at], p[a:a + HD, 0:P]
                    attention("fox", l, 4 * FOX_H, 8, lambda i: (1, P * (i % NT + 1)), 1.0, None, fox_o)

                def xa_o(i, p):
                    at = (slice(0, P), 4 + i // 2, slice((i % 2) * MEM, (i % 2 + 1) * MEM))
                    return ml[at], mh[at], p[:, 0:MEM]
                attention("xa", l, 2 * XA_H, 40 * l, lambda i: (2, MEM), float(P) ** -0.5, None, xa_o)
                for s in range(4):
                    lo(plan.slab["wo", l, s] + 1)
                    for b in range(2):
                        j = J["wo", l, s, b]
                        ready(dve, j)
                        add_x(j, 2 * s + b)
                norm(2 * l + 1, lambda t: V("norm_mlp", 8 * l + t))
                if l == 0:
                    dve.wait_ge(S("c_act"), 1)
                g0, j0, n0, a0 = plan.slab["up", (l, 0), 0], J["up", (l, 0), 0, 0], 32 * l, 256 * l + 16
                for c in loop(dve, CHUNKS1):
                    for i in range(8):
                        lo(g0 + i + 1, 8 * c)
                        dve.wait_ge(ada_landed[i % 2], 16 * (16 * l + i // 2 + 1) + 64 * c)
                        acc = ada_acc[:, bass.ds(c * (8 * ADA_COLS) + i * ADA_COLS, ADA_COLS)]
                        for k in range(KT):
                            w = ada[:, i % 2, k, :]
                            if k == 0:
                                ins = dve.tensor_scalar(acc, w, cact[:, 0:1], None, ALU.mult)
                            else:
                                dve.wait_ge(ada_done, a0 + 8 * i + k + 64 * c)
                                ins = dve.scalar_tensor_tensor(acc, w, cact[:, k:k + 1], acc, ALU.mult, ALU.add)
                            ins.then_inc(ada_done, 1)
                        for b in range(2):
                            m, j = 2 * i + b, j0 + 2 * i + b
                            if i < 4:
                                evacuated(dve, j, 2 * c)
                                dve.wait_ge(hid_done, n0 + m + 1 + 8 * c)
                                dve.tensor_tensor(f_v[:, m % 2, :], f_t[:, m % 2, :], f_t[:, m % 2, :], ALU.mult)\
                                   .then_inc(S("hidden_sq"), 1)
                                dve.wait_ge(S("hidden_sq"), n0 + m + 1 + 8 * c)
                                dve.wait_ge(hid_hi, n0 + m + 1 + 8 * c)
                                dve.tensor_tensor(ml[:, m, :], f_v[:, m % 2, :], f32(mh[:, m, :]), ALU.subtract)\
                                   .then_inc(hid_done, 1)
                            else:
                                ready(dve, j, 16 * c)
                                add_x(j, m - 8)
                j = J["mod", l]
                ready(dve, j)
                c = VEC["ada_b_2"][0] + 48 * l
                free(dve.tensor_tensor(mod[:, l, :], bank(j)[:, 0:48], vec[:, c:c + 48], ALU.add), j)
                evacuated(dve, j)
                for i, name in enumerate(("norm1_g_2", "norm2_g_2")):
                    c = VEC[name][0] + 8 * l
                    q.mark(dve.scalar_tensor_tensor(gmod[:, 2 * l + i, :], mod[:, l, 8 + 24 * i:16 + 24 * i], 1.0,
                                                    vec[:, c:c + 8], ALU.add, ALU.mult))
            q.settle()
            for l in range(2):
                norm(4 + 2 * l, lambda t: gmod[:, 2 * l, t:t + 1], (l, 0))

                shifted = [0]

                def before_part(name, s, b, mu, dst, rows=P):
                    j = J[name, l, s, b]
                    shifted[0] += 1
                    dve.wait_ge(S("shift_own"), SHIFT_TILES * l + shifted[0])
                    free(dve.scalar_tensor_tensor(dst[:, 1:T], bank(j)[0:rows, 0:T - 1], mu, dst[:, 1:T], ALU.mult, ALU.add), j)

                m0 = SHIFT_TILES * l
                for i, (name, dst) in enumerate((("r2", R2), ("k2", K2), ("v2", A2 if l else V2))):
                    for s in range(2):
                        lo(plan.slab[name, l, s] + 1)
                        for b in range(2):
                            t = 4 * i + 2 * s + b
                            before_part(name, s, b, V("mu_shift_2", m0 + t), dst[:, 2 * s + b, :])
                lo(plan.slab["lat", l, 0] + 1)
                before_part("lat", 0, 0, V("mu_shift_2", m0 + 12), LA)
                before_part("lat", 0, 1, V("mu_shift_2", m0 + 13), GL[:, 0, :])
                lo(plan.slab["gl1", l, 0] + 1)
                before_part("gl1", 0, 0, V("mu_shift_2", m0 + 14, 32), GL[0:32, 1, :], 32)
                if l:
                    lo(plan.slab["vl", l, 0] + 1)
                    before_part("vl", 0, 0, V("mu_v_2", 0, 32), VL[0:32, :], 32)
                evacuated(dve, J["k2", l, 1, 1])
                for t in range(4):
                    dve.tensor_scalar(KK[:, t, :], K2[:, t, :], V("k_k_2", 4 * l + t), None, ALU.mult).then_inc(S("kk_raw"), 1)
                for t in range(4):
                    evacuated(dve, J["lw", l, t])
                    q.mark(dve.tensor_tensor_scan(C2[:, t, :], keep[:, :], SG[:, t, :], 0.0, ALU.mult, ALU.add))
                if l:
                    q.mark(dve.tensor_tensor(V2, V2, A2, ALU.subtract))
                    evacuated(dve, J["lv", l, 3])
                    q.settle()
                    q.mark(dve.tensor_tensor(V2, V2, X1, ALU.mult))
                    q.settle()
                    q.mark(dve.tensor_tensor(V2, V2, A2, ALU.add))
                q.settle()
                dve.tensor_tensor(SG, C2, SG, ALU.subtract).then_inc(S("cum_decay"), 1)
                for t in range(4):
                    evacuated(dve, J["kn", l, t])
                    q.mark(dve.tensor_scalar(BON[:, t, :], BON[:, t, :], 1e-12, None, ALU.max))
                q.settle()
                q.mark(dve.reciprocal(BON, BON))
                q.settle()
                q.mark(dve.tensor_tensor(KK, KK, BON, ALU.mult))
                q.settle()
                evacuated(dve, J["la", l, 3])
                for t in range(4):
                    q.mark(dve.tensor_scalar(BON[:, t, :], X2[:, t, :], 1.0, V("k_a_2", 4 * l + t), ALU.subtract, ALU.mult))
                q.settle()
                q.mark(dve.scalar_tensor_tensor(K2, BON, 1.0, K2, ALU.add, ALU.mult))
                q.mark(dve.tensor_tensor(A2, X2, KK, ALU.mult))
                q.settle()
                for t in range(4):
                    dve.scalar_tensor_tensor(BON[:, t, :], R2[:, t, :], V("r_k_2", 4 * l + t), K2[:, t, :], ALU.mult, ALU.mult)\
                       .then_inc(S("bonus_in"), 1)
                dve.wait_ge(S("decays"), 3 * l + 3)
                dve.tensor_tensor(KK, KK, SG, ALU.mult).then_inc(S("features"), 1)
                dve.tensor_tensor(A2, A2, C2, ALU.mult).then_inc(S("features"), 1)
                dve.wait_ge(S("bonus_in"), 4 * l + 4)
                dve.tensor_tensor(K2, K2, C2, ALU.mult).then_inc(S("features"), 1)
                q.mark(dve.tensor_copy(PC[:, :, :], X1[:, :, CH - 1:T:CH]))
                q.mark(dve.memset(ST[:, 0, :, :], 0.0))
                q.settle()
                dve.tensor_tensor(R2, R2, X1, ALU.mult).then_inc(S("features"), 1)
                for t in range(4):
                    j = J["bon", l, t]
                    ready(dve, j)
                    free(dve.tensor_tensor(BON[:, t, :], bank(j), V2[:, t, :], ALU.mult), j)
                for m in range(NT):
                    def p4(j):
                        return bank(j).rearrange("p (j n) -> p j n", j=4)

                    for x, dst in ((2, KhT), (3, VT)):
                        j = J["tok", l, m, x]
                        ready(dve, j)
                        free(dve.tensor_copy(dst, bank(j)), j)
                    for name, dst in (("LT", LT), ("Akk", AK)):
                        for i in range(2):
                            j = J[name, l, m, i]
                            ready(dve, j)
                            free(dve.tensor_tensor(dst[:, i, :, :], p4(j), bc(strict[:, :]), ALU.mult), j)
                    for i in range(2):
                        j = J["L1", l, m, i]
                        ready(dve, j)
                        free(dve.tensor_tensor(T1[:, i, :, :], p4(j), bc(lvl[:, 0, :]), ALU.mult), j)
                        q.mark(dve.tensor_tensor(MT[:, i, :, :], LT[:, i, :, :], bc(pairup[:, :]), ALU.mult))
                    for i in range(2):
                        evacuated(dve, J["L1", l, m, i])
                    q.settle()
                    for i in range(2):
                        dve.tensor_tensor(MM[:, i, :, :], bc(ident[:, :]), T1[:, i, :, :], ALU.subtract).then_inc(S("inv_start"), 1)
                        dve.tensor_tensor(MT[:, i, :, :], bc(ident[:, :]), MT[:, i, :, :], ALU.subtract).then_inc(S("inv_start"), 1)
                    dve.wait_ge(S("inv_start"), 4 * (NT * l + m) + 4)
                    for n, b in enumerate(LEVELS):
                        for i in range(2):
                            j = J["LM", l, m, b, i]
                            ready(dve, j)
                            free(dve.tensor_tensor(T1[:, i, :, :], p4(j), bc(lvl[:, 1 + n, :]), ALU.mult), j)
                        for i in range(2):
                            for name, dst in (("MLM", MM), ("MLMt", MT)):
                                if (name, l, m, b, i) in J:
                                    j = J[name, l, m, b, i]
                                    ready(dve, j)
                                    free(dve.tensor_tensor(dst[:, i, :, :], dst[:, i, :, :], p4(j), ALU.subtract), j)
                    for name, dst in (("Ark", AR), ("Arb", AB)):
                        for i in range(2):
                            j = J[name, l, m, i]
                            ready(dve, j)
                            free(dve.tensor_tensor(dst[:, i, :, :], p4(j), bc(incl[:, :]), ALU.mult), j)
                    for c in range(2):
                        j = J["NH", l, m, c]
                        ready(dve, j)
                        p = bank(j).rearrange("p (x j n) -> p x j n", x=2, j=4)
                        eye = ident2[:, :].rearrange("p (a n) -> p a n", a=1).to_broadcast([P, 4, HD])
                        dve.tensor_tensor(GS[:, c, :, :], eye, p[:, 0, :, :], ALU.subtract)
                        free(dve.tensor_copy(HS[:, c, :, :], p[:, 1, :, :]), j)
                    for c in range(2):
                        cc = 2 * m + c
                        evacuated(dve, J["NH", l, m, c])
                        for i in range(2):
                            j = J["S", l, m, c, i]
                            a = slice(HD * i, HD * i + HD)
                            ready(dve, j)
                            new = ST[a, (cc + 1) % 3, :, :]
                            free(dve.tensor_tensor(new, bank(j)[a, 0:4 * HD].rearrange("p (j n) -> p j n", j=4),
                                                   HS[a, c, :, :], ALU.add), j)
                            evacuated(dve, j)
                            pc = PC[a, :, cc:cc + 1].to_broadcast([HD, 4, HD])
                            dve.tensor_tensor(new, new, pc, ALU.mult).then_inc(S("state"), 1)
                    for i in range(2):
                        j = J["U", l, m, i]
                        ready(dve, j)
                        free(dve.tensor_tensor(NU[:, 4 * i:4 * i + 4, :], WU[:, 4 * i:4 * i + 4, HD:P],
                                               bank(j)[:, 0:4 * HD].rearrange("p (j n) -> p j n", j=4), ALU.subtract), j)
                for t in range(4):
                    j = J["gmean", l, t]
                    ready(dve, j)
                    free(dve.tensor_tensor(R2[:, t, :], R2[:, t, :], bank(j), ALU.subtract), j)
                for t in range(4):
                    evacuated(dve, J["gvar", l, t])
                    q.mark(dve.reciprocal(A2[:, t, :], A2[:, t, :]))
                    q.settle()
                    q.mark(dve.scalar_tensor_tensor(R2[:, t, :], R2[:, t, :], V("lnx_g_2", 4 * l + t), A2[:, t, :], ALU.mult, ALU.mult))
                    q.settle()
                    q.mark(dve.scalar_tensor_tensor(R2[:, t, :], R2[:, t, :], V("lnx_b_2", 4 * l + t), BON[:, t, :], ALU.add, ALU.add))
                    q.settle()
                    j = J["g", l, t]
                    ready(dve, j)
                    free(dve.tensor_tensor(R2[:, t, :], R2[:, t, :], bank(j), ALU.mult), j)
                for t in range(4):
                    dve.wait_ge(S("ya_hi"), 4 * l + t + 1)
                    dve.tensor_tensor(ml[:, t, :], R2[:, t, :], f32(mh[:, t, :]), ALU.subtract).then_inc(S("ya_lo"), 1)
                lows("z", l, 2)
                for t, w in enumerate(WINDOWS):
                    evacuated(dve, J["z", l, t // 2, t % 2])
                    cur, step, n = K2[:, t, :], 1, 0
                    while step < w:
                        nxt = (A2, KK)[n % 2][:, t, :]
                        q.mark(dve.tensor_tensor(nxt[:, step:T], cur[:, step:T], cur[:, 0:T - step], ALU.add))
                        q.mark(dve.tensor_copy(nxt[:, 0:step], cur[:, 0:step]))
                        q.settle()
                        cur, step, n = nxt, 2 * step, n + 1
                    z = K2[:, t, :]
                    q.mark(dve.tensor_tensor(cur[:, 0:16], cur[:, 0:16], invc[:, t, :], ALU.mult))
                    dve.scalar_tensor_tensor(z[:, 16:T], cur[:, 16:T], 1.0 / w, z[:, 16:T], ALU.mult, ALU.subtract)
                    q.settle()
                    dve.tensor_tensor(z[:, 0:16], cur[:, 0:16], z[:, 0:16], ALU.subtract).then_inc(S("pooled"), 1)
                for t in range(4):
                    j = J["pool", l, t]
                    dve.wait_ge(S("yb_hi"), 4 * l + t + 1)
                    free(dve.scalar_tensor_tensor(ml[:, 4 + t, :], bank(j), V("pool_scale_2", 4 * l + t),
                                                  f32(mh[:, 4 + t, :]), ALU.mult, ALU.subtract), j)
                for p in range(4):
                    for name in ("g0", "g1"):
                        lo(plan.slab[name, (l, p), 0] + 1)
                    for i, name in enumerate(("pa", "pb")):
                        lo(plan.slab[name, (l, p), 0] + 1)
                        for b in range(2):
                            evacuated(dve, J[("g0", "g1")[i], (l, p), 0, b])
                            j = J[name, (l, p), 0, b]
                            ready(dve, j)
                            free(dve.tensor_tensor(BON[:, 2 * i + b, :], KK[:, 2 * i + b, :], bank(j), ALU.mult), j)
                    for b in range(2):
                        evacuated(dve, J["pa", (l, p), 0, b])
                        evacuated(dve, J["pb", (l, p), 0, b])
                        dve.tensor_tensor(mixed[2 * p + b], BON[:, b, :], BON[:, 2 + b, :], ALU.add).then_inc(S("mixed"), 1)
                for t in range(KT):
                    dve.wait_ge(S("mixed_hi"), 8 * l + t + 1)
                    dve.tensor_tensor(hl[:, t, :], mixed[t], f32(hh[:, t, :]), ALU.subtract).then_inc(S("mixed_lo"), 1)
                for s in range(4):
                    lo(plan.slab["wo2", l, s] + 1)
                    for b in range(2):
                        j, t = J["wo2", l, s, b], 2 * s + b
                        ready(dve, j)
                        add_x(j, t, mod[:, l, 16 + t:17 + t])
                norm(5 + 2 * l, lambda t: gmod[:, 2 * l + 1, t:t + 1], (l, 24))

                def gated(i, g0, j0, n0, c):
                    lo(g0 + 2 * i + 1, 12 * c)
                    lo(g0 + 2 * i + 2, 12 * c)
                    for b in range(2):
                        m, j = 2 * i + b, j0 + 4 * i + 2 + b
                        evacuated(dve, j - 2, 3 * c)
                        ready(dve, j, 24 * c)
                        dve.wait_ge(hid_done, n0 + m + 1 + 8 * c)
                        free(dve.tensor_tensor(f_v[:, m % 2, :], f_t[:, m % 2, :], bank(j), ALU.mult), j)
                    for b in range(2):
                        m = 2 * i + b
                        dve.wait_ge(hid_hi, n0 + m + 1 + 8 * c)
                        dve.tensor_tensor(ml[:, m, :], f_v[:, m % 2, :], f32(mh[:, m, :]), ALU.subtract).then_inc(hid_done, 1)

                g0, j0, n0 = plan.slab["fg", (l, 0, 0), 0], J["fg", (l, 0, 0), 0, 0], 64 + 22 * l
                for c in loop(dve, 2):
                    for i in range(4):
                        gated(i, g0, j0, n0, c)
                    for i in range(4):
                        lo(g0 + 8 + i + 1, 12 * c)
                        for b in range(2):
                            j, t = j0 + 16 + 2 * i + b, 2 * i + b
                            ready(dve, j, 24 * c)
                            add_x(j, t, mod[:, l, 40 + t:41 + t])
                g0, j0, n0 = g0 + 24, j0 + 48, n0 + 16
                for i in range(3):
                    gated(i, g0, j0, n0, 0)
                for i in range(4):
                    lo(g0 + 6 + i + 1)
                    for b in range(2):
                        j, t = j0 + 12 + 2 * i + b, 2 * i + b
                        ready(dve, j)
                        add_x(j, t, mod[:, l, 40 + t:41 + t])
            norm(8, lambda t: V("final_g_2", t))
            for i in range(1, 8, 2):
                j = J["outT", i]
                ready(dve, j)
                free(dve.tensor_copy(o_tok[:, i // 2, T:D], bank(j)), j)

        @block.tensor
        def _(pe):
            todo = [0]

            def start(*key, c=0, jobs=0):
                j = J[key]
                assert j == todo[0], (key, j, todo)
                todo[0] += 1
                if j >= BANKS:
                    pe.wait_ge(bank_read[j % BANKS], j // BANKS + (jobs // BANKS) * c)
                return bank(j)

            def done(ins):
                ins.then_inc(written, 1)

            def three(out, whi_, wlo_, xhi, xlo, first, last):
                pe.matmul(out, whi_, xhi, start=first, stop=False)
                pe.matmul(out, whi_, xlo, start=False, stop=False)
                return pe.matmul(out, wlo_, xhi, start=False, stop=last)

            def linear(name, layer, s, operand, K=KT, blocks=2, n=T, before=None, c=0, slabs=0, jobs=0):
                g = plan.slab[name, layer, s]
                pe.wait_ge(raw_used, g + 1 + slabs * c)
                xh, xl = operand
                for b in range(blocks):
                    p = start(name, layer, s, b, c=c, jobs=jobs)
                    for k in range(K):
                        if before and b == 0:
                            before(k)
                        w = (slice(0, P), g % 2, k, slice(b * P, (b + 1) * P))
                        ins = three(p[:, 0:n], whi[w], wlo[w], xh[:, k, 0:n], xl[:, k, 0:n], k == 0, k == K - 1)
                    done(ins)

            def linear_tokens(name, layer, s, operand, tiles):
                g = plan.slab[name, layer, s]
                pe.wait_ge(raw_used, g + 1)
                xh, xl = operand
                for b in range(tiles):
                    p = start(name, layer, s, b)
                    for k in range(KT):
                        t = slice(b * P, (b + 1) * P)
                        wh, wl = whi[:, g % 2, k, :], wlo[:, g % 2, k, :]
                        pe.matmul(p[:, 0:SLAB], xh[:, k, t], wh, start=(k == 0), stop=False)
                        pe.matmul(p[:, 0:SLAB], xl[:, k, t], wh, start=False, stop=False)
                        ins = pe.matmul(p[:, 0:SLAB], xh[:, k, t], wl, start=False, stop=(k == KT - 1))
                    done(ins)

            def mean_square(ni):
                pe.wait_ge(S("norm_added"), 7 * ni + 7)
                p = start("ms", ni)
                done(pe.matmul(p, mean_all[:, :], n_acc, start=True, stop=True))

            def normed(ni):
                return lambda k: pe.wait_ge(S("norm_lo"), 8 * ni + k + 1)

            def head_norm(l, tiles):
                base = 0 if l == 0 else 8
                for i, (m, r, n) in enumerate(tiles):
                    pe.wait_ge(S("head_sq"), base + i + 1)
                    p = start("hn", l, i)
                    done(pe.matmul(p[0:r, 0:n], m[0:r, 0:r], h_sq[0:r, i % 2, 0:n], start=True, stop=True))

            def attention(name, l, units, base, scores, turn, values):
                for i in range(units + 2):
                    if i < units:
                        done(scores(i, start(name + "_s", l, i)))
                    if 1 <= i <= units:
                        pe.wait_ge(S("att_probs"), base + i)
                        done(turn(i - 1, start(name + "_t", l, i - 1)))
                    if i >= 2:
                        evacuated(pe, J[name + "_t", l, i - 2])
                        done(values(i - 2, start(name + "_o", l, i - 2)))

            pe.wait_ge(s_const, 2)
            pe.wait_ge(s_vec, 16 * 34)
            for i in range(3):
                p = start("vec", i)
                done(pe.transpose(p[:, 0:P], vrows[:, i, :], ident[:, :]))
            pe.wait_ge(s_x, 16)
            for t in range(KT):
                p = start("xT", t)
                for s in range(NT):
                    ins = pe.transpose(p[:, s * P:(s + 1) * P], x_tok[:, s, t * P:(t + 1) * P], ident[:, :])
                done(ins)
            pe.wait_ge(S("mem_normed"), MT_)
            for i in range(4):
                p = start("memT", i)
                for t in range(2):
                    for s in range(MT_):
                        a = (2 * t + s) * P
                        ins = pe.transpose(p[:, a:a + P], mem_tok[:, s, (2 * i + t) * P:(2 * i + t + 1) * P], ident[:, :])
                done(ins)
            h, y = (hh, hl), (mh, ml)
            for l in range(2):
                mean_square(2 * l)
                pe.wait_ge(S("mem_lo"), 8 * l + 8)
                for s in range(2):
                    linear("memk", l, s, y, n=MEM)
                for s in range(2):
                    linear_tokens("memv", l, s, y, MT_)
                if l == 0:
                    for name in ("u", "gate", "xq"):
                        for s in range(2):
                            linear(name, l, s, h, before=normed(0) if name == "u" and s == 0 else None)
                    head_norm(l, [(mean_128, P, MEM)] * 4 + [(mean_128, P, T)] * 4)
                    pe.wait_ge(S("conv"), 4)
                    pe.wait_ge(s_small, 256)
                    for t in range(4):
                        for name, w in (("rgate", WR), ("igate", WI)):
                            p = start(name, t)
                            done(pe.matmul(p, w[:, t, :], UC[:, t, :], start=True, stop=True))
                else:
                    for name in ("q", "k"):
                        for s in range(2):
                            linear(name, l, s, h, before=normed(2) if name == "q" and s == 0 else None)
                    for s in range(2):
                        linear_tokens("v", l, s, h, NT)
                    linear("f", l, 0, h, blocks=1)
                    for s in range(2):
                        linear("xq", l, s, h)
                    head_norm(l, [(mean_64, HD, T)] * 16 + [(mean_128, P, MEM)] * 4 + [(mean_128, P, T)] * 4)
                    pe.wait_ge(S("head_done"), 8 + 16)
                    pe.wait_ge(s_aug, 32)

                    def fox_scores(i, p):
                        hd, t = i // NT, i % NT
                        n = P * (t + 1)
                        a = HD + 2
                        pe.matmul(p[:, 0:n], qaug[0:a, hd, t * P:(t + 1) * P], kaug[0:a, hd, 0:n], start=True, stop=False)
                        return pe.matmul(p[:, t * P:n], ident[:, :], causal[:, :], start=False, stop=True)

                    def fox_turn(i, p):
                        for k in range(i % NT + 1):
                            ins = pe.transpose(p[:, k * P:(k + 1) * P], a_p[:, i % 2, k * P:(k + 1) * P], ident[:, :])
                        return ins

                    def fox_values(i, p):
                        hd, t = i // NT, i % NT
                        a = HD * (hd % 2)
                        for k in range(t + 1):
                            ins = pe.matmul(p[a:a + HD, 0:P], vtok[:, k, hd * HD:(hd + 1) * HD],
                                            a_t[:, i % 2, k * P:(k + 1) * P], start=(k == 0), stop=(k == t))
                        return ins
                    attention("fox", l, 4 * FOX_H, 8, fox_scores, fox_turn, fox_values)
                pe.wait_ge(S("head_done"), 8 if l == 0 else 32)

                def xa_scores(i, p):
                    for s in range(2):
                        t = 2 * (i % 2) + s
                        ins = pe.matmul(p[:, s * MEM:(s + 1) * MEM], XQ[:, i // 2, t * P:(t + 1) * P], mK[:, i // 2, :],
                                        start=True, stop=True)
                    return ins

                def xa_turn(i, p):
                    for k in range(MT_):
                        for s in range(2):
                            ins = pe.transpose(p[:, k * MEM + s * P:k * MEM + (s + 1) * P],
                                               a_p[:, i % 2, s * MEM + k * P:s * MEM + (k + 1) * P], ident[:, :])
                    return ins

                def xa_values(i, p):
                    for k in range(MT_):
                        ins = pe.matmul(p[:, 0:MEM], mV[:, k, (i // 2) * P:(i // 2 + 1) * P],
                                        a_t[:, i % 2, k * MEM:(k + 1) * MEM], start=(k == 0), stop=(k == MT_ - 1))
                    return ins
                attention("xa", l, 2 * XA_H, 40 * l, xa_scores, xa_turn, xa_values)

                def mixer_out(k):
                    if k >= 4:
                        evacuated(pe, J["xa_o", l, 2 * (k - 4) + 1])
                    elif l == 0:
                        pe.wait_ge(S("lru_lo"), 1)
                    else:
                        evacuated(pe, J["fox_o", l, 2 * NT * (k + 1) - 1])
                for s in range(4):
                    linear("wo", l, s, y, before=mixer_out if s == 0 else None)
                mean_square(2 * l + 1)
                g0, n0 = plan.slab["up", (l, 0), 0], 32 * l
                for c in loop(pe, CHUNKS1):
                    for s in range(4):
                        linear("up", (l, 0), s, h, before=normed(2 * l + 1) if s == 0 else None, c=c, slabs=8, jobs=16)
                    for s in range(4):
                        linear("down", (l, 0), s, y, c=c, slabs=8, jobs=16,
                               before=(lambda k: pe.wait_ge(hid_done, n0 + k + 3 + 8 * c)) if s == 0 else None)
                todo[0] += 16 * (CHUNKS1 - 1)
                p = start("mod", l)
                pe.wait_ge(ada_done, 256 * (l + 1) + 16)
                for n in range(48):
                    ins = pe.matmul(p[:, n:n + 1], ada_acc[:, n * P:(n + 1) * P], ones[:, 0:1], start=True, stop=True)
                done(ins)
            for l in range(2):
                mean_square(4 + 2 * l)
                for name in ("r2", "k2", "v2"):
                    for s in range(2):
                        linear(name, l, s, h, before=normed(4 + 2 * l) if name == "r2" and s == 0 else None)
                linear("lat", l, 0, h)
                linear("gl1", l, 0, h, blocks=1)
                if l:
                    linear("vl", l, 0, h, blocks=1)
                small = 80 * l + (32 if l == 0 else 48)
                pe.wait_ge(s_lora, small)
                pe.wait_ge(S("decay_latent"), l + 1)
                for t in range(4):
                    p = start("lw", l, t)
                    done(pe.matmul(p, WA[0:HD, t * P:(t + 1) * P], LA[0:HD, :], start=True, stop=True))
                for t in range(4):
                    p = start("la", l, t)
                    done(pe.matmul(p, WA[HD:P, t * P:(t + 1) * P], LA[HD:P, :], start=True, stop=True))
                if l:
                    evacuated(pe, J["vl", l, 0, 0])
                    for t in range(4):
                        p = start("lv", l, t)
                        done(pe.matmul(p, VU[0:32, t * P:(t + 1) * P], VL[0:32, :], start=True, stop=True))
                pe.wait_ge(S("kk_sq"), l + 1)
                for t in range(4):
                    p = start("kn", l, t)
                    done(pe.matmul(p, sum_64[:, :], BON[:, t, :], start=True, stop=True))
                for t in range(4):
                    pe.wait_ge(S("bonus_in"), 4 * l + t + 1)
                    p = start("bon", l, t)
                    done(pe.matmul(p, sum_64[:, :], BON[:, t, :], start=True, stop=True))
                pe.wait_ge(S("features"), 4 * l + 4)
                for m in range(NT):
                    ms = slice(m * P, (m + 1) * P)
                    for x, src in enumerate((KK, A2, K2, V2)):
                        p = start("tok", l, m, x)
                        for t in range(4):
                            ins = pe.transpose(p[:, t * P:(t + 1) * P], src[:, t, ms], ident[:, :])
                        done(ins)

                    def products(name, left, right):
                        for i in range(2):
                            a = slice(HD * i, HD * i + HD)
                            p = start(name, l, m, i)
                            for t in range(4):
                                ins = pe.matmul(p[:, t * P:(t + 1) * P], left[a, t, ms], right[a, t, ms], start=True, stop=True)
                            done(ins)

                    def each(name, left, right, *key):
                        p = start(name, l, m, *key)
                        for t in range(4):
                            ins = pe.matmul(p[:, t * P:(t + 1) * P], left(t), right(t), start=True, stop=True)
                        done(ins)

                    products("LT", A2, KK)
                    products("Akk", K2, KK)
                    for i in range(2):
                        evacuated(pe, J["LT", l, m, i])
                        p = start("L1", l, m, i)
                        for t in range(4):
                            ins = pe.transpose(p[:, t * P:(t + 1) * P], LT[:, i, t, :], ident[:, :])
                        done(ins)
                    pe.wait_ge(S("inv_start"), 4 * (NT * l + m) + 4)
                    for n, b in enumerate(LEVELS):
                        for i in range(2):
                            if n:
                                evacuated(pe, J["MLM", l, m, LEVELS[n - 1], i])
                            each("LM", lambda t: LT[:, i, t, :], lambda t: MM[:, i, t, :], b, i)
                        for i in range(2):
                            evacuated(pe, J["LM", l, m, b, i])
                            if n:
                                evacuated(pe, J["MLMt", l, m, LEVELS[n - 1], i])
                            if b < LEVELS[-1]:
                                each("MLM", lambda t: MT[:, i, t, :], lambda t: T1[:, i, t, :], b, i)
                            each("MLMt", lambda t: T1[:, i, t, :], lambda t: MT[:, i, t, :], b, i)
                    products("Ark", K2, R2)
                    products("Arb", A2, R2)

                    def head(i, t):
                        return slice((2 * t + i) * HD, (2 * t + i + 1) * HD)
                    for i in range(2):
                        evacuated(pe, J["Akk", l, m, i])
                    for x in range(4):
                        evacuated(pe, J["tok", l, m, x])
                    p = start("AkkV", l, m)
                    for t in range(4):
                        for i in range(2):
                            ins = pe.matmul(p[:, head(i, t)], AK[:, i, t, :], VT[:, head(i, t)], start=True, stop=True)
                    done(ins)
                    for i in range(2):
                        evacuated(pe, J["MLMt", l, m, LEVELS[-1], i])
                    evacuated(pe, J["AkkV", l, m])
                    for i in range(2):
                        each("WU", lambda t: MT[:, i, t, :], lambda t: KA[:, :, head(i, t)], i)
                    p = start("WT", l, m)
                    for t in range(4):
                        for i in range(2):
                            ins = pe.matmul(p[HD * i:HD * i + HD, t * P:(t + 1) * P], KA[:, 0, head(i, t)], MT[:, i, t, :],
                                            start=True, stop=True)
                    done(ins)
                    for i in range(2):
                        evacuated(pe, J["WU", l, m, i])
                    for c in range(2):
                        p = start("NH", l, m, c)
                        s = slice(CH * c, CH * c + CH)
                        for t in range(4):
                            for i in range(2):
                                o = p[HD * i:HD * i + HD, :]
                                pe.matmul(o[:, t * HD:(t + 1) * HD], WU[s, 4 * i + t, 0:HD], BT[s, head(i, t)],
                                          start=True, stop=True)
                                a = 4 * HD + t * HD
                                pe.matmul(o[:, a:a + HD], KhT[s, head(i, t)], VT[s, head(i, t)], start=True, stop=False)
                                ins = pe.matmul(o[:, a:a + HD], BT[s, head(i, t)], WU[s, 4 * i + t, HD:P],
                                                start=False, stop=True)
                        done(ins)
                    for c in range(2):
                        cc = 2 * m + c
                        evacuated(pe, J["NH", l, m, c])
                        for i in range(2):
                            a = slice(HD * i, HD * i + HD)
                            if cc:
                                pe.wait_ge(S("state"), 16 * l + 2 * cc - 1 + i)
                            p = start("S", l, m, c, i)
                            for t in range(4):
                                ins = pe.matmul(p[a, t * HD:(t + 1) * HD], GS[a, c, t, :], ST[a, cc % 3, t, :], start=True, stop=True)
                            done(ins)
                    evacuated(pe, J["WT", l, m])
                    for i in range(2):
                        a = slice(HD * i, HD * i + HD)
                        p = start("U", l, m, i)
                        for c in range(2):
                            s = slice(CH * c, CH * c + CH)
                            for t in range(4):
                                ins = pe.matmul(p[s, t * HD:(t + 1) * HD], WT[a, t, s], ST[a, (2 * m + c) % 3, t, :],
                                                start=True, stop=True)
                        done(ins)
                    for i in range(2):
                        a = slice(HD * i, HD * i + HD)
                        evacuated(pe, J["U", l, m, i])
                        evacuated(pe, J["Ark", l, m, i])
                        evacuated(pe, J["Arb", l, m, i])
                        p = start("Y", l, m, i)
                        for t in range(4):
                            o = p[a, t * P:(t + 1) * P]
                            pe.matmul(o, VT[:, head(i, t)], AR[:, i, t, :], start=True, stop=False)
                            pe.matmul(o, NU[:, 4 * i + t, :], AB[:, i, t, :], start=False, stop=False)
                            for c in range(2):
                                s = slice(CH * c, CH * c + CH)
                                ins = pe.matmul(o[:, s], ST[a, (2 * m + c) % 3, t, :],
                                                R2[a, t, m * P + CH * c:m * P + CH * c + CH], start=False, stop=(c == 1))
                        done(ins)
                for i in range(2):
                    evacuated(pe, J["Y", l, NT - 1, i])
                for t in range(4):
                    p = start("gmean", l, t)
                    done(pe.matmul(p, mean_64[:, :], R2[:, t, :], start=True, stop=True))
                for t in range(4):
                    pe.wait_ge(S("gn_sq"), 4 * l + t + 1)
                    p = start("gvar", l, t)
                    done(pe.matmul(p, mean_64[:, :], K2[:, t, :], start=True, stop=True))
                pe.wait_ge(S("gate_latent"), 2 * l + 2)
                pe.wait_ge(s_lora, small + 48)
                for t in range(4):
                    p = start("g", l, t)
                    pe.matmul(p, GU[:, 0, t * P:(t + 1) * P], GL[:, 0, :], start=True, stop=False)
                    done(pe.matmul(p, GU[0:32, 1, t * P:(t + 1) * P], GL[0:32, 1, :], start=False, stop=True))
                for s in range(2):
                    linear("z", l, s, h)
                for t in range(4):
                    pe.wait_ge(S("pooled"), 4 * l + t + 1)
                    p = start("pool", l, t)
                    done(pe.matmul(p, PW[:, t, :], K2[:, t, :], start=True, stop=True))
                for b in range(4):
                    linear("g0", (l, b), 0, h)
                    linear("g1", (l, b), 0, h)
                    linear("pa", (l, b), 0, y, K=4, before=lambda k: pe.wait_ge(S("ya_lo"), 4 * l + k + 1))
                    linear("pb", (l, b), 0, (mh[:, 4:8, :], ml[:, 4:8, :]), K=4,
                           before=lambda k: evacuated(pe, J["pool", l, k]))
                for s in range(4):
                    linear("wo2", l, s, h, before=(lambda k: pe.wait_ge(S("mixed_lo"), 8 * l + k + 1)) if s == 0 else None)
                mean_square(5 + 2 * l)
                n0 = 64 + 22 * l
                for c in loop(pe, 2):
                    for i in range(4):
                        linear("fg", (l, 0, i), 0, h, before=normed(5 + 2 * l) if i == 0 else None, c=c, slabs=12, jobs=24)
                        linear("fu", (l, 0, i), 0, h, c=c, slabs=12, jobs=24)
                    for s in range(4):
                        linear("fd", (l, 0), s, y, c=c, slabs=12, jobs=24,
                               before=(lambda k: pe.wait_ge(hid_done, n0 + k + 3 + 8 * c)) if s == 0 else None)
                todo[0] += 24
                for i in range(3):
                    linear("fg", (l, 2, i), 0, h)
                    linear("fu", (l, 2, i), 0, h)
                for s in range(4):
                    linear("fd", (l, 2), s, y, K=6,
                           before=(lambda k: pe.wait_ge(hid_done, n0 + 16 + k + 3)) if s == 0 else None)
            mean_square(8)
            pe.wait_ge(S("norm_val"), 8 * NORMS)
            for i in range(8):
                p = start("outT", i)
                for t in range(4):
                    ins = pe.transpose(p[:, t * P:(t + 1) * P], o_val[:, 4 * (i % 2) + t, (i // 2) * P:(i // 2 + 1) * P], ident[:, :])
                done(ins)
            assert todo[0] == plan.n


NAMES = ["x", "mem", "norm_mix", "norm_mem", "w_mem_kv", "xa_q_gain", "xa_k_gain", "w_out", "norm_mlp", "w_mlp_in",
         "w_mlp_out", "w_in_a", "conv_w", "conv_b", "w_rgate", "b_rgate", "w_igate", "b_igate", "lru_lambda", "w_in_b",
         "b_forget", "fox_q_gain", "fox_k_gain", "c_2", "ada_w_2", "ada_b_2", "norm1_g_2", "w_in_2", "v_down_2",
         "mu_shift_2", "mu_v_2", "w0_2", "w_up_2", "a0_2", "a_up_2", "v0_2", "v_up_2", "g_up_2", "k_k_2", "k_a_2",
         "r_k_2", "lnx_g_2", "lnx_b_2", "pool_w_2", "pool_scale_2", "proj_a_2", "proj_b_2", "w_out_2", "norm2_g_2",
         "w_gu_2", "w_down_2", "final_g_2"]


def kernel(**inputs):
    import numpy as np
    import concourse.bacc as bacc
    from concourse.bass_utils import run_bass_kernel_spmd

    nc = bacc.Bacc("TRN2", target_bir_lowering=False, num_devices=1)
    arrays, d = {}, {}
    for name in NAMES:
        a = np.ascontiguousarray(inputs[name])
        arrays["in_" + name] = a
        d[name] = nc.dram_tensor("in_" + name, a.shape, F32, kind="ExternalInput").ap()
    out = nc.dram_tensor("out", (1, T, D), F32, kind="ExternalOutput").ap()
    program(nc, d, out)
    r = run_bass_kernel_spmd(nc, [arrays], core_ids=[0])
    return r.results[0]["out"]
```

```python
from contextlib import ExitStack

import concourse.bass as bass
from concourse import mybir

F32 = mybir.dt.float32
F32R = mybir.dt.float32r
ALU = mybir.AluOpType
ACT = mybir.ActivationFunctionType
AX = mybir.AxisListType

P = 128
D = 1024
T = 512
KT = D // P
NT = T // P
MEM = 256
MT_ = MEM // P
D_FF = 4096
D_FF2 = 2816
FOX_H = 8
HD = 64
XA_H = 4
CH = 64
SLAB = 256
BANKS = 8
NORMS = 9
EPS = 1e-6
EPS_GN = 64e-5
KAPPA = 0.6065306597126334
WINDOWS = (2, 4, 8, 16)
SHIFT_TILES = 15
ADA_COLS = 192
N_MOD = 6 * D
TURN, VALUES, STORE, RING = 2, 3, 4, 3
LEVELS = (2, 4, 8, 16, 32)
FILL = [[("tok", 2)], [("Akk", 0)], [("tok", 3)], [("Akk", 1)], [], [("AkkV",)],
        [], [("Ark", 0)], [], [("Arb", 0)], [("Arb", 1)]]
FF_TILES = 8
CHUNKS1 = D_FF // (FF_TILES * P)
CHUNKS2 = [8, 8, 6]
Z_AT = (0, 1, 2, 3)
Z_MID = len(Z_AT) + (4 - len(Z_AT)) // 2


def loop(eng, n):
    with eng.Fori(0, n) as c:
        yield c


def vector_rows():
    tiles = [
        [("norm_mix", 16), ("norm_mem", 16), ("norm_mlp", 16), ("conv_w", 16), ("conv_b", 4), ("b_rgate", 4),
         ("b_igate", 4), ("lru_lambda", 4), ("xa_q_gain", 2), ("xa_k_gain", 2), ("fox_q_gain", 1),
         ("fox_k_gain", 1), ("c_2", 8), ("final_g_2", 8), ("norm1_g_2", 16)],
        [("norm2_g_2", 16), ("w0_2", 8), ("a0_2", 8), ("v0_2", 4), ("k_k_2", 8), ("k_a_2", 8), ("r_k_2", 8),
         ("lnx_g_2", 8), ("lnx_b_2", 8), ("pool_scale_2", 8), ("mu_shift_2", 30), ("mu_v_2", 1),
         ("b_forget", 1)],
        [("ada_b_2", 96)],
    ]
    at = {}
    for i, tile in enumerate(tiles):
        row = 0
        for name, n in tile:
            at[name] = (i * P + row, n)
            row += n
        assert row <= P
    return at


class Plan:

    def __init__(self):
        self.job = {}
        self.slab = {}
        self.last = []
        self.n = 0
        self.walk()

    def add(self, *key):
        assert key not in self.job, key
        self.job[key] = self.n
        self.n += 1

    def slab_jobs(self, name, layer, s, blocks):
        self.slab[name, layer, s] = len(self.last)
        for b in range(blocks):
            self.add(name, layer, s, b)
        self.last.append(self.n - 1)

    def lin(self, name, layer, slabs, blocks=2):
        for s in range(slabs):
            self.slab_jobs(name, layer, s, blocks)

    def z_block(self, l, t):
        s, b = divmod(t, 2)
        if b == 0:
            self.slab["z", l, s] = len(self.last)
            self.last.append(0)
        self.add("z", l, s, b)
        self.last[self.slab["z", l, s]] = self.n - 1

    def mixed(self, name, layer, slabs, blocks, other, other_layer, first):
        for s in range(slabs):
            self.slab_jobs(name, layer, s, blocks)
            if s == 0:
                for i in range(4):
                    self.add(other, other_layer, first + i)

    def attend(self, name, layer, units):
        for i in range(units + VALUES):
            if i < units:
                self.add(name + "_s", layer, i)
            if TURN <= i < units + TURN:
                self.add(name + "_t", layer, i - TURN)
            if i >= VALUES:
                self.add(name + "_o", layer, i - VALUES)

    def walk(self):
        for t in range(KT):
            self.add("xT", t)
        for i in range(3):
            self.add("vec", i)
        for i in range(4):
            self.add("memT", i)
        for l in range(2):
            if l:
                self.add("ms", 2 * l)
            if l == 0:
                self.lin("memk", 0, 2)
                self.add("ms", 0)
                self.mixed("memv", 0, 2, 2, "hn", 0, 0)
                self.lin("u", 0, 2)
                self.lin("xq", 0, 2)
                self.mixed("gate", 0, 2, 2, "hn", 0, 4)
                for t in range(4):
                    self.add("rgate", t)
                    self.add("igate", t)
                self.lin("memk", 1, 2)
                self.lin("memv", 1, 2)
            else:
                self.add("mod", 0)
                self.lin("f", l, 1, 1)
                self.mixed("xq", l, 2, 2, "hn", 1, 0)
                self.mixed("q", l, 2, 2, "hn", 1, 4)
                self.mixed("k", l, 2, 2, "hn", 1, 8)
                self.mixed("v", l, 2, 4, "hn", 1, 12)
                self.attend("fox", l, 4 * FOX_H)
            self.attend("xa", l, 2 * XA_H)
            self.lin("wo", l, 4)
            self.add("ms", 2 * l + 1)
            for c in range(CHUNKS1):
                self.lin("up", (l, c), 4)
                self.lin("down", (l, c), 4)
        for l in range(2):
            self.add("ms", 4 + 2 * l)
            if l == 0:
                self.add("mod", 1)
            self.lin("lat", l, 1)
            self.lin("gl1", l, 1, 1)
            if l:
                self.lin("vl", l, 1, 1)
            self.slab_jobs("k2", l, 0, 2)
            for name in ("lw", "la") + (("lv",) if l else ()):
                for t in range(4):
                    self.add(name, l, t)
            self.slab_jobs("k2", l, 1, 2)
            self.mixed("r2", l, 2, 2, "kn", l, 0)
            self.lin("v2", l, 2)
            for t in range(4):
                self.add("bon", l, t)
            for i in range(2):
                self.add("LT", l, 0, i)
            for m in range(NT):
                for i in range(2):
                    self.add("L", l, m, i)
                for x in range(2):
                    self.add("tok", l, m, x)
                for n in range(len(LEVELS)):
                    for i in range(2):
                        self.add("LM", l, m, n, i)
                    for i in range(2) if n else ():
                        self.add("TR", l, m, n - 1, i)
                    for f in FILL[2 * n]:
                        self.add(f[0], l, m, *f[1:])
                    for i in range(2):
                        self.add("MLM", l, m, n, i)
                    for f in FILL[2 * n + 1]:
                        self.add(f[0], l, m, *f[1:])
                for i in range(2):
                    self.add("TR", l, m, len(LEVELS) - 1, i)
                for f in FILL[-1]:
                    self.add(f[0], l, m, *f[1:])
                for i in range(2):
                    self.add("WU", l, m, i)
                self.add("WT", l, m)
                for c in range(2):
                    self.add("NH", l, m, c)
                for i in range(2):
                    self.add("S", l, m, 0, i)
                if m in Z_AT:
                    self.z_block(l, Z_AT.index(m))
                self.add("Ark", l, m, 1)
                for i in range(2):
                    self.add("U", l, m, i)
                for i in range(2):
                    self.add("S", l, m, 1, i)
                if m + 1 < NT:
                    for i in range(2):
                        self.add("LT", l, m + 1, i)
                for i in range(2):
                    self.add("Y", l, m, i)
            for t in range(4):
                self.add("gmean", l, t)
            for t in range(len(Z_AT), Z_MID):
                self.z_block(l, t)
            for t in range(4):
                self.add("gvar", l, t)
            for t in range(Z_MID, 4):
                self.z_block(l, t)
            for t in range(4):
                self.add("g", l, t)
            for p in range(4):
                for name in ("g0", "g1"):
                    self.lin(name, (l, p), 1)
                if p == 0:
                    for t in range(4):
                        self.add("pool", l, t)
                for name in ("pa", "pb"):
                    self.lin(name, (l, p), 1)
            self.lin("wo2", l, 4)
            self.add("ms", 5 + 2 * l)
            for c, n in enumerate(CHUNKS2):
                for i in range(n // 2):
                    self.lin("fg", (l, c, i), 1)
                    self.lin("fu", (l, c, i), 1)
                self.lin("fd", (l, c), 4)
        self.add("ms", 8)
        for i in range(8):
            self.add("outT", i)


class Seq:

    def __init__(self, eng, sem):
        self.eng, self.sem, self.n = eng, sem, 0

    def mark(self, ins):
        self.n += 1
        ins.then_inc(self.sem, 1)

    def step(self, ins):
        self.mark(ins)
        self.settle()

    def settle(self):
        self.eng.wait_ge(self.sem, self.n)


def program(nc, d, out):
    plan = Plan()
    J = plan.job
    VEC = vector_rows()
    ctx = ExitStack()
    with ctx:
        def sb(name, shape, dt=F32, at=None):
            return (at or ctx).enter_context(nc.sbuf_tensor(name, shape, dt))

        def sem(name):
            return ctx.enter_context(nc.semaphore(name))

        psum = ctx.enter_context(nc.psum_tensor("psum", [P, BANKS, 512], F32))
        xT = sb("xT", [P, KT, T])
        raw = sb("raw", [P, 2, KT, SLAB])
        whi = sb("whi", [P, 2, KT, SLAB], F32R)
        wlo = sb("wlo", [P, 2, KT, SLAB], F32R)
        vrows = sb("vrows", [P, 3, P])
        vec = sb("vec", [P, 3 * P])
        ident = sb("ident", [P, P])
        ident2 = sb("ident2", [P, HD])
        mean_all = sb("mean_all", [P, P])
        mean_128 = sb("mean_128", [P, P])
        mean_64 = sb("mean_64", [P, P])
        sum_64 = sb("sum_64", [P, P])
        ones = sb("ones", [P, 8])
        zeros = sb("zeros", [P, P])
        causal = sb("causal", [P, P])
        strict = sb("strict", [P, P])
        incl = sb("incl", [P, P])
        pairup = sb("pairup", [P, P])
        lvl = sb("lvl", [P, 1 + len(LEVELS), CH])
        keep = sb("keep", [P, T])
        invc = sb("invc", [P, 4, 16])
        epst = sb("epst", [P, 2])
        cact = sb("cact", [P, 8])
        mod = sb("mod", [P, 2, 48])
        gmod = sb("gmod", [P, 4, 8])
        omm = sb("omm", [P, 31])
        nsp = sb("nsp", [P, 4])
        tiny = sb("tiny", [P, 8, 8])
        gq8 = sb("gq8", [P, 2])
        stat = sb("stat", [P, 3, 2 * RING])
        PC = sb("PC", [P, 4, T // CH])
        e = ExitStack()
        hh = sb("hh", [P, KT, T], F32R, e)
        hl = sb("hl", [P, KT, T], F32R, e)
        e.close()
        ho = sb("ho", [P, 2 * KT * T])
        e = ExitStack()
        mh = sb("mh", [P, KT, T], F32R, e)
        ml = sb("ml", [P, KT, T], F32R, e)
        e.close()
        mo = sb("mo", [P, 2 * KT * T])
        REST = 16 * 1024
        rest = sb("rest", [P, REST])

        def carve(buf, off, *shape):
            n = 1
            for x in shape:
                n *= x
            assert off + n <= buf.shape[1], (off, shape)
            v = buf[:, off:off + n]
            names = "abcd"[:len(shape)]
            if len(shape) == 1:
                return v
            return v.rearrange(f"p ({' '.join(names)}) -> p {' '.join(names)}",
                               **{k: s for k, s in zip(names, shape)})

        B = 4 * T
        x_tok = carve(mo, 0, NT, D)
        mem_tok = carve(mo, NT * D, MT_, D)
        mem_sq = carve(mo, NT * D + MT_ * D, D)
        lvl2 = carve(rest, REST - 13 * P, 6, P)
        blockm = carve(rest, REST - 7 * P, 7, P)
        memT = carve(rest, 0, KT, MEM)
        V2 = carve(rest, 0, 4, T)
        n_sq = carve(rest, B, 3, T)
        n_acc = carve(rest, B + 3 * T, T)
        n_rs = carve(rest, B + 4 * T, T)
        n_rstd = carve(rest, B + 5 * T, T)
        n_val = carve(rest, B + 6 * T, 3, T)
        f_t = carve(rest, B, 2, T)
        f_v = carve(rest, B + 2 * T, 2, T)
        ada = carve(rest, B + 9 * T, 2, KT, ADA_COLS)
        ada_acc = carve(rest, B + 9 * T + 2 * KT * ADA_COLS, N_MOD)
        mK = [carve(rest, B, 4, MEM), carve(rest, 0, 4, MEM)]
        mV = [carve(rest, B + 2 * T, MT_, T), carve(rest, 2 * T, MT_, T)]
        XQ = carve(rest, B + 4 * T, 4, T)
        o = B + 8 * T
        U = carve(rest, o, 4, T + 3)
        G = carve(rest, o + B + 12, 4, T)
        UC = carve(rest, o + 2 * B + 12, 4, T)
        WR = carve(rest, o + 3 * B + 12, 4, P)
        WI = carve(rest, o + 3 * B + 12 + T, 4, P)
        RB = carve(ho, 0, 4, T)
        IB = carve(ho, B, 4, T)
        DB = carve(ho, 2 * B, 4, T)
        vtok = carve(rest, o, NT, T)
        qaug = carve(rest, o + B, FOX_H, T)
        kaug = carve(rest, o + B + FOX_H * T, FOX_H, T)
        fbuf = carve(rest, o, 4, T)
        fwork = carve(rest, B + 4 * T, 2, T)
        a_p = carve(ho, 2 * B, RING, T)
        a_t = carve(ho, 2 * B + RING * T, RING, T)
        m_sq = carve(rest, o + 3 * B + 12 + 2 * T, 4, MEM)
        m_rs = carve(rest, o + 3 * B + 12 + 4 * T, 4, MEM)
        x_sq = carve(rest, o + 3 * B + 12 + 2 * T, 4, T)
        h_sq, h_rs, qraw, kraw = (carve(mo, i * B, 4, T) for i in range(4))
        R2, K2, A2, KK, BON = (carve(rest, (1 + i) * B, 4, T) for i in range(5))
        o = 6 * B
        GL = carve(rest, o, 2, T)
        ST = carve(rest, o + 2 * T, 3, 4, HD)
        o += 2 * T + 3 * 4 * HD
        LA = carve(rest, o, T)
        VL = carve(rest, o + T, T)
        WA = carve(rest, o + 2 * T, T)
        VU = carve(rest, o + 3 * T, T)
        VD = carve(rest, o, 4, T)
        GU = carve(rest, o, 2, T)
        PW = carve(rest, o + 2 * T, 4, P)
        SG, C2, X1, X2 = (carve(mo, i * B, 4, T) for i in range(4))
        Q = 8 * P
        LT, MT = carve(mo, 0, 8, P), carve(mo, Q, 8, P)
        MM, T1 = carve(mo, 2 * Q, 8, CH), carve(mo, 2 * Q + T, 8, CH)
        AK, AR, AB = (carve(mo, i * Q, 8, P) for i in (3, 4, 5))
        KA = carve(mo, 6 * Q, 2, T)
        BT = carve(mo, 7 * Q, T)
        KhT = carve(mo, 7 * Q + T, T)
        VT = VU
        GS, HS = carve(mo, 0, 2, 4, HD), carve(mo, T, 2, 4, HD)
        WT, NU, WU = carve(mo, 2 * Q, 4, P), carve(mo, 2 * Q + T, 8, HD), carve(mo, 3 * Q, 8, P)
        mixed = [K2[:, t, :] for t in range(4)] + [A2[:, t, :] for t in range(4)]
        Z = [K2[:, :, t * P:(t + 1) * P] for t in range(4)]
        pool_sum = carve(mo, 7 * Q, 2, T)
        o_val = carve(ho, 0, KT, T)
        o_tok = carve(mo, 0, NT, D)

        made = {}

        def S(name):
            if name not in made:
                made[name] = ctx.enter_context(nc.semaphore(name))
            return made[name]

        s_vec = S("vectors_landed")
        s_x = S("x_landed")
        s_mem = S("mem_landed")
        s_const = S("constants")
        s_small = S("small_landed")
        s_lora = S("lora_landed")
        s_aug = S("decay_rows_landed")
        s_out = S("output_written")
        landed = [S(f"slab_landed{i}") for i in range(2)]
        ada_landed = [S(f"ada_landed{i}") for i in range(2)]
        hi_done = S("hi_done")
        raw_used = S("raw_used")
        written = S("written")
        bank_read = [S(f"bank_read{i}") for i in range(BANKS)]
        hid_hi = S("hidden_hi")
        hid_done = S("hidden_done")
        ada_done = S("ada_done")
        block = ctx.enter_context(nc.Block())

        def V(name, i=0, rows=P):
            c = VEC[name][0] + i
            return vec[0:rows, c:c + 1]

        def bank(job):
            return psum[:, job % BANKS, :]


        def ready(eng, job, more=0):
            eng.wait_ge(written, job + 1 + more)

        def evacuated(eng, job, more=0):
            eng.wait_ge(bank_read[job % BANKS], job // BANKS + 1 + more)

        def x_ready(eng, ver, t):
            if ver == 0:
                evacuated(eng, J["xT", t])
            elif ver < 5 and ver % 2:
                evacuated(eng, J["wo", ver // 2, t // 2, t % 2])
            elif ver < 5:
                evacuated(eng, J["down", (ver // 2 - 1, CHUNKS1 - 1), t // 2, t % 2])
            elif ver % 2:
                evacuated(eng, J["wo2", (ver - 5) // 2, t // 2, t % 2])
            else:
                evacuated(eng, J["fd", ((ver - 6) // 2, len(CHUNKS2) - 1), t // 2, t % 2])

        def bc(m, n=4):
            return m.rearrange("p (a b) -> p a b", a=1).to_broadcast([P, n, m.shape[1]])

        vector_loads = []

        def rows(name, src, r=0, cols=slice(0, P)):
            c, n = VEC[name][0] + r, src.shape[0]
            vector_loads.append((vrows[c % P:c % P + n, c // P, cols], src))
        for name in ("norm_mix", "norm_mem", "norm_mlp", "conv_b", "b_rgate", "b_igate", "lru_lambda",
                     "xa_q_gain", "xa_k_gain", "c_2", "norm1_g_2", "norm2_g_2", "w0_2", "a0_2", "v0_2",
                     "k_k_2", "k_a_2", "lnx_g_2", "lnx_b_2", "pool_scale_2", "ada_b_2"):
            rows(name, d[name].rearrange("l (t p) -> (l t) p", p=P))
        rows("conv_w", d["conv_w"][0].rearrange("j (t p) -> (j t) p", p=P))
        rows("r_k_2", d["r_k_2"].rearrange("l (t h) n -> (l t) (h n)", h=2))
        rows("final_g_2", d["final_g_2"].rearrange("(t p) -> t p", p=P))
        for name in ("fox_q_gain", "fox_k_gain"):
            for i in range(2):
                rows(name, d[name], cols=slice(i * HD, i * HD + HD))
        for l in range(2):
            rows("mu_shift_2", d["mu_shift_2"][l, 0:14 * P].rearrange("(t p) -> t p", p=P), SHIFT_TILES * l)
            rows("mu_shift_2", d["mu_shift_2"][l:l + 1, 14 * P:14 * P + 32], SHIFT_TILES * l + 14, slice(0, 32))
        for name, n in (("mu_v_2", 32), ("b_forget", 8)):
            rows(name, d[name], cols=slice(0, n))

        @block.sync
        def _(sp):
            sp.dma_start(x_tok, d["x"][0].rearrange("(t p) f -> p t f", p=P)).then_inc(s_x, 16)
            sp.dma_start(mem_tok, d["mem"][0].rearrange("(t p) f -> p t f", p=P)).then_inc(s_mem, 16)
            sp.wait_ge(s_const, 1)
            for dst, src in vector_loads[1::2]:
                sp.dma_start(dst, src).then_inc(s_vec, 16)

            def cols(w):
                return w.rearrange("(k p) n -> p k n", p=P)

            def slab(g, src, K=KT, n=SLAB, more=0):
                if g >= 2:
                    sp.wait_ge(raw_used, g - 1 + more)
                sp.dma_start(raw[:, g % 2, 0:K, 0:n], src).then_inc(landed[g % 2], 16)

            def lin(name, layer, w, col, slabs=2):
                for s in range(slabs):
                    slab(plan.slab[name, layer, s], cols(w)[:, :, col + s * SLAB:col + (s + 1) * SLAB])

            for l in range(2):
                if l == 0:
                    lin("memk", 0, d["w_mem_kv"][0], 0)
                    for n in range(8):
                        a, t = HD * (n % 2), n // 2
                        sp.dma_start(WR[a:a + HD, t, a:a + HD], d["w_rgate"][0, n]).then_inc(s_small, 16)
                        sp.dma_start(WI[a:a + HD, t, a:a + HD], d["w_igate"][0, n]).then_inc(s_small, 16)
                    lin("memv", 0, d["w_mem_kv"][0], T)
                    for i, name in ((0, "u"), (2, "xq"), (1, "gate")):
                        lin(name, l, d["w_in_a"][0], i * T)
                    lin("memk", 1, d["w_mem_kv"][1], 0)
                    lin("memv", 1, d["w_mem_kv"][1], T)
                else:
                    slab(plan.slab["f", l, 0], cols(d["w_in_b"][0])[:, :, 3 * T:3 * T + P], n=P)
                    lin("xq", l, d["w_in_b"][0], 3 * T + FOX_H)
                    for i, name in enumerate(("q", "k", "v")):
                        lin(name, l, d["w_in_b"][0], i * T)
                lin("wo", l, d["w_out"][l], 0, 4)
                g0 = plan.slab["up", (l, 0), 0]
                for c in loop(sp, CHUNKS1):
                    for i in range(4):
                        slab(g0 + i, cols(d["w_mlp_in"][l])[:, :, bass.ds(c * D + i * SLAB, SLAB)], more=8 * c)
                    for i in range(4):
                        slab(g0 + 4 + i, cols(d["w_mlp_out"][l])[:, bass.ds(c * KT, KT), i * SLAB:(i + 1) * SLAB],
                             more=8 * c)
            for l in range(2):
                w = d["w_in_2"][l]
                lin("lat", l, w, 3 * T, 1)
                slab(plan.slab["gl1", l, 0], cols(w)[:, :, 14 * P:15 * P], n=P)
                if l:
                    slab(plan.slab["vl", l, 0], cols(d["v_down_2"][0]), n=32)
                lin("k2", l, w, T)
                lin("r2", l, w, 0)
                lin("v2", l, w, 2 * T)
                lin("z", l, w, 1824)
                for p in range(4):
                    for i, name in enumerate(("g0", "g1")):
                        slab(plan.slab[name, (l, p), 0],
                             cols(w)[:, :, 1824 + T + i * D + p * SLAB:1824 + T + i * D + (p + 1) * SLAB])
                    for name in ("pa", "pb"):
                        slab(plan.slab[name, (l, p), 0],
                             cols(d[{"pa": "proj_a_2", "pb": "proj_b_2"}[name]][l])[:, :, p * SLAB:(p + 1) * SLAB], K=4)
                lin("wo2", l, d["w_out_2"][l], 0, 4)
                wg, wd = d["w_gu_2"][l], d["w_down_2"][l]
                for c in loop(sp, 2):
                    g0 = plan.slab["fg", (l, 0, 0), 0]
                    for i in range(4):
                        slab(g0 + 2 * i, cols(wg)[:, :, bass.ds(c * D + i * SLAB, SLAB)], more=12 * c)
                        slab(g0 + 2 * i + 1, cols(wg)[:, :, bass.ds(c * D + D_FF2 + i * SLAB, SLAB)], more=12 * c)
                    for i in range(4):
                        slab(g0 + 8 + i, cols(wd)[:, bass.ds(c * KT, KT), i * SLAB:(i + 1) * SLAB], more=12 * c)
                for i in range(3):
                    g0 = plan.slab["fg", (l, 2, i), 0]
                    slab(g0, cols(wg)[:, :, 2 * D + i * SLAB:2 * D + (i + 1) * SLAB])
                    slab(g0 + 1, cols(wg)[:, :, 2 * D + D_FF2 + i * SLAB:2 * D + D_FF2 + (i + 1) * SLAB])
                for i in range(4):
                    slab(plan.slab["fd", (l, 2), i], cols(wd)[:, 16:22, i * SLAB:(i + 1) * SLAB], K=6)
            for t in range(NT):
                evacuated(sp, J["outT", 2 * t])
                evacuated(sp, J["outT", 2 * t + 1])
                sp.dma_start(out[0, t * P:(t + 1) * P, :], o_tok[:, t, :]).then_inc(s_out, 16)
            sp.wait_ge(s_out, 16 * NT)

        @block.gpsimd
        def _(pool):
            q = Seq(pool, S("pool_seq"))
            q.step(pool.memset(vrows[:, :, :], 0.0))
            q.step(pool.memset(WR, 0.0))
            pool.memset(WI, 0.0).then_inc(s_const, 1)
            pool.wait_ge(s_const, 1)
            q.step(pool.memset(zeros[:, :], 0.0))
            pool.affine_select(out=ident[:, :], in_=zeros[:, :], compare_op=ALU.not_equal, fill=1.0, base=0,
                               pattern=[[-1, P]], channel_multiplier=1).then_inc(s_const, 1)
            pool.wait_ge(s_const, 2)
            q.step(pool.memset(blockm[:, :, :], 1.0))
            q.step(pool.memset(ones[:, :], 1.0))
            q.step(pool.memset(mean_all[:, :], 1.0 / D))
            q.step(pool.memset(mean_128[:, :], 1.0 / P))
            for m, v in ((mean_64, 1.0 / HD), (sum_64, 1.0)):
                q.step(pool.memset(m[:, :], 0.0))
                q.step(pool.memset(m[0:HD, 0:HD], v))
                q.step(pool.memset(m[HD:P, HD:P], v))
            q.step(pool.memset(epst[:, 0:1], EPS))
            q.step(pool.memset(epst[:, 1:2], EPS_GN))
            pool.memset(tiny[:, :, :], 0.0).then_inc(s_const, 1)
            q.step(pool.memset(keep[:, :], 1.0))
            for g, w in enumerate(WINDOWS):
                q.step(pool.memset(invc[:, g, :], 1.0 / w))
            for g, w in enumerate(WINDOWS):
                for t in range(w - 1):
                    q.step(pool.memset(invc[:, g, t:t + 1], 1.0 / (t + 1)))
            q.step(pool.memset(keep[:, 0:T:CH], 0.0))
            q.step(pool.affine_select(out=causal[:, :], in_=zeros[:, :], compare_op=ALU.is_ge, fill=-1e30, base=0,
                                      pattern=[[-1, P]], channel_multiplier=1))
            for i in range(7):
                b = 2 ** i
                m = blockm[:, i, :].rearrange("p (a b) -> p a b", b=b)
                q.step(pool.affine_select(out=m, in_=m, compare_op=ALU.is_ge, fill=0.0, base=0,
                                          pattern=[[-b, P // b], [0, b]], channel_multiplier=1))
                q.step(pool.affine_select(out=m, in_=m, compare_op=ALU.is_ge, fill=0.0, base=b - 1,
                                          pattern=[[b, P // b], [0, b]], channel_multiplier=-1))
            q.step(pool.tensor_tensor(ident2[:, :], ident[:, 0:HD], ident[:, HD:P], ALU.add))
            q.step(pool.affine_select(out=strict[:, :], in_=blockm[:, 6, :], compare_op=ALU.is_gt, fill=0.0, base=0,
                                      pattern=[[1, P]], channel_multiplier=-1))
            q.step(pool.affine_select(out=incl[:, :], in_=blockm[:, 6, :], compare_op=ALU.is_ge, fill=0.0, base=0,
                                      pattern=[[1, P]], channel_multiplier=-1))
            q.step(pool.affine_select(out=pairup[:, :], in_=blockm[:, 1, :], compare_op=ALU.is_gt, fill=0.0, base=0,
                                      pattern=[[1, P]], channel_multiplier=-1))
            for i in range(6):
                q.step(pool.tensor_tensor(lvl2[:, i, :], blockm[:, i + 1, :], blockm[:, i, :], ALU.subtract))
            for i in range(6):
                q.step(pool.affine_select(out=lvl2[:, i, :], in_=lvl2[:, i, :], compare_op=ALU.is_gt, fill=0.0, base=0,
                                          pattern=[[-1, P]], channel_multiplier=1))
            pool.tensor_tensor(lvl[:, :, :], lvl2[:, :, 0:CH], lvl2[:, :, CH:P], ALU.add).then_inc(s_const, 1)
            pool.sem_inc(hid_done, 2)
            pool.sem_inc(ada_done, 16)
            per = N_MOD // ADA_COLS // CHUNKS1
            for l in range(2):
                if l:
                    pool.wait_ge(S("decay_rows"), 2)
                    pool.dma_start(qaug[HD:HD + 1, :, :], fbuf[0:FOX_H, 0, :]).then_inc(s_aug, 16)
                    pool.dma_start(kaug[HD + 1:HD + 2, :, :], fbuf[0:FOX_H, 1, :]).then_inc(s_aug, 16)
                else:
                    pool.wait_ge(S("lru_a"), 1)
                    pool.tensor_tensor(DB, RB, RB, ALU.mult).then_inc(S("lru_a2"), 1)
                    evacuated(pool, J["igate", 3])
                    pool.tensor_tensor(IB, IB, UC, ALU.mult).then_inc(S("lru_iu"), 1)
                    pool.wait_ge(S("lru_scan"), 4)
                    pool.tensor_tensor(UC, UC, G, ALU.mult).then_inc(S("lru_y"), 1)
                ready(pool, J["ms", 2 * l + 1])
                w = d["ada_w_2"][l].rearrange("(k p) n -> p k n", p=P)
                n0 = l * CHUNKS1 * per
                for c in loop(pool, CHUNKS1):
                    for s in range(per):
                        pool.wait_ge(ada_done, 8 * (n0 + s) + 8 + c * (8 * per))
                        pool.dma_start(ada[:, s % 2, :, :], w[:, :, bass.ds(c * (per * ADA_COLS) + s * ADA_COLS, ADA_COLS)])\
                            .then_inc(ada_landed[s % 2], 16)
            def windows(l):
                ready(pool, J["Y", l, NT - 1, 1])
                for t, w in enumerate(WINDOWS):
                    evacuated(pool, J["z", l, t // 2, t % 2])
                    q.step(pool.tensor_copy(pool_sum[:, 0, :].rearrange("p (a b) -> p a b", a=4), Z[t]))
                    cur, step, n = pool_sum[:, 0, :], 1, 1
                    while step < w:
                        nxt = pool_sum[:, n % 2, :]
                        q.step(pool.tensor_tensor(nxt[:, step:T], cur[:, step:T], cur[:, 0:T - step], ALU.add))
                        q.step(pool.tensor_copy(nxt[:, 0:step], cur[:, 0:step]))
                        cur, step, n = nxt, 2 * step, n + 1
                    q.step(pool.tensor_tensor(cur[:, 0:16], cur[:, 0:16], invc[:, t, :], ALU.mult))
                    q.step(pool.tensor_scalar(cur[:, 16:T], cur[:, 16:T], 1.0 / w, None, ALU.mult))
                    pool.tensor_tensor(Z[t], cur.rearrange("p (a b) -> p a b", a=4), Z[t], ALU.subtract).then_inc(S("pooled"), 1)
                    pool.wait_ge(S("pooled"), 4 * l + t + 1)

            for l in range(2):
                ready(pool, J["mod", 1] if l == 0 else J["pool", 0, 3])
                pool.dma_start(WA[0:HD, :], d["w_up_2"][l]).then_inc(s_lora, 16)
                pool.dma_start(WA[HD:P, :], d["a_up_2"][l]).then_inc(s_lora, 16)
                if l:
                    pool.dma_start(VU[0:32, :], d["v_up_2"][0]).then_inc(s_lora, 16)
                pool.wait_ge(S("decays"), 3 * l + 3)
                pool.wait_ge(S("b_made"), l + 1)
                pool.tensor_tensor(KK, KK, SG, ALU.mult).then_inc(S("features"), 1)
                pool.tensor_tensor(A2, A2, C2, ALU.mult).then_inc(S("features"), 1)
                pool.wait_ge(S("values"), l + 1)
                pool.dma_start(GU[:, 0, :], d["g_up_2"][l, 0:P, :]).then_inc(s_lora, 16)
                pool.dma_start(GU[0:32, 1, :], d["g_up_2"][l, P:P + 32, :]).then_inc(s_lora, 16)
                pool.dma_start(PW, d["pool_w_2"][l].rearrange("g c d -> c g d")).then_inc(s_lora, 16)
                for m in range(NT):
                    if m:
                        ready(pool, J["WT", l, m - 1])
                    for i in range(2):
                        hs = slice(4 * i, 4 * i + 4)
                        evacuated(pool, J["LT", l, m, i])
                        q.step(pool.tensor_tensor(MT[:, hs, :], LT[:, hs, :], bc(pairup[:, :]), ALU.mult))
                        pool.tensor_tensor(MT[:, hs, :], bc(ident[:, :]), MT[:, hs, :], ALU.subtract).then_inc(S("mt_start"), 1)
                windows(l)

        @block.scalar
        def _(act):
            q = Seq(act, S("act_seq"))

            def hi(g, c=0, slabs=0, last=None, jobs=0):
                if g >= len(plan.last):
                    return
                act.wait_ge(landed[g % 2], 16 * (g // 2 + 1) + 8 * slabs * c)
                if g >= 2:
                    act.wait_ge(written, (plan.last[g - 2] if last is None else last) + 1 + jobs * c)
                act.activation(whi[:, g % 2, :, :], raw[:, g % 2, :, :], ACT.Copy).then_inc(hi_done, 1)

            def free(ins, job):
                ins.then_inc(bank_read[job % BANKS], 1)

            def evac(name, layer, dest, slabs=range(2), n=T, func=ACT.Copy, high=True):
                for s in slabs:
                    if high:
                        hi(plan.slab[name, layer, s] + 1)
                    for b in range(2):
                        j = J[name, layer, s, b]
                        ready(act, j)
                        free(act.activation(dest(2 * s + b), bank(j)[:, 0:n], func), j)

            def evac_tokens(name, layer, dest, tiles, slabs=range(2), high=True):
                for s in slabs:
                    if high:
                        hi(plan.slab[name, layer, s] + 1)
                    for b in range(tiles):
                        j = J[name, layer, s, b]
                        ready(act, j)
                        free(act.activation(dest[:, b, s * SLAB:(s + 1) * SLAB], bank(j)[:, 0:SLAB], ACT.Copy), j)

            def norm_squares(ni, tiles=range(KT)):
                for t in tiles:
                    x_ready(act, ni, t)
                    if t >= 3:
                        act.wait_ge(S("norm_added"), 7 * ni + max(1, t - 3))
                    act.activation(n_sq[:, t % 3, :], xT[:, t, :], ACT.Square).then_inc(S("norm_sq"), 1)

            def norm_root(ni):
                j = J["ms", ni]
                ready(act, j)
                free(act.activation(n_rs, bank(j), ACT.Sqrt, bias=epst[:, 0:1]), j)

            def norm_hi(ni, shift=None):
                for t in range(KT):
                    act.wait_ge(S("norm_val"), 8 * ni + t + 1)
                    b = mod[:, shift[0], shift[1] + t:shift[1] + t + 1] if shift else 0.0
                    act.activation(hh[:, t, :], n_val[:, t % 3, :], ACT.Identity, bias=b).then_inc(S("norm_hi"), 1)

            def squares(sq, tiles):
                for i, x in enumerate(tiles):
                    act.activation(sq[:, i, :], x, ACT.Square).then_inc(S("head_sq"), 1)

            def roots(rs, l, first, n=T):
                for i in range(4):
                    j = J["hn", l, first + i]
                    ready(act, j)
                    free(act.activation(rs[:, i, :], bank(j)[:, 0:n], ACT.Sqrt, bias=epst[:, 0:1]), j)

            def attention(name, l, units, base, parts, cols, o):
                for i in range(units + STORE):
                    if i < units:
                        act.wait_ge(S("att_max"), base + i + 1)
                        if i >= RING:
                            ready(act, J[name + "_t", l, i - RING])
                        for s, (dst, src, scale) in enumerate(parts(i)):
                            c = 2 * (i % RING) + s
                            ins = act.activation(dst, src, ACT.Exp, bias=stat[:, 0, c:c + 1], scale=scale,
                                                 accum_out=stat[:, 1, c:c + 1])
                        free(ins, J[name + "_s", l, i])
                    u = i - TURN
                    if 0 <= u < units:
                        j = J[name + "_t", l, u]
                        ready(act, j)
                        if u >= RING:
                            ready(act, J[name + "_o", l, u - RING])
                        n = cols(u)
                        free(act.activation(a_t[:, u % RING, 0:n], bank(j)[:, 0:n], ACT.Copy), j)
                    u = i - STORE
                    if u >= 0:
                        j = J[name + "_o", l, u]
                        ready(act, j)
                        dst, src = o(u, bank(j))
                        act.activation(dst, src, ACT.Copy).then_inc(S("att_hi"), 1)

            act.wait_ge(s_const, 1)
            for dst, src in vector_loads[0::2]:
                act.dma_start(dst, src).then_inc(s_vec, 16)
            act.wait_ge(s_mem, 16)
            act.wait_ge(s_const, 3)
            for t in range(MT_):
                q.mark(act.activation(mem_sq, mem_tok[:, t, :], ACT.Square, accum_out=tiny[:, 0, t:t + 1]))
                q.settle()
            act.activation(tiny[:, 1, 0:2], tiny[:, 0, 0:2], ACT.Sqrt, scale=1.0 / D, bias=epst[:, 0:1])\
               .then_inc(S("mem_root"), 1)
            hi(0)
            for i in range(4):
                j = J["memT", i]
                ready(act, j)
                free(act.activation(memT[:, 2 * i:2 * i + 2, :], bank(j).rearrange("p (a b) -> p a b", a=2), ACT.Copy), j)
            for l in range(2):
                def mem_high(m):
                    for t in range(KT):
                        act.activation(mh[:, t, m * MEM:(m + 1) * MEM], memT[:, t, :], ACT.Copy,
                                       scale=V("norm_mem", 8 * m + t)).then_inc(S("mem_hi"), 1)
                if l == 0:
                    for i in range(3):
                        evacuated(act, J["vec", i])
                    for i in range(4):
                        evacuated(act, J["memT", i])
                    mem_high(0)
                    hi(1)
                    norm_squares(0)
                    act.wait_ge(S("norm_added"), 7)
                    for s in range(2):
                        evac("memk", 0, lambda t: mK[0][:, t, :], [s], MEM, high=s > 0)
                    norm_root(0)
                    for i in range(4):
                        evacuated(act, J["memk", 0, i // 2, i % 2])
                    squares(m_sq, [mK[0][:, t, :] for t in range(4)])
                    evac_tokens("memv", 0, mV[0], MT_, [0])
                    hi(plan.slab["u", 0, 0])
                    roots(m_rs, 0, 0, MEM)
                    norm_hi(0)
                    evac_tokens("memv", 0, mV[0], MT_, [1], high=False)
                    evac("u", l, lambda t: U[:, t, 3:T + 3])
                    evac("xq", l, lambda t: XQ[:, t, :])
                    mem_high(1)
                    act.wait_ge(S("lam_abs"), 1)
                    act.activation(tiny[:, 3, 0:4], tiny[:, 2, 0:4], ACT.Exp, scale=-1.0).then_inc(S("lam_exp"), 1)
                    act.activation(cact[:, :], vec[:, VEC["c_2"][0]:VEC["c_2"][0] + 8], ACT.Silu).then_inc(S("c_act"), 1)
                    for i in range(4):
                        evacuated(act, J["xq", l, i // 2, i % 2])
                    act.wait_ge(S("head_done"), 4)
                    squares(x_sq, [XQ[:, t, :] for t in range(4)])
                    evac("gate", l, lambda t: G[:, t, :], [0], func=ACT.Gelu_apprx_tanh)
                    hi(plan.slab["gate", l, 1] + 1)
                    roots(x_sq, 0, 4)
                    for b in range(2):
                        j = J["gate", l, 1, b]
                        ready(act, j)
                        free(act.activation(G[:, 2 + b, :], bank(j), ACT.Gelu_apprx_tanh), j)
                    for t in range(4):
                        for dst, name, b in ((RB, "rgate", "b_rgate"), (IB, "igate", "b_igate")):
                            j = J[name, t]
                            ready(act, j)
                            free(act.activation(dst[:, t, :], bank(j), ACT.Sigmoid, bias=V(b, t)), j)
                    act.wait_ge(S("lru_loga"), 4)
                    act.activation(U[:, :, 0:T], RB, ACT.Tanh, scale=-1.0).then_inc(S("lru_tanh"), 1)
                    act.wait_ge(S("lru_tanh"), 1)
                    act.activation(RB, RB, ACT.Exp).then_inc(S("lru_a"), 1)
                    evac("memk", 1, lambda t: mK[1][:, t, :], [0], MEM)
                    act.wait_ge(S("lru_1ma2"), 1)
                    act.activation(U[:, :, 0:T], U[:, :, 0:T], ACT.Sqrt).then_inc(S("lru_root"), 1)
                    evac("memk", 1, lambda t: mK[1][:, t, :], [1], MEM)
                    evac_tokens("memv", 1, mV[1], MT_)
                else:
                    norm_squares(2)
                    norm_root(2)
                    norm_hi(2)
                    for i in range(4):
                        evacuated(act, J["memk", 1, i // 2, i % 2])
                    squares(h_sq[:, :, 0:MEM], [mK[1][:, t, :] for t in range(4)])
                    hi(plan.slab["f", l, 0] + 1)
                    act.wait_ge(S("forget_x"), 1)
                    q.mark(act.activation(fbuf[0:FOX_H, 1, :], fbuf[0:FOX_H, 0, :], ACT.Abs))
                    q.settle()
                    act.activation(fbuf[0:FOX_H, 1, :], fbuf[0:FOX_H, 1, :], ACT.Exp, scale=-1.0).then_inc(S("forget_exp"), 1)
                    dst = {"q": lambda t: qraw[:, t, :], "k": lambda t: kraw[:, t, :], "xq": lambda t: XQ[:, t, :]}
                    first, n = 0, MEM
                    act.wait_ge(S("forget_end"), 1)
                    for name in ("xq", "q", "k", "v"):
                        if name == "v":
                            act.wait_ge(s_aug, 32)
                            evac_tokens("v", l, vtok, NT, [0])
                        else:
                            evac(name, l, dst[name], [0])
                        if first:
                            act.wait_ge(S("head_done"), 8 + first)
                        hi(plan.slab[name, l, 1] + 1)
                        roots(h_rs[:, :, 0:n], l, first, n)
                        first, n = first + 4, T
                        for b in range(4 if name == "v" else 2):
                            j = J[name, l, 1, b]
                            ready(act, j)
                            if name == "v":
                                free(act.activation(vtok[:, b, SLAB:2 * SLAB], bank(j)[:, 0:SLAB], ACT.Copy), j)
                            else:
                                free(act.activation(dst[name](2 + b), bank(j), ACT.Copy), j)
                        if name != "v":
                            for i in range(4):
                                evacuated(act, J[name, l, i // 2, i % 2])
                            squares(h_sq, [dst[name](t) for t in range(4)])

                    def fox_parts(i):
                        n = P * (i % NT + 1)
                        return [(a_p[:, i % RING, 0:n], bank(J["fox_s", 1, i])[:, 0:n], 1.0)]

                    def fox_o(i, p):
                        h, t = i // NT, i % NT
                        a = HD * (h % 2)
                        return mh[a:a + HD, h // 2, t * P:(t + 1) * P], p[a:a + HD, 0:P]
                    attention("fox", l, 4 * FOX_H, 8, fox_parts, lambda i: P * (i % NT + 1), fox_o)

                def xa_parts(i):
                    b = bank(J["xa_s", l, i])
                    return [(a_p[:, i % RING, s * MEM:(s + 1) * MEM], b[:, s * MEM:(s + 1) * MEM], float(P) ** -0.5)
                            for s in range(2)]
                attention("xa", l, 2 * XA_H, 40 * l, xa_parts, lambda i: T,
                          lambda i, p: (mh[:, 4 + i // 2, (i % 2) * MEM:(i % 2 + 1) * MEM], p[:, 0:MEM]))
                if l == 0:
                    act.wait_ge(S("lru_y"), 1)
                    act.activation(mh[:, 0:4, :], UC, ACT.Copy).then_inc(S("lru_hi"), 1)
                for s in range(4):
                    hi(plan.slab["wo", l, s] + 1)
                    if s:
                        norm_squares(2 * l + 1, (2 * s - 2, 2 * s - 1))
                norm_squares(2 * l + 1, (6, 7))
                norm_root(2 * l + 1)
                norm_hi(2 * l + 1)
                g0, j0, n0 = plan.slab["up", (l, 0), 0], J["up", (l, 0), 0, 0], 32 * l
                for c in loop(act, CHUNKS1):
                    for i in range(8):
                        hi(g0 + i + 1, c, 8, j0 + 2 * i - 1, 16)
                        for b in range(2) if i < 4 else ():
                            m, j = 2 * i + b, j0 + 2 * i + b
                            ready(act, j, 16 * c)
                            act.wait_ge(hid_done, n0 + m + 1 + 8 * c)
                            free(act.activation(f_t[:, m % 2, :], bank(j), ACT.Relu), j)
                            evacuated(act, j, 2 * c)
                            act.activation(mh[:, m, :], f_t[:, m % 2, :], ACT.Square).then_inc(hid_hi, 1)
            for l in range(2):
                if l == 0:
                    norm_squares(4)
                norm_root(4 + 2 * l)
                norm_hi(4 + 2 * l, (l, 0))

                def own_part(name, s, b, c, dst, rows=P):
                    j = J[name, l, s, b]
                    ready(act, j)
                    act.activation(dst, bank(j)[0:rows, :], ACT.Copy, scale=omm[0:rows, c:c + 1])\
                       .then_inc(S("shift_own"), 1)

                c0 = SHIFT_TILES * l

                def own_tiles(i, name, s, dst):
                    hi(plan.slab[name, l, s] + 1)
                    for b in range(2):
                        own_part(name, s, b, c0 + 4 * i + 2 * s + b, dst[:, 2 * s + b, :])

                hi(plan.slab["lat", l, 0] + 1)
                own_part("lat", 0, 0, c0 + 12, LA)
                own_part("lat", 0, 1, c0 + 13, GL[:, 0, :])
                hi(plan.slab["gl1", l, 0] + 1)
                own_part("gl1", 0, 0, c0 + 14, GL[0:32, 1, :], 32)
                if l:
                    hi(plan.slab["vl", l, 0] + 1)
                    own_part("vl", 0, 0, 2 * SHIFT_TILES, VL[0:32, :], 32)
                evacuated(act, J["gl1", l, 0, 0])
                act.activation(LA[0:HD, :], LA[0:HD, :], ACT.Tanh).then_inc(S("decay_latent"), 1)
                act.activation(GL[:, 0, :], GL[:, 0, :], ACT.Sigmoid).then_inc(S("gate_latent"), 1)
                act.activation(GL[0:32, 1, :], GL[0:32, 1, :], ACT.Sigmoid).then_inc(S("gate_latent"), 1)
                own_tiles(1, "k2", 0, K2)
                hi(plan.slab["k2", l, 1] + 1)
                for name, dst, b0 in (("lw", SG, "w0_2"), ("la", X2, "a0_2")) + ((("lv", BON, "v0_2"),) if l else ()):
                    for t in range(4):
                        j = J[name, l, t]
                        ready(act, j)
                        b = V(b0, t if name == "lv" else 4 * l + t)
                        free(act.activation(dst[:, t, :], bank(j), ACT.Sigmoid, bias=b), j)
                for b in range(2):
                    own_part("k2", 1, b, c0 + 6 + b, K2[:, 2 + b, :])
                act.wait_ge(S("kk_raw"), 4 * l + 4)
                act.activation(X1, KK, ACT.Square).then_inc(S("kk_sq"), 1)
                own_tiles(0, "r2", 0, R2)
                hi(plan.slab["r2", l, 1] + 1)
                for t in range(4):
                    j = J["kn", l, t]
                    ready(act, j)
                    free(act.activation(X1[:, t, :], bank(j), ACT.Sqrt), j)
                for b in range(2):
                    own_part("r2", 1, b, c0 + 2 + b, R2[:, 2 + b, :])
                hi(plan.slab["v2", l, 0] + 1)
                act.wait_ge(S("kk_done"), l + 1)
                act.wait_ge(S("cum_decay"), l + 1)
                act.activation(X1, C2, ACT.Exp, scale=-KAPPA).then_inc(S("decays"), 1)
                act.activation(SG, SG, ACT.Exp, scale=-KAPPA).then_inc(S("decays"), 1)
                act.wait_ge(S("decays"), 3 * l + 2)
                act.activation(C2, C2, ACT.Exp, scale=KAPPA).then_inc(S("decays"), 1)
                v_dst = VD if l else V2
                for b in range(2):
                    own_part("v2", 0, b, c0 + 8 + b, v_dst[:, b, :])
                own_tiles(2, "v2", 1, v_dst)
                hi(plan.slab["z", l, 0] + 1)
                def z_out(t):
                    j = J["z", l, t // 2, t % 2]
                    ready(act, j)
                    free(act.activation(Z[t], bank(j).rearrange("p (a b) -> p a b", a=4), ACT.Copy), j)

                for m in range(NT):
                    def token_major(x, dst):
                        j = J["tok", l, m, x]
                        ready(act, j)
                        free(act.activation(dst, bank(j), ACT.Copy), j)

                    def transposed(n):
                        if n == 0:
                            act.wait_ge(S("mt_start"), 2 * (NT * l + m) + 2)
                        for i in range(2):
                            j = J["TR", l, m, n, i]
                            ready(act, j)
                            p = bank(j).rearrange("p (h n) -> p h n", h=4)
                            for c in range(2):
                                s = slice(CH * c, CH * c + CH)
                                ins = act.activation(MT[s, 4 * i:4 * i + 4, s], p[0:CH, :, s], ACT.Copy)
                            free(ins, j)

                    token_major(0, KA[:, 0, :])
                    token_major(1, BT)
                    for n in range(1, len(LEVELS)):
                        transposed(n - 1)
                        if n == 1:
                            token_major(3, VT)
                        if n == 3:
                            j = J["AkkV", l, m]
                            ready(act, j)
                            free(act.activation(KA[:, 1, :], bank(j), ACT.Copy), j)
                    transposed(len(LEVELS) - 1)
                    for i in range(2):
                        j = J["WU", l, m, i]
                        ready(act, j)
                        p = bank(j).rearrange("p (j n) -> p j n", j=4)
                        act.activation(WU[:, 4 * i:4 * i + 4, 0:HD], p[:, :, 0:HD], ACT.Copy)
                        free(act.activation(WU[:, 4 * i:4 * i + 4, HD:P], p[:, :, HD:P], ACT.Copy, scale=-1.0), j)
                    j = J["WT", l, m]
                    ready(act, j)
                    free(act.activation(WT, bank(j).rearrange("p (j n) -> p j n", j=4), ACT.Copy), j)
                    if m in Z_AT:
                        ready(act, J["Ark", l, m, 1])
                        z_out(Z_AT.index(m))
                    for i in range(2):
                        j = J["Y", l, m, i]
                        ready(act, j)
                        a = HD * i
                        free(act.activation(R2[a:a + HD, :, m * P:(m + 1) * P],
                                            bank(j)[a:a + HD, :].rearrange("p (j n) -> p j n", j=4), ACT.Copy), j)
                for t in range(4):
                    evacuated(act, J["gmean", l, t])
                    act.activation(KK[:, t, :], R2[:, t, :], ACT.Square).then_inc(S("gn_sq"), 1)
                for t in range(len(Z_AT), Z_MID):
                    z_out(t)
                hi(plan.slab["z", l, 1] + 1)
                for t in range(4):
                    j = J["gvar", l, t]
                    ready(act, j)
                    free(act.activation(A2[:, t, :], bank(j), ACT.Sqrt, bias=epst[:, 1:2]), j)
                for t in range(Z_MID, 4):
                    z_out(t)
                hi(plan.slab["g0", (l, 0), 0] + 1)
                for t in range(4):
                    evacuated(act, J["g", l, t])
                    act.activation(mh[:, t, :], R2[:, t, :], ACT.Copy).then_inc(S("ya_hi"), 1)
                for p in range(4):
                    for i, name in enumerate(("g0", "g1")):
                        if (p, name) != (0, "g0"):
                            hi(plan.slab[name, (l, p), 0] + 1)
                        for b in range(2):
                            j = J[name, (l, p), 0, b]
                            ready(act, j)
                            if p >= 1:
                                evacuated(act, J["pb", (l, p - 1), 0, 1])
                            free(act.activation(KK[:, 2 * i + b, :], bank(j), ACT.Sigmoid), j)
                    for t in range(4) if p == 0 else ():
                        j = J["pool", l, t]
                        ready(act, j)
                        act.activation(mh[:, 4 + t, :], bank(j), ACT.Copy, scale=V("pool_scale_2", 4 * l + t))\
                           .then_inc(S("yb_hi"), 1)
                    for name in ("pa", "pb"):
                        hi(plan.slab[name, (l, p), 0] + 1)
                ready(act, J["g1", (l, 3), 0, 1])
                for t in range(KT):
                    act.wait_ge(S("mixed"), 8 * l + t + 1)
                    act.activation(hh[:, t, :], mixed[t], ACT.Copy).then_inc(S("mixed_hi"), 1)
                for s in range(4):
                    hi(plan.slab["wo2", l, s] + 1)
                    if s:
                        norm_squares(5 + 2 * l, (2 * s - 2, 2 * s - 1))
                norm_squares(5 + 2 * l, (6, 7))
                norm_root(5 + 2 * l)
                norm_hi(5 + 2 * l, (l, 24))

                def gated(i, g0, j0, n0, c):
                    hi(g0 + 2 * i + 1, c, 12, j0 + 4 * i - 1, 24)
                    for b in range(2):
                        m, j = 2 * i + b, j0 + 4 * i + b
                        ready(act, j, 24 * c)
                        act.wait_ge(hid_done, n0 + m + 1 + 8 * c)
                        free(act.activation(f_t[:, m % 2, :], bank(j), ACT.Silu), j)
                    hi(g0 + 2 * i + 2, c, 12, j0 + 4 * i + 1, 24)
                    for b in range(2):
                        m, j = 2 * i + b, j0 + 4 * i + 2 + b
                        evacuated(act, j, 3 * c)
                        act.activation(mh[:, m, :], f_v[:, m % 2, :], ACT.Copy).then_inc(hid_hi, 1)

                g0, j0, n0 = plan.slab["fg", (l, 0, 0), 0], J["fg", (l, 0, 0), 0, 0], 64 + 22 * l
                for c in loop(act, 2):
                    for i in range(4):
                        gated(i, g0, j0, n0, c)
                    for i in range(4):
                        hi(g0 + 8 + i + 1, c, 12, j0 + 16 + 2 * i - 1, 24)
                g0, j0, n0 = g0 + 24, j0 + 48, n0 + 16
                for i in range(3):
                    gated(i, g0, j0, n0, 0)
                for i in range(4):
                    hi(g0 + 6 + i + 1)
                    if i:
                        norm_squares(6 + 2 * l, (2 * i - 2, 2 * i - 1))
                norm_squares(6 + 2 * l, (6, 7))
            norm_root(8)
            for i in range(0, 8, 2):
                j = J["outT", i]
                ready(act, j)
                free(act.activation(o_tok[:, i // 2, 0:T], bank(j), ACT.Copy), j)

        @block.vector
        def _(dve):
            q = Seq(dve, S("dve_seq"))

            def free(ins, job):
                ins.then_inc(bank_read[job % BANKS], 1)

            def f32(x):
                return x.bitcast(F32)

            def lo(g, more=0):
                if g >= len(plan.last):
                    return
                dve.wait_ge(hi_done, g + 1 + more)
                dve.tensor_tensor(wlo[:, g % 2, :, :], raw[:, g % 2, :, :], f32(whi[:, g % 2, :, :]), ALU.subtract)\
                   .then_inc(raw_used, 1)

            def lows(name, layer, slabs):
                for s in slabs if type(slabs) is list else range(slabs):
                    lo(plan.slab[name, layer, s] + 1)

            def norm_sums(ni, tiles=range(1, KT)):
                for t in tiles:
                    dve.wait_ge(S("norm_sq"), 8 * ni + t + 1)
                    if t == 1:
                        dve.tensor_tensor(n_acc, n_sq[:, 0, :], n_sq[:, 1, :], ALU.add).then_inc(S("norm_added"), 1)
                    else:
                        dve.wait_ge(S("norm_added"), 7 * ni + t - 1)
                        dve.tensor_tensor(n_acc, n_acc, n_sq[:, t % 3, :], ALU.add).then_inc(S("norm_added"), 1)

            def norm(ni, gain, shift=None, slab=None):
                evacuated(dve, J["ms", ni])
                q.mark(dve.reciprocal(n_rstd, n_rs))
                if slab is not None:
                    lo(slab)
                q.settle()
                for t in range(KT + 1):
                    if t < KT:
                        if 3 <= t and ni < 8:
                            dve.wait_ge(S("norm_lo"), 8 * ni + t - 2)
                        if ni < 8:
                            dst = n_val[:, t % 3, :]
                        else:
                            dst = o_val[:, t, :]
                        dve.scalar_tensor_tensor(dst, xT[:, t, :], gain(t), n_rstd, ALU.mult, ALU.mult)\
                           .then_inc(S("norm_val"), 1)
                    if t >= 1 and ni < 8:
                        s = t - 1
                        dve.wait_ge(S("norm_hi"), 8 * ni + s + 1)
                        if shift:
                            b = mod[:, shift[0], shift[1] + s:shift[1] + s + 1]
                            dve.scalar_tensor_tensor(hl[:, s, :], n_val[:, s % 3, :], b, f32(hh[:, s, :]),
                                                     ALU.add, ALU.subtract).then_inc(S("norm_lo"), 1)
                        else:
                            dve.tensor_tensor(hl[:, s, :], n_val[:, s % 3, :], f32(hh[:, s, :]), ALU.subtract)\
                               .then_inc(S("norm_lo"), 1)

            def head_norm(rs, l, first, i, parts, n=T):
                evacuated(dve, J["hn", l, first + i])
                q.mark(dve.reciprocal(rs[:, i, 0:n], rs[:, i, 0:n]))
                q.settle()
                for out, x, gain, r in parts:
                    ins = dve.scalar_tensor_tensor(out, x, gain, rs[r, i, 0:n], ALU.mult, ALU.mult)
                ins.then_inc(S("head_done"), 1)

            every = slice(0, P)

            def softplus_tail(x, e, s, u, p, dst, scale):
                q.mark(dve.tensor_scalar(u, e, 2.0, None, ALU.add))
                q.settle()
                q.mark(dve.reciprocal(u, u))
                q.settle()
                q.mark(dve.tensor_tensor(s, e, u, ALU.mult))
                q.settle()
                q.mark(dve.tensor_tensor(u, s, s, ALU.mult))
                q.settle()
                q.mark(dve.tensor_scalar(p, u, 1.0 / 19, None, ALU.mult))
                for k in range(17, 1, -2):
                    q.settle()
                    q.mark(dve.scalar_tensor_tensor(p, p, 1.0 / k, u, ALU.add, ALU.mult))
                q.settle()
                q.mark(dve.scalar_tensor_tensor(p, p, 1.0, s, ALU.add, ALU.mult))
                q.mark(dve.tensor_scalar(u, x, 0.0, scale, ALU.max, ALU.mult))
                q.settle()
                ins = dve.scalar_tensor_tensor(dst, p, 2.0 * scale, u, ALU.mult, ALU.add)
                q.mark(ins)
                q.settle()

            def adaln(l):
                j = J["mod", l]
                ready(dve, j)
                c = VEC["ada_b_2"][0] + 48 * l
                free(dve.tensor_tensor(mod[:, l, :], bank(j)[:, 0:48], vec[:, c:c + 48], ALU.add), j)
                evacuated(dve, j)
                for i, name in enumerate(("norm1_g_2", "norm2_g_2")):
                    c = VEC[name][0] + 8 * l
                    q.mark(dve.scalar_tensor_tensor(gmod[:, 2 * l + i, :], mod[:, l, 8 + 24 * i:16 + 24 * i], 1.0,
                                                    vec[:, c:c + 8], ALU.add, ALU.mult))
                q.settle()

            def attention(name, l, units, base, width, scale, probs, o):
                for i in range(units + STORE):
                    if i < units:
                        j = J[name + "_s", l, i]
                        parts, n = width(i)
                        c = 2 * (i % RING)
                        ready(dve, j)
                        src = bank(j)[:, 0:parts * n].rearrange("p (a n) -> p a n", a=parts)
                        ins = dve.tensor_reduce(stat[:, 0, c:c + parts], src, AX.X, ALU.max, negate=True)
                        if scale != 1.0:
                            q.mark(ins)
                            q.settle()
                            ins = dve.tensor_scalar(stat[:, 0, c:c + parts], stat[:, 0, c:c + parts], scale, None, ALU.mult)
                        ins.then_inc(S("att_max"), 1)
                    if 1 <= i <= units:
                        parts, n = width(i - 1)
                        c = 2 * ((i - 1) % RING)
                        evacuated(dve, J[name + "_s", l, i - 1])
                        q.mark(dve.reciprocal(stat[:, 2, c:c + parts], stat[:, 1, c:c + parts]))
                        q.settle()
                        for s in range(parts):
                            x = a_p[:, (i - 1) % RING, s * n:(s + 1) * n]
                            ins = dve.tensor_scalar(x, x, stat[:, 2, c + s:c + s + 1], None, ALU.mult)
                        ins.then_inc(S("att_probs"), 1)
                    u = i - STORE
                    if u >= 0:
                        j = J[name + "_o", l, u]
                        dve.wait_ge(S("att_hi"), base + u + 1)
                        low, high, src = o(u, bank(j))
                        free(dve.tensor_tensor(low, src, f32(high), ALU.subtract), j)

            def add_x(j, t, gate=None):
                if gate is None:
                    free(dve.tensor_tensor(xT[:, t, :], xT[:, t, :], bank(j), ALU.add), j)
                else:
                    free(dve.scalar_tensor_tensor(xT[:, t, :], bank(j), gate, xT[:, t, :], ALU.mult, ALU.add), j)

            for t in range(KT):
                j = J["xT", t]
                ready(dve, j)
                free(dve.tensor_copy(xT[:, t, :], bank(j)), j)
            dve.wait_ge(s_const, 3)
            for i in range(3):
                j = J["vec", i]
                ready(dve, j)
                free(dve.tensor_copy(vec[:, i * P:(i + 1) * P], bank(j)[:, 0:P]), j)
                evacuated(dve, j)
            c = VEC["mu_shift_2"][0]
            dve.tensor_scalar(omm[:, :], vec[:, c:c + 31], -1.0, 1.0, ALU.mult, ALU.add)
            c = VEC["fox_q_gain"][0]
            q.mark(dve.tensor_scalar(gq8[:, 0:1], vec[:, c:c + 1], float(HD) ** -0.5, None, ALU.mult))
            c = VEC["lru_lambda"][0]
            q.mark(dve.tensor_scalar(tiny[:, 4, 0:4], vec[:, c:c + 4], -1.0, None, ALU.mult))
            q.settle()
            dve.tensor_tensor(tiny[:, 2, 0:4], tiny[:, 4, 0:4], vec[:, c:c + 4], ALU.max).then_inc(S("lam_abs"), 1)
            dve.wait_ge(S("mem_root"), 1)
            q.mark(dve.reciprocal(tiny[:, 1, 2:4], tiny[:, 1, 0:2]))
            q.settle()
            for t in range(MT_):
                dve.tensor_scalar(mem_tok[:, t, :], mem_tok[:, t, :], tiny[:, 1, 2 + t:3 + t], None, ALU.mult)\
                   .then_inc(S("mem_normed"), 1)
            lo(0)
            dve.wait_ge(s_const, 4)
            for l in range(2):
                def mem_low(m):
                    ms = slice(m * MEM, (m + 1) * MEM)
                    for t in range(KT):
                        dve.wait_ge(S("mem_hi"), 8 * m + t + 1)
                        dve.scalar_tensor_tensor(ml[:, t, ms], memT[:, t, :], V("norm_mem", 8 * m + t),
                                                 f32(mh[:, t, ms]), ALU.mult, ALU.subtract).then_inc(S("mem_lo"), 1)

                def x_tiles(t):
                    return [(XQ[:, t, :], XQ[:, t, :], V("xa_q_gain", l), every)]

                def mem_tiles(t):
                    return [(mK[l][:, t, :], mK[l][:, t, :], V("xa_k_gain", l), every)]
                if l == 0:
                    mem_low(0)
                    lows("memk", 0, [0])
                    norm_sums(0)
                    lows("memk", 0, [1])
                    lows("memv", 0, [0])
                else:
                    norm_sums(2 * l)
                norm(2 * l, lambda t: V("norm_mix", 8 * l + t), slab=None if l else plan.slab["u", 0, 0])
                if l == 1:
                    adaln(0)
                if l == 0:
                    q.mark(dve.memset(U[:, :, 0:3], 0.0))
                    for s in range(2):
                        lows("u", l, [s])
                        for t in (2 * s, 2 * s + 1):
                            head_norm(m_rs, 0, 0, t, mem_tiles(t), MEM)
                    q.settle()
                    for s in range(2):
                        lows("xq", l, [s])
                        ts = (2 * s, 2 * s + 1)
                        for t in ts:
                            evacuated(dve, J["u", l, t // 2, t % 2])
                            q.mark(dve.tensor_scalar(UC[:, t, :], U[:, t, 0:T], V("conv_w", t), V("conv_b", t), ALU.mult, ALU.add))
                        for j in range(1, 4):
                            q.settle()
                            for t in ts:
                                ins = dve.scalar_tensor_tensor(UC[:, t, :], U[:, t, j:j + T], V("conv_w", 4 * j + t),
                                                               UC[:, t, :], ALU.mult, ALU.add)
                                if j < 3:
                                    q.mark(ins)
                                else:
                                    ins.then_inc(S("conv"), 1)
                    lows("gate", l, 2)
                    for t in range(2):
                        head_norm(x_sq, 0, 4, t, x_tiles(t))
                    mem_low(1)
                    dve.wait_ge(S("lam_exp"), 1)
                    softplus_tail(tiny[:, 4, 0:4], tiny[:, 3, 0:4], tiny[:, 5, 0:4], tiny[:, 6, 0:4], tiny[:, 7, 0:4], nsp[:, :], -8.0)
                    for t in range(4):
                        evacuated(dve, J["rgate", t])
                        dve.tensor_scalar(RB[:, t, :], RB[:, t, :], nsp[:, t:t + 1], None, ALU.mult).then_inc(S("lru_loga"), 1)
                    lows("memk", 1, [0])
                    dve.wait_ge(S("lru_a2"), 1)
                    dve.scalar_tensor_tensor(U[:, :, 0:T], DB, 1.0, U[:, :, 0:T], ALU.add, ALU.mult).then_inc(S("lru_1ma2"), 1)
                    lows("memk", 1, [1])
                    head_norm(x_sq, 0, 4, 2, x_tiles(2))
                    lows("memv", 1, [0])
                    head_norm(x_sq, 0, 4, 3, x_tiles(3))
                    dve.wait_ge(S("lru_root"), 1)
                    dve.wait_ge(S("lru_iu"), 1)
                    q.mark(dve.tensor_tensor(IB, IB, U[:, :, 0:T], ALU.mult))
                    lows("memv", 1, [1])
                    q.settle()
                    for t in range(4):
                        dve.tensor_tensor_scan(UC[:, t, :], RB[:, t, :], IB[:, t, :], 0.0, ALU.mult, ALU.add)\
                           .then_inc(S("lru_scan"), 1)
                else:
                    ready(dve, J["mod", 0])
                    for x in (qaug, kaug):
                        dve.memset(x[HD:HD + 2, :, :], 1.0).then_inc(S("decay_rows_one"), 1)

                    def pair(raw_, out, gain, t):
                        return [(out[0:HD, 2 * t + i, :], raw_[HD * i:HD * i + HD, t, :], gain[HD * i:HD * i + HD, :],
                                 slice(HD * i, HD * i + HD)) for i in range(2)]
                    lows("f", l, 1)
                    j = J["f", l, 0, 0]
                    ready(dve, j)
                    dve.tensor_scalar(fbuf[0:FOX_H, 0, :], bank(j)[0:FOX_H, :], V("b_forget", 0, FOX_H), -1.0,
                                      ALU.add, ALU.mult).then_inc(S("forget_x"), 1)
                    dve.wait_ge(S("forget_x"), 1)
                    free(dve.memset(fbuf[0:FOX_H, 3, :], 1.0), j)
                    dve.wait_ge(S("forget_exp"), 1)
                    f = [fbuf[0:FOX_H, i, :] for i in range(4)]
                    softplus_tail(f[0], f[1], f[2], fwork[0:FOX_H, 0, :], fwork[0:FOX_H, 1, :], f[1], 1.0)
                    dve.tensor_tensor_scan(f[0], f[3], f[1], 0.0, ALU.mult, ALU.subtract).then_inc(S("decay_rows"), 1)
                    dve.wait_ge(S("decay_rows"), 1)
                    dve.tensor_scalar(f[1], f[0], -1.0, None, ALU.mult).then_inc(S("decay_rows"), 1)
                    dve.sem_inc(S("forget_end"), 1)
                    lows("xq", l, [0])
                    groups = [mem_tiles, x_tiles, lambda t: pair(qraw, qaug, gq8[:, 0:1], t),
                              lambda t: pair(kraw, kaug, V("fox_k_gain"), t)]
                    steps = [("xq", 1), ("q", 0), ("q", 1), ("k", 0), ("k", 1), ("v", 0), ("v", 1)]
                    for i, (name, s) in enumerate(steps):
                        lows(name, l, [s])
                        g = i // 2
                        ts = (0, 1) if i % 2 == 0 else (2, 3)
                        for t in ts if i < 6 else range(4):
                            head_norm(h_rs, l, 4 * g, t, groups[g](t), T if g else MEM)

                    def fox_o(i, p):
                        h, t = i // NT, i % NT
                        a = HD * (h % 2)
                        at = (slice(a, a + HD), h // 2, slice(t * P, (t + 1) * P))
                        return ml[at], mh[at], p[a:a + HD, 0:P]
                    attention("fox", l, 4 * FOX_H, 8, lambda i: (1, P * (i % NT + 1)), 1.0, None, fox_o)

                def xa_o(i, p):
                    at = (slice(0, P), 4 + i // 2, slice((i % 2) * MEM, (i % 2 + 1) * MEM))
                    return ml[at], mh[at], p[:, 0:MEM]
                attention("xa", l, 2 * XA_H, 40 * l, lambda i: (2, MEM), float(P) ** -0.5, None, xa_o)
                if l == 0:
                    dve.wait_ge(S("lru_hi"), 1)
                    dve.tensor_tensor(ml[:, 0:4, :], UC, f32(mh[:, 0:4, :]), ALU.subtract).then_inc(S("lru_lo"), 1)
                for s in range(4):
                    lo(plan.slab["wo", l, s] + 1)
                    for b in range(2):
                        j = J["wo", l, s, b]
                        ready(dve, j)
                        add_x(j, 2 * s + b)
                    if s:
                        norm_sums(2 * l + 1, range(max(1, 2 * s - 2), 2 * s))
                norm_sums(2 * l + 1, (6, 7))
                norm(2 * l + 1, lambda t: V("norm_mlp", 8 * l + t))
                if l == 0:
                    dve.wait_ge(S("c_act"), 1)
                g0, j0, n0, a0 = plan.slab["up", (l, 0), 0], J["up", (l, 0), 0, 0], 32 * l, 256 * l + 16
                for c in loop(dve, CHUNKS1):
                    for i in range(8):
                        lo(g0 + i + 1, 8 * c)
                        dve.wait_ge(ada_landed[i % 2], 16 * (16 * l + i // 2 + 1) + 64 * c)
                        acc = ada_acc[:, bass.ds(c * (8 * ADA_COLS) + i * ADA_COLS, ADA_COLS)]
                        for k in range(KT):
                            w = ada[:, i % 2, k, :]
                            if k == 0:
                                ins = dve.tensor_scalar(acc, w, cact[:, 0:1], None, ALU.mult)
                            else:
                                dve.wait_ge(ada_done, a0 + 8 * i + k + 64 * c)
                                ins = dve.scalar_tensor_tensor(acc, w, cact[:, k:k + 1], acc, ALU.mult, ALU.add)
                            ins.then_inc(ada_done, 1)
                        for b in range(2):
                            m, j = 2 * i + b, j0 + 2 * i + b
                            if i < 4:
                                evacuated(dve, j, 2 * c)
                                dve.wait_ge(hid_done, n0 + m + 1 + 8 * c)
                                dve.tensor_tensor(f_v[:, m % 2, :], f_t[:, m % 2, :], f_t[:, m % 2, :], ALU.mult)\
                                   .then_inc(S("hidden_sq"), 1)
                                dve.wait_ge(S("hidden_sq"), n0 + m + 1 + 8 * c)
                                dve.wait_ge(hid_hi, n0 + m + 1 + 8 * c)
                                dve.tensor_tensor(ml[:, m, :], f_v[:, m % 2, :], f32(mh[:, m, :]), ALU.subtract)\
                                   .then_inc(hid_done, 1)
                            else:
                                ready(dve, j, 16 * c)
                                add_x(j, m - 8)
            for l in range(2):
                if l == 0:
                    norm_sums(4)
                norm(4 + 2 * l, lambda t: gmod[:, 2 * l, t:t + 1], (l, 0))
                if l == 0:
                    adaln(1)

                shifted = [0]

                def before_part(name, s, b, mu, dst, rows=P):
                    j = J[name, l, s, b]
                    shifted[0] += 1
                    dve.wait_ge(S("shift_own"), SHIFT_TILES * l + shifted[0])
                    free(dve.scalar_tensor_tensor(dst[:, 1:T], bank(j)[0:rows, 0:T - 1], mu, dst[:, 1:T], ALU.mult, ALU.add), j)

                m0 = SHIFT_TILES * l

                def before_tiles(i, name, s, dst):
                    lo(plan.slab[name, l, s] + 1)
                    for b in range(2):
                        t = 4 * i + 2 * s + b
                        before_part(name, s, b, V("mu_shift_2", m0 + t), dst[:, 2 * s + b, :])

                lo(plan.slab["lat", l, 0] + 1)
                before_part("lat", 0, 0, V("mu_shift_2", m0 + 12), LA)
                before_part("lat", 0, 1, V("mu_shift_2", m0 + 13), GL[:, 0, :])
                lo(plan.slab["gl1", l, 0] + 1)
                before_part("gl1", 0, 0, V("mu_shift_2", m0 + 14, 32), GL[0:32, 1, :], 32)
                if l:
                    lo(plan.slab["vl", l, 0] + 1)
                    before_part("vl", 0, 0, V("mu_v_2", 0, 32), VL[0:32, :], 32)
                for s in range(2):
                    before_tiles(1, "k2", s, K2)
                evacuated(dve, J["k2", l, 1, 1])
                for t in range(4):
                    dve.tensor_scalar(KK[:, t, :], K2[:, t, :], V("k_k_2", 4 * l + t), None, ALU.mult).then_inc(S("kk_raw"), 1)
                for t in range(4):
                    evacuated(dve, J["lw", l, t])
                    q.mark(dve.tensor_tensor_scan(C2[:, t, :], keep[:, :], SG[:, t, :], 0.0, ALU.mult, ALU.add))
                q.settle()
                dve.tensor_tensor(SG, C2, SG, ALU.subtract).then_inc(S("cum_decay"), 1)
                dve.wait_ge(S("kk_raw"), 4 * l + 4)
                for s in range(2):
                    before_tiles(0, "r2", s, R2)
                    for t in (2 * s, 2 * s + 1):
                        evacuated(dve, J["kn", l, t])
                        q.mark(dve.tensor_scalar(X1[:, t, :], X1[:, t, :], 1e-12, None, ALU.max))
                        q.settle()
                        q.mark(dve.reciprocal(X1[:, t, :], X1[:, t, :]))
                        q.settle()
                        q.mark(dve.tensor_tensor(KK[:, t, :], KK[:, t, :], X1[:, t, :], ALU.mult))
                q.settle()
                dve.sem_inc(S("kk_done"), 1)
                evacuated(dve, J["la", l, 3])
                dve.tensor_tensor(A2, X2, KK, ALU.mult).then_inc(S("b_made"), 1)
                dve.wait_ge(S("b_made"), l + 1)
                for t in range(4):
                    q.mark(dve.tensor_scalar(X2[:, t, :], X2[:, t, :], 1.0, V("k_a_2", 4 * l + t), ALU.subtract, ALU.mult))
                q.settle()
                q.mark(dve.scalar_tensor_tensor(K2, X2, 1.0, K2, ALU.add, ALU.mult))
                v_dst = VD if l else V2
                before_tiles(2, "v2", 0, v_dst)
                q.settle()
                evacuated(dve, J["r2", l, 1, 1])
                for t in range(4):
                    dve.scalar_tensor_tensor(X2[:, t, :], R2[:, t, :], V("r_k_2", 4 * l + t), K2[:, t, :], ALU.mult, ALU.mult)\
                       .then_inc(S("bonus_in"), 1)
                dve.wait_ge(S("decays"), 3 * l + 3)
                dve.wait_ge(S("bonus_in"), 4 * l + 4)
                dve.tensor_tensor(K2, K2, C2, ALU.mult).then_inc(S("features"), 1)
                q.mark(dve.tensor_copy(PC[:, :, :], X1[:, :, CH - 1:T:CH]))
                q.mark(dve.memset(ST[:, 0, :, :], 0.0))
                q.settle()
                dve.tensor_tensor(R2, R2, X1, ALU.mult).then_inc(S("features"), 1)
                before_tiles(2, "v2", 1, v_dst)
                evacuated(dve, J["v2", l, 1, 1])
                if l:
                    q.mark(dve.tensor_tensor(V2, V2, VD, ALU.subtract))
                    evacuated(dve, J["lv", l, 3])
                    q.settle()
                    q.mark(dve.tensor_tensor(V2, V2, BON, ALU.mult))
                    q.settle()
                    q.mark(dve.tensor_tensor(V2, V2, VD, ALU.add))
                    q.settle()
                dve.sem_inc(S("values"), 1)
                for t in range(4):
                    j = J["bon", l, t]
                    ready(dve, j)
                    free(dve.tensor_tensor(BON[:, t, :], bank(j), V2[:, t, :], ALU.mult), j)
                lo(plan.slab["z", l, 0] + 1)
                def p4(j):
                    return bank(j).rearrange("p (j n) -> p j n", j=4)

                def pc4(j):
                    return bank(j)[:, 0:4 * CH].rearrange("p (j n) -> p j n", j=4)

                def masked(name, m, i, dst, mask):
                    j = J[name, l, m, i]
                    ready(dve, j)
                    free(dve.tensor_tensor(dst[:, 4 * i:4 * i + 4, :], p4(j), bc(mask[:, :]), ALU.mult), j)

                def fill(m, jobs):
                    for f in jobs:
                        if f == ("tok", 2):
                            j = J["tok", l, m, 2]
                            ready(dve, j)
                            free(dve.tensor_copy(KhT, bank(j)), j)
                        if f[0] == "Akk":
                            masked("Akk", m, f[1], AK, strict)
                        if f[0] in ("Ark", "Arb"):
                            masked(f[0], m, f[1], AR if f[0] == "Ark" else AB, incl)

                def state_step(m, c):
                    cc = 2 * m + c
                    evacuated(dve, J["NH", l, m, c])
                    for i in range(2):
                        j = J["S", l, m, c, i]
                        a = slice(HD * i, HD * i + HD)
                        ready(dve, j)
                        new = ST[a, (cc + 1) % 3, :, :]
                        free(dve.tensor_tensor(new, bank(j)[a, 0:4 * HD].rearrange("p (j n) -> p j n", j=4),
                                               HS[a, c, :, :], ALU.add), j)
                        evacuated(dve, j)
                        pc = PC[a, :, cc:cc + 1].to_broadcast([HD, 4, HD])
                        dve.tensor_tensor(new, new, pc, ALU.mult).then_inc(S("state"), 1)

                for i in range(2):
                    masked("LT", 0, i, LT, strict)
                for m in range(NT):
                    if m:
                        ready(dve, J["Y", l, m - 1, 1])
                    half = [slice(0, 4), slice(4, 8)]
                    for i in range(2):
                        j = J["L", l, m, i]
                        ready(dve, j)
                        for c in range(2):
                            s = slice(CH * c, CH * c + CH)
                            mask = lvl[s, 0:1, :].to_broadcast([CH, 4, CH])
                            ins = dve.tensor_tensor(T1[s, half[i], :], p4(j)[s, :, s], mask, ALU.mult)
                        free(ins, j)
                    for i in range(2):
                        evacuated(dve, J["L", l, m, i])
                        dve.tensor_tensor(MM[:, half[i], :], bc(ident2[:, :]), T1[:, half[i], :], ALU.subtract)\
                           .then_inc(S("inv_start"), 1)
                    for n in range(len(LEVELS)):
                        for i in range(2):
                            j = J["LM", l, m, n, i]
                            ready(dve, j)
                            free(dve.tensor_tensor(T1[:, half[i], :], pc4(j), bc(lvl[:, 1 + n, :]), ALU.mult), j)
                        fill(m, FILL[2 * n])
                        for i in range(2):
                            j = J["MLM", l, m, n, i]
                            ready(dve, j)
                            free(dve.tensor_tensor(MM[:, half[i], :], MM[:, half[i], :], pc4(j), ALU.subtract), j)
                        fill(m, FILL[2 * n + 1])
                    fill(m, FILL[-1])
                    for c in range(2):
                        j = J["NH", l, m, c]
                        ready(dve, j)
                        p = bank(j).rearrange("p (x j n) -> p x j n", x=2, j=4)
                        dve.tensor_tensor(GS[:, c, :, :], bc(ident2[:, :]), p[:, 0, :, :], ALU.subtract)
                        free(dve.tensor_copy(HS[:, c, :, :], p[:, 1, :, :]), j)
                    state_step(m, 0)
                    fill(m, [("Ark", 1)])
                    for i in range(2):
                        j = J["U", l, m, i]
                        ready(dve, j)
                        free(dve.tensor_tensor(NU[:, 4 * i:4 * i + 4, :], WU[:, 4 * i:4 * i + 4, HD:P],
                                               bank(j)[:, 0:4 * HD].rearrange("p (j n) -> p j n", j=4), ALU.subtract), j)
                    state_step(m, 1)
                    if m + 1 < NT:
                        for i in range(2):
                            evacuated(dve, J["S", l, m, 1, i])
                            evacuated(dve, J["U", l, m, i])
                        for i in range(2):
                            masked("LT", m + 1, i, LT, strict)
                for t in range(4):
                    j = J["gmean", l, t]
                    ready(dve, j)
                    free(dve.tensor_tensor(R2[:, t, :], R2[:, t, :], bank(j), ALU.subtract), j)
                lo(plan.slab["z", l, 1] + 1)
                for t in range(4):
                    if t == 3:
                        lo(plan.slab["g0", (l, 0), 0] + 1)
                    evacuated(dve, J["gvar", l, t])
                    q.mark(dve.reciprocal(A2[:, t, :], A2[:, t, :]))
                    q.settle()
                    q.mark(dve.scalar_tensor_tensor(R2[:, t, :], R2[:, t, :], V("lnx_g_2", 4 * l + t), A2[:, t, :], ALU.mult, ALU.mult))
                    q.settle()
                    q.mark(dve.scalar_tensor_tensor(R2[:, t, :], R2[:, t, :], V("lnx_b_2", 4 * l + t), BON[:, t, :], ALU.add, ALU.add))
                    q.settle()
                    j = J["g", l, t]
                    ready(dve, j)
                    free(dve.tensor_tensor(R2[:, t, :], R2[:, t, :], bank(j), ALU.mult), j)
                for t in range(4):
                    dve.wait_ge(S("ya_hi"), 4 * l + t + 1)
                    dve.tensor_tensor(ml[:, t, :], R2[:, t, :], f32(mh[:, t, :]), ALU.subtract).then_inc(S("ya_lo"), 1)
                for p in range(4):
                    for name in ("g0", "g1"):
                        if (p, name) != (0, "g0"):
                            lo(plan.slab[name, (l, p), 0] + 1)
                    if p == 0:
                        dve.wait_ge(S("pooled"), 4 * l + 4)
                    for t in range(4) if p == 0 else ():
                        j = J["pool", l, t]
                        dve.wait_ge(S("yb_hi"), 4 * l + t + 1)
                        free(dve.scalar_tensor_tensor(ml[:, 4 + t, :], bank(j), V("pool_scale_2", 4 * l + t),
                                                      f32(mh[:, 4 + t, :]), ALU.mult, ALU.subtract), j)
                    for i, name in enumerate(("pa", "pb")):
                        lo(plan.slab[name, (l, p), 0] + 1)
                        for b in range(2):
                            evacuated(dve, J[("g0", "g1")[i], (l, p), 0, b])
                            j = J[name, (l, p), 0, b]
                            ready(dve, j)
                            free(dve.tensor_tensor(BON[:, 2 * i + b, :], KK[:, 2 * i + b, :], bank(j), ALU.mult), j)
                    for b in range(2):
                        evacuated(dve, J["pa", (l, p), 0, b])
                        evacuated(dve, J["pb", (l, p), 0, b])
                        dve.tensor_tensor(mixed[2 * p + b], BON[:, b, :], BON[:, 2 + b, :], ALU.add).then_inc(S("mixed"), 1)
                for t in range(KT):
                    dve.wait_ge(S("mixed_hi"), 8 * l + t + 1)
                    dve.tensor_tensor(hl[:, t, :], mixed[t], f32(hh[:, t, :]), ALU.subtract).then_inc(S("mixed_lo"), 1)
                for s in range(4):
                    lo(plan.slab["wo2", l, s] + 1)
                    for b in range(2):
                        j, t = J["wo2", l, s, b], 2 * s + b
                        ready(dve, j)
                        add_x(j, t, mod[:, l, 16 + t:17 + t])
                    if s:
                        norm_sums(5 + 2 * l, range(max(1, 2 * s - 2), 2 * s))
                norm_sums(5 + 2 * l, (6, 7))
                norm(5 + 2 * l, lambda t: gmod[:, 2 * l + 1, t:t + 1], (l, 24))

                def gated(i, g0, j0, n0, c):
                    lo(g0 + 2 * i + 1, 12 * c)
                    lo(g0 + 2 * i + 2, 12 * c)
                    for b in range(2):
                        m, j = 2 * i + b, j0 + 4 * i + 2 + b
                        evacuated(dve, j - 2, 3 * c)
                        ready(dve, j, 24 * c)
                        dve.wait_ge(hid_done, n0 + m + 1 + 8 * c)
                        free(dve.tensor_tensor(f_v[:, m % 2, :], f_t[:, m % 2, :], bank(j), ALU.mult), j)
                    for b in range(2):
                        m = 2 * i + b
                        dve.wait_ge(hid_hi, n0 + m + 1 + 8 * c)
                        dve.tensor_tensor(ml[:, m, :], f_v[:, m % 2, :], f32(mh[:, m, :]), ALU.subtract).then_inc(hid_done, 1)

                g0, j0, n0 = plan.slab["fg", (l, 0, 0), 0], J["fg", (l, 0, 0), 0, 0], 64 + 22 * l
                for c in loop(dve, 2):
                    for i in range(4):
                        gated(i, g0, j0, n0, c)
                    for i in range(4):
                        lo(g0 + 8 + i + 1, 12 * c)
                        for b in range(2):
                            j, t = j0 + 16 + 2 * i + b, 2 * i + b
                            ready(dve, j, 24 * c)
                            add_x(j, t, mod[:, l, 40 + t:41 + t])
                g0, j0, n0 = g0 + 24, j0 + 48, n0 + 16
                for i in range(3):
                    gated(i, g0, j0, n0, 0)
                for i in range(4):
                    lo(g0 + 6 + i + 1)
                    for b in range(2):
                        j, t = j0 + 12 + 2 * i + b, 2 * i + b
                        ready(dve, j)
                        add_x(j, t, mod[:, l, 40 + t:41 + t])
                    if i:
                        norm_sums(6 + 2 * l, range(max(1, 2 * i - 2), 2 * i))
                norm_sums(6 + 2 * l, (6, 7))
            norm(8, lambda t: V("final_g_2", t))
            for i in range(1, 8, 2):
                j = J["outT", i]
                ready(dve, j)
                free(dve.tensor_copy(o_tok[:, i // 2, T:D], bank(j)), j)

        @block.tensor
        def _(pe):
            todo = [0]

            def start(*key, c=0, jobs=0):
                j = J[key]
                assert j == todo[0], (key, j, todo)
                todo[0] += 1
                if j >= BANKS:
                    pe.wait_ge(bank_read[j % BANKS], j // BANKS + (jobs // BANKS) * c)
                return bank(j)

            def done(ins):
                ins.then_inc(written, 1)

            def three(out, whi_, wlo_, xhi, xlo, first, last):
                pe.matmul(out, whi_, xhi, start=first, stop=False)
                pe.matmul(out, whi_, xlo, start=False, stop=False)
                return pe.matmul(out, wlo_, xhi, start=False, stop=last)

            def linear(name, layer, s, operand, K=KT, blocks=2, n=T, before=None, c=0, slabs=0, jobs=0, only=None):
                g = plan.slab[name, layer, s]
                pe.wait_ge(raw_used, g + 1 + slabs * c)
                xh, xl = operand

                def tile(p, b, k):
                    w = (slice(0, P), g % 2, k, slice(b * P, (b + 1) * P))
                    ins = three(p[:, 0:n], whi[w], wlo[w], xh[:, k, 0:n], xl[:, k, 0:n], k == 0, k == K - 1)
                    if k == K - 1:
                        done(ins)
                if before:
                    banks = [start(name, layer, s, b, c=c, jobs=jobs) for b in range(blocks)]
                    for k in range(K):
                        before(k)
                        for b in range(blocks):
                            tile(banks[b], b, k)
                    return
                for b in range(blocks) if only is None else [only]:
                    p = start(name, layer, s, b, c=c, jobs=jobs)
                    for k in range(K):
                        tile(p, b, k)

            def linear_tokens(name, layer, s, operand, tiles):
                g = plan.slab[name, layer, s]
                pe.wait_ge(raw_used, g + 1)
                xh, xl = operand
                for b in range(tiles):
                    p = start(name, layer, s, b)
                    for k in range(KT):
                        t = slice(b * P, (b + 1) * P)
                        wh, wl = whi[:, g % 2, k, :], wlo[:, g % 2, k, :]
                        pe.matmul(p[:, 0:SLAB], xh[:, k, t], wh, start=(k == 0), stop=False)
                        pe.matmul(p[:, 0:SLAB], xl[:, k, t], wh, start=False, stop=False)
                        ins = pe.matmul(p[:, 0:SLAB], xh[:, k, t], wl, start=False, stop=(k == KT - 1))
                    done(ins)

            def mean_square(ni):
                pe.wait_ge(S("norm_added"), 7 * ni + 7)
                p = start("ms", ni)
                done(pe.matmul(p, mean_all[:, :], n_acc, start=True, stop=True))

            def normed(ni):
                return lambda k: pe.wait_ge(S("norm_lo"), 8 * ni + k + 1)

            def head_means(l, first, m, sq, n=T):
                for i in range(4):
                    pe.wait_ge(S("head_sq"), (8 if l else 0) + first + i + 1)
                    p = start("hn", l, first + i)
                    done(pe.matmul(p[:, 0:n], m[:, :], sq[:, i, 0:n], start=True, stop=True))

            def adaln(l):
                p = start("mod", l)
                pe.wait_ge(ada_done, 256 * (l + 1) + 16)
                for n in range(48):
                    ins = pe.matmul(p[:, n:n + 1], ada_acc[:, n * P:(n + 1) * P], ones[:, 0:1], start=True, stop=True)
                done(ins)

            def attention(name, l, units, base, scores, turn, values):
                for i in range(units + VALUES):
                    if i < units:
                        done(scores(i, start(name + "_s", l, i)))
                    u = i - TURN
                    if 0 <= u < units:
                        pe.wait_ge(S("att_probs"), base + u + 1)
                        done(turn(u, start(name + "_t", l, u)))
                    u = i - VALUES
                    if u >= 0:
                        evacuated(pe, J[name + "_t", l, u])
                        done(values(u, start(name + "_o", l, u)))

            pe.wait_ge(s_const, 2)
            pe.wait_ge(s_x, 16)
            for t in range(KT):
                p = start("xT", t)
                for s in range(NT):
                    ins = pe.transpose(p[:, s * P:(s + 1) * P], x_tok[:, s, t * P:(t + 1) * P], ident[:, :])
                done(ins)
            pe.wait_ge(s_vec, 16 * len(vector_loads))
            for i in range(3):
                p = start("vec", i)
                done(pe.transpose(p[:, 0:P], vrows[:, i, :], ident[:, :]))
            pe.wait_ge(s_const, 3)
            pe.wait_ge(S("mem_normed"), MT_)
            for i in range(4):
                p = start("memT", i)
                for t in range(2):
                    for s in range(MT_):
                        a = (2 * t + s) * P
                        ins = pe.transpose(p[:, a:a + P], mem_tok[:, s, (2 * i + t) * P:(2 * i + t + 1) * P], ident[:, :])
                done(ins)
            h, y = (hh, hl), (mh, ml)
            for l in range(2):
                if l == 1:
                    mean_square(2 * l)
                    adaln(0)
                mem_operand = [(mh[:, :, m * MEM:(m + 1) * MEM], ml[:, :, m * MEM:(m + 1) * MEM]) for m in range(2)]
                if l == 0:
                    for s in range(2):
                        linear("memk", 0, s, mem_operand[0], n=MEM,
                               before=None if s else lambda k: pe.wait_ge(S("mem_lo"), k + 1))
                    mean_square(0)
                    linear_tokens("memv", 0, 0, mem_operand[0], MT_)
                    head_means(0, 0, mean_128, m_sq, MEM)
                    linear_tokens("memv", 0, 1, mem_operand[0], MT_)
                    for name in ("u", "xq"):
                        for s in range(2):
                            linear(name, l, s, h, before=normed(0) if name == "u" and s == 0 else None)
                    linear("gate", l, 0, h)
                    head_means(0, 4, mean_128, x_sq)
                    linear("gate", l, 1, h)
                    pe.wait_ge(S("conv"), 4)
                    pe.wait_ge(s_small, 256)
                    for t in range(4):
                        for name, w in (("rgate", WR), ("igate", WI)):
                            p = start(name, t)
                            done(pe.matmul(p, w[:, t, :], UC[:, t, :], start=True, stop=True))
                    pe.wait_ge(S("mem_lo"), 16)
                    for s in range(2):
                        linear("memk", 1, s, mem_operand[1], n=MEM)
                    for s in range(2):
                        linear_tokens("memv", 1, s, mem_operand[1], MT_)
                else:
                    linear("f", l, 0, h, before=normed(2), blocks=1)
                    means = [mean_128, mean_128, mean_64, mean_64]
                    for g, name in enumerate(("xq", "q", "k", "v")):
                        for s in range(2):
                            if name == "v":
                                linear_tokens("v", l, s, h, NT)
                            else:
                                linear(name, l, s, h)
                            if s == 0:
                                head_means(l, 4 * g, means[g], h_sq, T if g else MEM)
                    pe.wait_ge(s_aug, 32)
                    pe.wait_ge(S("head_done"), 24)

                    def fox_scores(i, p):
                        hd, t = i // NT, i % NT
                        n = P * (t + 1)
                        a = HD + 2
                        pe.matmul(p[:, 0:n], qaug[0:a, hd, t * P:(t + 1) * P], kaug[0:a, hd, 0:n], start=True, stop=False)
                        return pe.matmul(p[:, t * P:n], ident[:, :], causal[:, :], start=False, stop=True)

                    def fox_turn(i, p):
                        for k in range(i % NT + 1):
                            ins = pe.transpose(p[:, k * P:(k + 1) * P], a_p[:, i % RING, k * P:(k + 1) * P], ident[:, :])
                        return ins

                    def fox_values(i, p):
                        hd, t = i // NT, i % NT
                        a = HD * (hd % 2)
                        for k in range(t + 1):
                            ins = pe.matmul(p[a:a + HD, 0:P], vtok[:, k, hd * HD:(hd + 1) * HD],
                                            a_t[:, i % RING, k * P:(k + 1) * P], start=(k == 0), stop=(k == t))
                        return ins
                    attention("fox", l, 4 * FOX_H, 8, fox_scores, fox_turn, fox_values)
                pe.wait_ge(S("head_done"), 8 if l == 0 else 24)

                def xa_scores(i, p):
                    for s in range(2):
                        t = 2 * (i % 2) + s
                        ins = pe.matmul(p[:, s * MEM:(s + 1) * MEM], XQ[:, i // 2, t * P:(t + 1) * P], mK[l][:, i // 2, :],
                                        start=True, stop=True)
                    return ins

                def xa_turn(i, p):
                    for k in range(MT_):
                        for s in range(2):
                            ins = pe.transpose(p[:, k * MEM + s * P:k * MEM + (s + 1) * P],
                                               a_p[:, i % RING, s * MEM + k * P:s * MEM + (k + 1) * P], ident[:, :])
                    return ins

                def xa_values(i, p):
                    for k in range(MT_):
                        ins = pe.matmul(p[:, 0:MEM], mV[l][:, k, (i // 2) * P:(i // 2 + 1) * P],
                                        a_t[:, i % RING, k * MEM:(k + 1) * MEM], start=(k == 0), stop=(k == MT_ - 1))
                    return ins
                attention("xa", l, 2 * XA_H, 40 * l, xa_scores, xa_turn, xa_values)

                def mixer_out(k):
                    if k >= 4:
                        evacuated(pe, J["xa_o", l, 2 * (k - 4) + 1])
                    elif l == 0:
                        pe.wait_ge(S("lru_lo"), 1)
                    else:
                        evacuated(pe, J["fox_o", l, 2 * NT * (k + 1) - 1])
                for s in range(4):
                    linear("wo", l, s, y, before=mixer_out if s == 0 else None)
                mean_square(2 * l + 1)
                g0, n0 = plan.slab["up", (l, 0), 0], 32 * l
                for c in loop(pe, CHUNKS1):
                    for s in range(4):
                        linear("up", (l, 0), s, h, before=normed(2 * l + 1) if s == 0 else None, c=c, slabs=8, jobs=16)
                    for s in range(4):
                        linear("down", (l, 0), s, y, c=c, slabs=8, jobs=16,
                               before=(lambda k: pe.wait_ge(hid_done, n0 + k + 3 + 8 * c)) if s == 0 else None)
                todo[0] += 16 * (CHUNKS1 - 1)
            for l in range(2):
                mean_square(4 + 2 * l)
                if l == 0:
                    adaln(1)
                linear("lat", l, 0, h, before=normed(4 + 2 * l))
                linear("gl1", l, 0, h, blocks=1)
                if l:
                    linear("vl", l, 0, h, blocks=1)
                linear("k2", l, 0, h)
                small = 80 * l + (32 if l == 0 else 48)
                pe.wait_ge(s_lora, small)
                pe.wait_ge(S("decay_latent"), l + 1)
                for t in range(4):
                    p = start("lw", l, t)
                    done(pe.matmul(p, WA[0:HD, t * P:(t + 1) * P], LA[0:HD, :], start=True, stop=True))
                for t in range(4):
                    p = start("la", l, t)
                    done(pe.matmul(p, WA[HD:P, t * P:(t + 1) * P], LA[HD:P, :], start=True, stop=True))
                if l:
                    evacuated(pe, J["vl", l, 0, 0])
                    for t in range(4):
                        p = start("lv", l, t)
                        done(pe.matmul(p, VU[0:32, t * P:(t + 1) * P], VL[0:32, :], start=True, stop=True))
                linear("k2", l, 1, h)
                linear("r2", l, 0, h)
                pe.wait_ge(S("kk_sq"), l + 1)
                for t in range(4):
                    p = start("kn", l, t)
                    done(pe.matmul(p, sum_64[:, :], X1[:, t, :], start=True, stop=True))
                linear("r2", l, 1, h)
                for s in range(2):
                    linear("v2", l, s, h)
                for t in range(4):
                    pe.wait_ge(S("bonus_in"), 4 * l + t + 1)
                    p = start("bon", l, t)
                    done(pe.matmul(p, sum_64[:, :], X2[:, t, :], start=True, stop=True))
                pe.wait_ge(S("features"), 4 * l + 4)
                def products(name, m, i, left, right):
                    ms, a = slice(m * P, (m + 1) * P), slice(HD * i, HD * i + HD)
                    p = start(name, l, m, i)
                    for t in range(4):
                        ins = pe.matmul(p[:, t * P:(t + 1) * P], left[a, t, ms], right[a, t, ms], start=True, stop=True)
                    done(ins)

                def head(i, t):
                    return slice((2 * t + i) * HD, (2 * t + i + 1) * HD)

                def fill(m, jobs):
                    for f in jobs:
                        if f[0] == "tok":
                            src = (KK, A2, K2, V2)[f[1]]
                            if f[1] == 3 and m == 0:
                                pe.wait_ge(S("values"), l + 1)
                            p = start("tok", l, m, f[1])
                            for t in range(4):
                                ins = pe.transpose(p[:, t * P:(t + 1) * P], src[:, t, m * P:(m + 1) * P], ident[:, :])
                            done(ins)
                        elif f[0] == "AkkV":
                            for i in range(2):
                                evacuated(pe, J["Akk", l, m, i])
                            evacuated(pe, J["tok", l, m, 3])
                            p = start("AkkV", l, m)
                            for t in range(4):
                                for i in range(2):
                                    ins = pe.matmul(p[:, head(i, t)], AK[:, 4 * i + t, :], VT[:, head(i, t)], start=True, stop=True)
                            done(ins)
                        else:
                            products(f[0], m, f[1], A2 if f[0] == "Arb" else K2, KK if f[0] == "Akk" else R2)

                def blocks(name, m, n, i, left, right):
                    p = start(name, l, m, n, i)
                    for t in range(4):
                        ins = pe.matmul(p[:, t * CH:(t + 1) * CH], left[:, 4 * i + t, :], right[:, 4 * i + t, :], start=True, stop=True)
                    done(ins)

                def turned(src, rows, *key):
                    for i in range(2):
                        p = start(*key, i)
                        for t in range(4):
                            ins = pe.transpose(p[0:rows, t * P:(t + 1) * P], src[:, 4 * i + t, :], ident[:, :])
                        done(ins)

                for i in range(2):
                    products("LT", 0, i, A2, KK)
                for m in range(NT):
                    for i in range(2):
                        evacuated(pe, J["LT", l, m, i])
                    turned(LT, P, "L", l, m)
                    fill(m, [("tok", 0), ("tok", 1)])
                    for n in range(len(LEVELS)):
                        for i in range(2):
                            if n:
                                evacuated(pe, J["MLM", l, m, n - 1, i])
                            else:
                                pe.wait_ge(S("inv_start"), 2 * (NT * l + m) + i + 1)
                            blocks("LM", m, n, i, LT, MM)
                        if n:
                            turned(MM, CH, "TR", l, m, n - 1)
                        fill(m, FILL[2 * n])
                        for i in range(2):
                            evacuated(pe, J["LM", l, m, n, i])
                            if n:
                                evacuated(pe, J["TR", l, m, n - 1, i])
                            else:
                                pe.wait_ge(S("mt_start"), 2 * (NT * l + m) + i + 1)
                            blocks("MLM", m, n, i, MT, T1)
                        fill(m, FILL[2 * n + 1])
                    for i in range(2):
                        evacuated(pe, J["MLM", l, m, len(LEVELS) - 1, i])
                    turned(MM, CH, "TR", l, m, len(LEVELS) - 1)
                    fill(m, FILL[-1])
                    for i in range(2):
                        evacuated(pe, J["TR", l, m, len(LEVELS) - 1, i])
                    evacuated(pe, J["AkkV", l, m])
                    evacuated(pe, J["tok", l, m, 0])
                    for i in range(2):
                        p = start("WU", l, m, i)
                        for t in range(4):
                            ins = pe.matmul(p[:, t * P:(t + 1) * P], MT[:, 4 * i + t, :], KA[:, :, head(i, t)], start=True, stop=True)
                        done(ins)
                    p = start("WT", l, m)
                    for t in range(4):
                        for i in range(2):
                            ins = pe.matmul(p[HD * i:HD * i + HD, t * P:(t + 1) * P], KA[:, 0, head(i, t)], MT[:, 4 * i + t, :],
                                            start=True, stop=True)
                    done(ins)
                    for i in range(2):
                        evacuated(pe, J["WU", l, m, i])
                    evacuated(pe, J["tok", l, m, 1])
                    evacuated(pe, J["tok", l, m, 2])
                    for c in range(2):
                        p = start("NH", l, m, c)
                        s = slice(CH * c, CH * c + CH)
                        for t in range(4):
                            for i in range(2):
                                o = p[HD * i:HD * i + HD, :]
                                pe.matmul(o[:, t * HD:(t + 1) * HD], WU[s, 4 * i + t, 0:HD], BT[s, head(i, t)],
                                          start=True, stop=True)
                                a = 4 * HD + t * HD
                                pe.matmul(o[:, a:a + HD], KhT[s, head(i, t)], VT[s, head(i, t)], start=True, stop=False)
                                ins = pe.matmul(o[:, a:a + HD], BT[s, head(i, t)], WU[s, 4 * i + t, HD:P],
                                                start=False, stop=True)
                        done(ins)

                    def state_step(c):
                        cc = 2 * m + c
                        evacuated(pe, J["NH", l, m, c])
                        for i in range(2):
                            a = slice(HD * i, HD * i + HD)
                            if cc:
                                pe.wait_ge(S("state"), 16 * l + 2 * cc - 1 + i)
                            p = start("S", l, m, c, i)
                            for t in range(4):
                                ins = pe.matmul(p[a, t * HD:(t + 1) * HD], GS[a, c, t, :], ST[a, cc % 3, t, :], start=True, stop=True)
                            done(ins)
                    state_step(0)
                    if m in Z_AT:
                        t = Z_AT.index(m)
                        linear("z", l, t // 2, h, only=t % 2)
                    fill(m, [("Ark", 1)])
                    evacuated(pe, J["WT", l, m])
                    for i in range(2):
                        a = slice(HD * i, HD * i + HD)
                        pe.wait_ge(S("state"), 16 * l + 4 * m + 1 + i)
                        p = start("U", l, m, i)
                        for c in range(2):
                            s = slice(CH * c, CH * c + CH)
                            for t in range(4):
                                ins = pe.matmul(p[s, t * HD:(t + 1) * HD], WT[a, t, s], ST[a, (2 * m + c) % 3, t, :],
                                                start=True, stop=True)
                        done(ins)
                    state_step(1)
                    if m + 1 < NT:
                        for i in range(2):
                            products("LT", m + 1, i, A2, KK)
                    for i in range(2):
                        a = slice(HD * i, HD * i + HD)
                        evacuated(pe, J["U", l, m, i])
                        evacuated(pe, J["Ark", l, m, i])
                        evacuated(pe, J["Arb", l, m, i])
                        p = start("Y", l, m, i)
                        for t in range(4):
                            o = p[a, t * P:(t + 1) * P]
                            pe.matmul(o, VT[:, head(i, t)], AR[:, 4 * i + t, :], start=True, stop=False)
                            pe.matmul(o, NU[:, 4 * i + t, :], AB[:, 4 * i + t, :], start=False, stop=False)
                            for c in range(2):
                                s = slice(CH * c, CH * c + CH)
                                ins = pe.matmul(o[:, s], ST[a, (2 * m + c) % 3, t, :],
                                                R2[a, t, m * P + CH * c:m * P + CH * c + CH], start=False, stop=(c == 1))
                        done(ins)
                for i in range(2):
                    evacuated(pe, J["Y", l, NT - 1, i])
                for t in range(4):
                    p = start("gmean", l, t)
                    done(pe.matmul(p, mean_64[:, :], R2[:, t, :], start=True, stop=True))
                for t in range(len(Z_AT), Z_MID):
                    linear("z", l, t // 2, h, only=t % 2)
                for t in range(4):
                    pe.wait_ge(S("gn_sq"), 4 * l + t + 1)
                    p = start("gvar", l, t)
                    done(pe.matmul(p, mean_64[:, :], KK[:, t, :], start=True, stop=True))
                for t in range(Z_MID, 4):
                    linear("z", l, t // 2, h, only=t % 2)
                pe.wait_ge(S("gate_latent"), 2 * l + 2)
                pe.wait_ge(s_lora, small + 48)
                for t in range(4):
                    p = start("g", l, t)
                    pe.matmul(p, GU[:, 0, t * P:(t + 1) * P], GL[:, 0, :], start=True, stop=False)
                    done(pe.matmul(p, GU[0:32, 1, t * P:(t + 1) * P], GL[0:32, 1, :], start=False, stop=True))
                for b in range(4):
                    linear("g0", (l, b), 0, h)
                    linear("g1", (l, b), 0, h)
                    for t in range(4) if b == 0 else ():
                        pe.wait_ge(S("pooled"), 4 * l + t + 1)
                        p = start("pool", l, t)
                        done(pe.matmul(p, PW[:, t, :], Z[t], start=True, stop=True))
                    linear("pa", (l, b), 0, y, K=4, before=lambda k: pe.wait_ge(S("ya_lo"), 4 * l + k + 1))
                    linear("pb", (l, b), 0, (mh[:, 4:8, :], ml[:, 4:8, :]), K=4,
                           before=lambda k: evacuated(pe, J["pool", l, k]))
                for s in range(4):
                    linear("wo2", l, s, h, before=(lambda k: pe.wait_ge(S("mixed_lo"), 8 * l + k + 1)) if s == 0 else None)
                mean_square(5 + 2 * l)
                n0 = 64 + 22 * l
                for c in loop(pe, 2):
                    for i in range(4):
                        linear("fg", (l, 0, i), 0, h, before=normed(5 + 2 * l) if i == 0 else None, c=c, slabs=12, jobs=24)
                        linear("fu", (l, 0, i), 0, h, c=c, slabs=12, jobs=24)
                    for s in range(4):
                        linear("fd", (l, 0), s, y, c=c, slabs=12, jobs=24,
                               before=(lambda k: pe.wait_ge(hid_done, n0 + k + 3 + 8 * c)) if s == 0 else None)
                todo[0] += 24
                for i in range(3):
                    linear("fg", (l, 2, i), 0, h)
                    linear("fu", (l, 2, i), 0, h)
                for s in range(4):
                    linear("fd", (l, 2), s, y, K=6,
                           before=(lambda k: pe.wait_ge(hid_done, n0 + 16 + k + 3)) if s == 0 else None)
            mean_square(8)
            pe.wait_ge(S("norm_val"), 8 * NORMS)
            for i in range(8):
                p = start("outT", i)
                for t in range(4):
                    ins = pe.transpose(p[:, t * P:(t + 1) * P], o_val[:, 4 * (i % 2) + t, (i // 2) * P:(i // 2 + 1) * P], ident[:, :])
                done(ins)
            assert todo[0] == plan.n


NAMES = ["x", "mem", "norm_mix", "norm_mem", "w_mem_kv", "xa_q_gain", "xa_k_gain", "w_out", "norm_mlp", "w_mlp_in",
         "w_mlp_out", "w_in_a", "conv_w", "conv_b", "w_rgate", "b_rgate", "w_igate", "b_igate", "lru_lambda", "w_in_b",
         "b_forget", "fox_q_gain", "fox_k_gain", "c_2", "ada_w_2", "ada_b_2", "norm1_g_2", "w_in_2", "v_down_2",
         "mu_shift_2", "mu_v_2", "w0_2", "w_up_2", "a0_2", "a_up_2", "v0_2", "v_up_2", "g_up_2", "k_k_2", "k_a_2",
         "r_k_2", "lnx_g_2", "lnx_b_2", "pool_w_2", "pool_scale_2", "proj_a_2", "proj_b_2", "w_out_2", "norm2_g_2",
         "w_gu_2", "w_down_2", "final_g_2"]


def kernel(**inputs):
    import numpy as np
    import concourse.bacc as bacc
    from concourse.bass_utils import run_bass_kernel_spmd

    nc = bacc.Bacc("TRN2", target_bir_lowering=False, num_devices=1)
    arrays, d = {}, {}
    for name in NAMES:
        a = np.ascontiguousarray(inputs[name])
        arrays["in_" + name] = a
        d[name] = nc.dram_tensor("in_" + name, a.shape, F32, kind="ExternalInput").ap()
    out = nc.dram_tensor("out", (1, T, D), F32, kind="ExternalOutput").ap()
    program(nc, d, out)
    r = run_bass_kernel_spmd(nc, [arrays], core_ids=[0])
    return r.results[0]["out"]
```
